# Optimizing a Trainium2 kernel written in Bass

```python
import jax
import jax.numpy as jnp
from jax import lax
import numpy as np

D_MODEL = 1024
BATCH = 1
SEQ = 1024
DEPTH = 1
DEC_BATCH = 1
DEC_SEQ = 512
PAST_LEN = 128

MIX_WIDTH = D_MODEL
POOL_WIDTH = MIX_WIDTH // 2
HG_WIDTH = MIX_WIDTH - POOL_WIDTH
POOL_WINDOWS = (2, 4, 8, 16)
POOL_GROUPS = len(POOL_WINDOWS)
POOL_GROUP_DIM = POOL_WIDTH // POOL_GROUPS
HG_EXPAND = 128
HG_HEADS = HG_WIDTH // HG_EXPAND
HG_DK = HG_EXPAND
HG_DV = HG_WIDTH // HG_HEADS
CHUNK = 16
IN_COLS = POOL_WIDTH + 5 * HG_WIDTH
N_GROUPS = 4
EXPERTS_PER_GROUP = 8
N_EXPERTS = N_GROUPS * EXPERTS_PER_GROUP
TOP_K = 2
D_EXPERT = D_MODEL // 2
EXPERT_BLOCK = 128
EPS = 1e-6

kernel_name = 'hybrid_pool_hgrn2_hiermoe_encoder'

def rmsnorm(x, gain):
    xf = x.astype(jnp.float32)
    y = xf * lax.rsqrt(jnp.mean(xf * xf, axis=-1, keepdims=True) + EPS)
    return (y * gain.astype(jnp.float32)).astype(x.dtype)

def multiscale_pool(u, pool_w, pool_scale):
    B, S, _ = u.shape
    ug = u.astype(jnp.float32).reshape(B, S, POOL_GROUPS, POOL_GROUP_DIM)
    cs = jnp.concatenate([jnp.zeros((B, 1, POOL_GROUPS, POOL_GROUP_DIM), jnp.float32),
                          jnp.cumsum(ug, axis=1)], axis=1)
    t = jnp.arange(S)
    groups = []
    for gi, w in enumerate(POOL_WINDOWS):
        lo = jnp.clip(t - w // 2, 0, S)
        hi = jnp.clip(t + w // 2, 0, S)
        cs_g = cs[:, :, gi]
        window_sum = jnp.take(cs_g, hi, axis=1) - jnp.take(cs_g, lo, axis=1)
        count = (hi - lo).astype(jnp.float32)[None, :, None]
        groups.append(window_sum / count - ug[:, :, gi])
    pooled = jnp.stack(groups, axis=2)
    y = jnp.einsum('bsgc,gcd->bsgd', pooled, pool_w.astype(jnp.float32))
    y = y.reshape(B, S, POOL_WIDTH) * pool_scale.astype(jnp.float32)
    return y.astype(u.dtype)

def chunked_gated_recurrence(q, k, v, log_f):
    B, S, H, DK = q.shape
    DV = v.shape[-1]
    N = S // CHUNK

    def chunks(a):
        return a.reshape(B, N, CHUNK, H, a.shape[-1]).transpose(0, 3, 1, 2, 4)

    q, k, v, log_f = chunks(q), chunks(k), chunks(v), chunks(log_f)
    b = jnp.cumsum(log_f, axis=3)
    b_last = b[:, :, :, -1:, :]
    q_dec = q * jnp.exp(b)
    k_intra = k * jnp.exp(-b)
    k_state = k * jnp.exp(b_last - b)
    chunk_decay = jnp.exp(b_last[:, :, :, 0, :])
    tri_mask = jnp.tril(jnp.ones((CHUNK, CHUNK), dtype=bool))
    scores = jnp.einsum('bhncd,bhnsd->bhncs', q_dec, k_intra)
    scores = jnp.where(tri_mask, scores, 0.0)
    o_intra = jnp.einsum('bhncs,bhnse->bhnce', scores, v)

    def step(state, xs):
        q_c, k_c, v_c, dec_c = xs
        o_c = jnp.einsum('bhcd,bhde->bhce', q_c, state)
        state = dec_c[..., None] * state + jnp.einsum('bhcd,bhce->bhde', k_c, v_c)
        return state, o_c

    xs = (jnp.moveaxis(q_dec, 2, 0), jnp.moveaxis(k_state, 2, 0),
          jnp.moveaxis(v, 2, 0), jnp.moveaxis(chunk_decay, 2, 0))
    _, o_inter = lax.scan(step, jnp.zeros((B, H, DK, DV), jnp.float32), xs)
    o = o_intra + jnp.moveaxis(o_inter, 0, 2)
    return o.transpose(0, 2, 3, 1, 4).reshape(B, S, H, DV)

def hgrn2_mixer(u_q, u_ff, u_fb, u_i, u_g, lb_fwd, lb_bwd, hg_norm_gain):
    B, S, _ = u_q.shape

    def heads(a):
        return a.astype(jnp.float32).reshape(B, S, HG_HEADS, -1)

    q = jax.nn.silu(heads(u_q))
    v = heads(u_i)

    def gate(logit, lb):
        f = lb + (1.0 - lb) * jax.nn.sigmoid(logit.astype(jnp.float32))
        return heads(1.0 - f), heads(jnp.log(f))

    k_f, g_f = gate(u_ff, lb_fwd)
    k_b, g_b = gate(u_fb, lb_bwd)
    o_fwd = chunked_gated_recurrence(q, k_f, v, g_f)

    def rev(a):
        return jnp.flip(a, axis=1)

    o_bwd = rev(chunked_gated_recurrence(rev(q), rev(k_b), rev(v), rev(g_b)))
    o = o_fwd + o_bwd
    o = o * lax.rsqrt(jnp.mean(o * o, axis=-1, keepdims=True) + EPS) * hg_norm_gain.astype(jnp.float32)
    o = o.reshape(B, S, HG_WIDTH) * jax.nn.silu(u_g.astype(jnp.float32))
    return o.astype(u_q.dtype)

def hierarchical_moe(x, router_group_w, router_group_b, router_expert_w, router_expert_b, w1, w3, w2):
    B, S, D = x.shape
    T = B * S
    A = T * TOP_K
    xt = x.reshape(T, D)
    group_logits = (jnp.einsum('td,dg->tg', xt, router_group_w).astype(jnp.float32)
                    + router_group_b.astype(jnp.float32))
    group_prob = jax.nn.softmax(group_logits, axis=-1)
    _, grp = lax.top_k(group_logits, 1)
    grp_prob = jnp.take_along_axis(group_prob, grp, axis=1)
    expert_logits = (jnp.einsum('td,de->te', xt, router_expert_w).astype(jnp.float32)
                     + router_expert_b.astype(jnp.float32)).reshape(T, N_GROUPS, EXPERTS_PER_GROUP)
    in_group = jnp.take_along_axis(expert_logits, grp[:, :, None], axis=1)[:, 0]
    top_val, top_idx = lax.top_k(in_group, TOP_K)
    gate = jax.nn.softmax(top_val, axis=-1) * grp_prob
    expert_id = grp * EXPERTS_PER_GROUP + top_idx

    flat_e = expert_id.reshape(A).astype(jnp.int32)
    order = jnp.argsort(flat_e)
    sorted_e = flat_e[order]
    tok_sorted = (order // TOP_K).astype(jnp.int32)
    gate_sorted = gate.reshape(A)[order]
    counts = jnp.zeros((N_EXPERTS,), jnp.int32).at[flat_e].add(1)
    start = jnp.cumsum(counts) - counts
    padded = (counts + EXPERT_BLOCK - 1) // EXPERT_BLOCK * EXPERT_BLOCK
    pend = jnp.cumsum(padded)
    pstart = pend - padded
    dest = pstart[sorted_e] + jnp.arange(A, dtype=jnp.int32) - start[sorted_e]
    n_blocks = -(-A // EXPERT_BLOCK) + N_EXPERTS
    slot_tok = jnp.full((n_blocks * EXPERT_BLOCK,), T, jnp.int32).at[dest].set(tok_sorted)
    block_expert = jnp.minimum(
        jnp.searchsorted(pend, jnp.arange(n_blocks, dtype=jnp.int32) * EXPERT_BLOCK, side='right'),
        N_EXPERTS - 1)
    x_pad = jnp.concatenate([xt, jnp.zeros((1, D), xt.dtype)], axis=0)

    def expert_block(args):
        toks, e = args
        xb = x_pad[toks]
        h = jax.nn.silu(xb @ w1[e]) * (xb @ w3[e])
        return h @ w2[e]

    y_blocks = lax.map(expert_block, (slot_tok.reshape(n_blocks, EXPERT_BLOCK), block_expert))
    y_sorted = y_blocks.reshape(n_blocks * EXPERT_BLOCK, D)[dest]
    y = jax.ops.segment_sum(y_sorted * gate_sorted[:, None].astype(x.dtype), tok_sorted, num_segments=T)
    return y.reshape(B, S, D).astype(x.dtype)

def layer_lower_bounds(param):
    return jnp.cumsum(jax.nn.softmax(param.astype(jnp.float32), axis=0), axis=0)

def encoder_layer(x, w_in, w_out, pool_w, pool_scale, lb_fwd, lb_bwd, hg_norm_gain, norm_mix, norm_ffn,
                  router_group_w, router_group_b, router_expert_w, router_expert_b, w1, w3, w2):
    n = rmsnorm(x, norm_mix)
    u = jnp.einsum('bsd,de->bse', n, w_in)
    cuts = [POOL_WIDTH + j * HG_WIDTH for j in range(5)]
    u_pool, u_q, u_ff, u_fb, u_i, u_g = jnp.split(u, cuts, axis=-1)
    mix = jnp.concatenate([multiscale_pool(u_pool, pool_w, pool_scale),
                           hgrn2_mixer(u_q, u_ff, u_fb, u_i, u_g, lb_fwd, lb_bwd, hg_norm_gain)], axis=-1)
    x = x + jnp.einsum('bse,ed->bsd', mix, w_out)
    x = x + hierarchical_moe(rmsnorm(x, norm_ffn), router_group_w, router_group_b,
                             router_expert_w, router_expert_b, w1, w3, w2)
    return x

def trunk(x, w_in, w_out, pool_w, pool_scale, hg_lb_fwd, hg_lb_bwd, hg_norm_gain, norm_mix, norm_ffn,
          router_group_w, router_group_b, router_expert_w, router_expert_b,
          expert_w1, expert_w3, expert_w2, norm_final):
    lb_f = layer_lower_bounds(hg_lb_fwd)
    lb_b = layer_lower_bounds(hg_lb_bwd)
    for l in range(DEPTH):
        x = encoder_layer(x, w_in[l], w_out[l], pool_w[l], pool_scale[l], lb_f[l], lb_b[l], hg_norm_gain[l],
                          norm_mix[l], norm_ffn[l], router_group_w[l], router_group_b[l],
                          router_expert_w[l], router_expert_b[l], expert_w1[l], expert_w3[l], expert_w2[l])
    return rmsnorm(x, norm_final)

def setup_inputs(seed: int = 0) -> dict:
    key = jax.random.key(seed)
    ks = jax.random.split(key, 20)

    def nrm(k, shape, scale):
        return jax.random.normal(k, shape, jnp.float32) * scale

    return {
        'x_prompt': nrm(ks[0], (BATCH, SEQ, D_MODEL), 1.0),
        'x_sample': nrm(ks[1], (DEC_BATCH, DEC_SEQ, D_MODEL), 1.0),
        'w_in': nrm(ks[2], (DEPTH, D_MODEL, IN_COLS), D_MODEL ** -0.5),
        'w_out': nrm(ks[3], (DEPTH, MIX_WIDTH, D_MODEL), MIX_WIDTH ** -0.5),
        'pool_w': nrm(ks[4], (DEPTH, POOL_GROUPS, POOL_GROUP_DIM, POOL_GROUP_DIM), POOL_GROUP_DIM ** -0.5),
        'pool_scale': 1.0 + nrm(ks[5], (DEPTH, POOL_WIDTH), 0.02),
        'hg_lb_fwd': nrm(ks[6], (DEPTH + 1, HG_WIDTH), 0.5),
        'hg_lb_bwd': nrm(ks[7], (DEPTH + 1, HG_WIDTH), 0.5),
        'hg_norm_gain': 1.0 + nrm(ks[8], (DEPTH, HG_DV), 0.02),
        'norm_mix': 1.0 + nrm(ks[9], (DEPTH, D_MODEL), 0.02),
        'norm_ffn': 1.0 + nrm(ks[10], (DEPTH, D_MODEL), 0.02),
        'router_group_w': nrm(ks[11], (DEPTH, D_MODEL, N_GROUPS), D_MODEL ** -0.5),
        'router_group_b': nrm(ks[12], (DEPTH, N_GROUPS), 0.01),
        'router_expert_w': nrm(ks[13], (DEPTH, D_MODEL, N_EXPERTS), D_MODEL ** -0.5),
        'router_expert_b': nrm(ks[14], (DEPTH, N_EXPERTS), 0.01),
        'expert_w1': nrm(ks[15], (DEPTH, N_EXPERTS, D_MODEL, D_EXPERT), D_MODEL ** -0.5),
        'expert_w3': nrm(ks[16], (DEPTH, N_EXPERTS, D_MODEL, D_EXPERT), D_MODEL ** -0.5),
        'expert_w2': nrm(ks[17], (DEPTH, N_EXPERTS, D_EXPERT, D_MODEL), D_EXPERT ** -0.5),
        'norm_final': 1.0 + nrm(ks[18], (D_MODEL,), 0.02),
    }

def reference(x_prompt, x_sample, w_in, w_out, pool_w, pool_scale, hg_lb_fwd, hg_lb_bwd, hg_norm_gain,
              norm_mix, norm_ffn, router_group_w, router_group_b, router_expert_w, router_expert_b,
              expert_w1, expert_w3, expert_w2, norm_final):
    y_prompt = trunk(x_prompt, w_in, w_out, pool_w, pool_scale, hg_lb_fwd, hg_lb_bwd, hg_norm_gain,
                     norm_mix, norm_ffn, router_group_w, router_group_b, router_expert_w, router_expert_b,
                     expert_w1, expert_w3, expert_w2, norm_final)
    y_sample = trunk(x_sample, w_in, w_out, pool_w, pool_scale, hg_lb_fwd, hg_lb_bwd, hg_norm_gain,
                     norm_mix, norm_ffn, router_group_w, router_group_b, router_expert_w, router_expert_b,
                     expert_w1, expert_w3, expert_w2, norm_final)
    return (y_prompt, y_sample)


_drawn_inputs = setup_inputs


def setup_inputs(seed=0):
    import zlib

    import numpy as np

    out = dict(_drawn_inputs(seed))
    spreads = {}
    factors = {'pool_scale': 8.324,
     'hg_norm_gain': 11.744,
     'router_group_b': 15.991,
     'router_expert_b': 16.537,
     'norm_final': 8.404,
     'norm_ffn': 3.816}
    for name, (base, spread) in spreads.items():
        noise = np.random.default_rng([zlib.crc32(name.encode()), seed]).standard_normal(out[name].shape)
        drawn = base * np.exp(spread * noise) if base else spread * noise
        out[name] = jnp.asarray(drawn.astype(out[name].dtype))
    for name, factor in factors.items():
        out[name] = (out[name] * factor).astype(out[name].dtype)
    return out
```

```python
import concourse.bass as bass
from concourse import mybir
from contextlib import ExitStack

P = 128
D = 1024
KT = D // P
T_PROMPT, T_SAMPLE = 1024, 512
T = T_PROMPT + T_SAMPLE
NT = T // P
GT = 512
NG = T // GT
BG = GT // P
HEADS = 4
SUB = 32
NSUB = P // SUB
WIDTH = 512
Q, FF, FB, OG, VAL = range(5)
SECTION_COLUMN = [1 * WIDTH, 2 * WIDTH, 3 * WIDTH, 5 * WIDTH, 4 * WIDTH]
SECTIONS = len(SECTION_COLUMN)
UNITS = SECTIONS * NG
POOLS = 4
POOL_UNITS = POOLS * NG
WINDOWS = (2, 4, 8, 16)
PAD = 8
POOL_W = T + 4 * PAD
EPS = 1e-6
FWD, BWD = 0, 1
STEPS = [(BWD, 2), (BWD, 1), (BWD, 0), (FWD, 0), (FWD, 1), (FWD, 2)]
NEW_SEQUENCE = {(BWD, 2), (BWD, 1), (FWD, 0), (FWD, 2)}
NS = len(STEPS)
BEFORE, PER_STEP = 3, 2
assert BEFORE + NS * PER_STEP == UNITS

W_LOADS = [(), (0,), (), (1,), (2,), (3, 4)]

N_GROUPS, PER_GROUP = 4, 8
NE = N_GROUPS * PER_GROUP
NLOG = N_GROUPS + NE
FE = 512
FT = FE // P
MAX_BLOCKS = (2 * T + NE * (P - 1)) // P
MIN_BLOCKS = 2 * T // P
SLOTS = MAX_BLOCKS * P
C_MIX, C_SCALE, C_GAIN, C_LB = 0, KT, KT + POOLS, KT + POOLS + 1
C_N = C_LB + 4 * HEADS
R_FFN, R_FINAL, R_BIAS = 0, D, 2 * D
R_N = 2 * D + NLOG


def pool_column(t):
    return PAD + t + (2 * PAD if t >= T_PROMPT else 0)


def static(i, value):
    return isinstance(i, int) and i == value


def trunk_program(nc, x_all, w_in, w_out, pool_w, cols, rows, inv_count, router_w,
                  w1, w3, w2, out):
    f32, i32, u32 = mybir.dt.float32, mybir.dt.int32, mybir.dt.uint32
    ALU, ACT, AX = mybir.AluOpType, mybir.ActivationFunctionType, mybir.AxisListType
    ds = bass.ds

    def scratch(name, shape, dt=f32):
        return nc.dram_tensor(name, shape, dt, kind="Internal").ap()

    u_dram = scratch("u_dram", (HEADS * SECTIONS * P, T))
    mix_dram = scratch("mix_dram", (KT * P, T))
    x1_dram = scratch("x1_dram", (T, D))
    xn_dram = scratch("xn_dram", (T, D))
    y_dram = scratch("y_dram", (SLOTS, D))

    always, mixing = ExitStack(), ExitStack()

    def sb(stack, name, shape, dt=f32):
        return stack.enter_context(nc.sbuf_tensor(name, shape, dt))

    with always:
        def sem(name):
            return always.enter_context(nc.semaphore(name))

        bank = [always.enter_context(nc.psum_tensor(f"bank{i}", [P, 512], f32)) for i in range(8)]
        ident = sb(always, "ident", [P, P])
        ones = sb(always, "ones", [P, P])
        colc = sb(always, "colc", [P, C_N])
        eps_col = sb(always, "eps_col", [P, 1])
        ss = sb(always, "ss", [P, 2])
        rstd = sb(always, "rstd", [P, 2])

        nT = sb(mixing, "nT", [P, KT, T])
        wsec = sb(mixing, "wsec", [P, SECTIONS, KT, P])
        ustage = sb(mixing, "ustage", [P, 3, GT])
        usig = sb(mixing, "usig", [P, GT])
        rin = sb(mixing, "rin", [P, 2, 3, GT])
        ogate = sb(mixing, "ogate", [P, NG, GT])
        keep = sb(mixing, "keep", [P, GT])
        logf = sb(mixing, "logf", [P, GT])
        cum = sb(mixing, "cum", [P, GT])
        dist = sb(mixing, "dist", [P, GT])
        exq = sb(mixing, "exq", [P, GT])
        exk = sb(mixing, "exk", [P, GT])
        LW = NSUB * (P + SUB)
        lev = [sb(mixing, f"lev{d}", [P, BG, LW]) for d in (FWD, BWD)]
        small = sb(mixing, "small", [P, BG, 9])
        smalle = sb(mixing, "smalle", [P, BG, 9])
        qs = sb(mixing, "qs", [P, GT])
        qint = sb(mixing, "qint", [P, GT])
        kst = sb(mixing, "kst", [P, GT])
        ktok = sb(mixing, "ktok", [P, BG, P])
        vtok = sb(mixing, "vtok", [P, NT, P])
        scT = [sb(mixing, f"scT{d}", [P, BG, P]) for d in (FWD, BWD)]
        state = sb(mixing, "state", [P, BG + 1, P])
        obwd = sb(mixing, "obwd", [P, T])
        osum = sb(mixing, "osum", [P, GT])
        osq = sb(mixing, "osq", [P, GT])
        rms = sb(mixing, "rms", [P, GT])
        mixst = sb(mixing, "mixst", [P, NG, GT])
        scan_mask = sb(mixing, "scan_mask", [P, GT])
        tri = [sb(mixing, f"tri{d}", [P, P]) for d in (FWD, BWD)]
        lbs = sb(mixing, "lbs", [P, HEADS, 6])
        lbcur = sb(mixing, "lbcur", [P, 6])
        lbw = sb(mixing, "lbw", [P, 2, 2, HEADS])
        lbx = sb(mixing, "lbx", [P, 2, HEADS])
        wpool = sb(mixing, "wpool", [P, POOLS, P])
        zeros = sb(mixing, "zeros", [P, D])
        early = sb(mixing, "early", [P, 4, POOL_W])
        xin = early[:, 0:2, 0:D]
        xs = early[:, 2:4, 0:D]
        ptok, pwin, pinv = early[:, 0, :], [early[:, 1, :], early[:, 2, :]], early[:, 3, :]
        pooled = rin[:, :, :, :].rearrange("p a b c -> p (a b c)")[:, 0:POOL_W]
        mixing.pop_all().close()

        experts, projecting, blockwise = ExitStack(), ExitStack(), ExitStack()
        rowc = sb(experts, "rowc", [P, R_N])
        w1t = sb(experts, "w1t", [P, 2, KT, FE])
        w3t = sb(experts, "w3t", [P, 2, KT, FE])
        w2t = sb(experts, "w2t", [P, 2, FT, D])
        logits = sb(experts, "logits", [P, NT, NLOG])
        gate = sb(experts, "gate", [P, NT, 2])
        slot_of = sb(experts, "slot_of", [P, 2, NT], i32)
        token_of = sb(experts, "token_of", [P, MAX_BLOCKS + 1], i32)
        expert_of = sb(experts, "expert_of", [P, MAX_BLOCKS + 1], i32)
        blocks_over = sb(experts, "blocks_over", [P, 1], i32)
        wout = sb(projecting, "wout", [P, KT, D])
        mixt = sb(projecting, "mixt", [P, 2, KT, P])
        xres = sb(projecting, "xres", [P, 2, D])
        x1t = sb(projecting, "x1t", [P, 2, D])
        xnt = sb(projecting, "xnt", [P, 2, D])
        xnT = sb(projecting, "xnT", [P, KT, P])
        rw = sb(projecting, "rw", [P, KT, NLOG])
        projecting.pop_all().close()
        group_rank = sb(blockwise, "group_rank", [P, N_GROUPS])
        expert_rank = sb(blockwise, "expert_rank", [P, NE])
        token_id = sb(blockwise, "token_id", [P, NT])
        lane = sb(blockwise, "lane", [P, P])
        before = sb(blockwise, "before", [P, P])
        masked = sb(blockwise, "masked", [P, NT, NE])
        pick = [sb(blockwise, f"pick{j}", [P, NT, NE]) for j in range(2)]
        work = sb(blockwise, "work", [P, NT, NE])
        slots = sb(blockwise, "slots", [P, NT, NE])
        grp = sb(blockwise, "grp", [P, NT, N_GROUPS])
        top = sb(blockwise, "top", [P, 4, NT])
        offset = sb(blockwise, "offset", [P, NT + 1, NE])
        bcount = sb(blockwise, "bcount", [P, NE])
        bend = sb(blockwise, "bend", [P, NE])
        bcmp = sb(blockwise, "bcmp", [P, (MAX_BLOCKS + 1) * NE])
        bsum = sb(blockwise, "bsum", [P, MAX_BLOCKS + 1])
        where = sb(blockwise, "where", [P, 2, NT])
        whole = sb(blockwise, "whole", [P, 3, 2 * NT], i32)
        parts = sb(blockwise, "parts", [P, 2, 2 * NT])
        hot = sb(blockwise, "hot", [P, 2, P])
        hotb = sb(blockwise, "hotb", [P, 2, MAX_BLOCKS + 1])
        gidx = sb(blockwise, "gidx", [P, 2, 2], i32)
        xg = sb(blockwise, "xg", [P, 2, D])
        xgT = sb(blockwise, "xgT", [P, KT, P])
        sil = sb(blockwise, "sil", [P, FE])
        hid = sb(blockwise, "hid", [P, FE])
        hidT = sb(blockwise, "hidT", [P, FT, P])
        yst = sb(blockwise, "yst", [P, 2, D])
        ya = sb(blockwise, "ya", [P, 2, 2, D])
        blockwise.pop_all().close()
        experts.pop_all().close()

        consts_ready = sem("consts_ready")
        cols_loaded = sem("cols_loaded")
        x_loaded = [sem(f"x_loaded{s}") for s in range(2)]
        y_zeroed = sem("y_zeroed")
        rms_ready = sem("rms_ready")
        rstd_ready = sem("rstd_ready")
        xs_ready = sem("xs_ready")
        xT_ready = sem("xT_ready")
        nT_ready = sem("nT_ready")
        w_loaded = [sem(f"w_loaded{s}") for s in range(SECTIONS)]
        gemm_done = sem("gemm_done")
        usig_ready = sem("usig_ready")
        act_units = sem("act_units")
        dve_units = sem("dve_units")
        u_stored = [sem(f"u_stored{s}") for s in range(3)]
        wpool_loaded = sem("wpool_loaded")
        inv_loaded = sem("inv_loaded")
        pooled_ready = sem("pooled_ready")
        py_ready = sem("py_ready")
        pmix_ready = sem("pmix_ready")
        rin_loaded = [sem(f"rin_loaded{s}") for s in range(2)]
        ogate_loaded = [sem(f"ogate_loaded{s}") for s in range(NG)]
        lbw_ready = sem("lbw_ready")
        lbexp_ready = sem("lbexp_ready")
        lb_ready = sem("lb_ready")
        logf_ready = sem("logf_ready")
        dist_ready = sem("dist_ready")
        exps_ready = sem("exps_ready")
        keys_ready = sem("keys_ready")
        qint_ready = sem("qint_ready")
        kT_ready = sem("kT_ready")
        ktok_ready = sem("ktok_ready")
        kv_ready = sem("kv_ready")
        sc_ready = sem("sc_ready")
        st_ready = sem("st_ready")
        o_ready = sem("o_ready")
        ob_ready = sem("ob_ready")
        osum_ready = sem("osum_ready")
        osq_ready = sem("osq_ready")
        ms_ready = sem("ms_ready")
        rr_ready = sem("rr_ready")
        mix_ready = sem("mix_ready")
        mix_stored = [sem(f"mix_stored{s}") for s in range(NG)]
        wout_loaded = sem("wout_loaded")
        mixt_loaded = [sem(f"mixt_loaded{s}") for s in range(2)]
        xres_loaded = [sem(f"xres_loaded{s}") for s in range(2)]
        wo_ready = sem("wo_ready")
        x1_ready = sem("x1_ready")
        rms2_ready = sem("rms2_ready")
        xn_ready = sem("xn_ready")
        x1_stored = [sem(f"x1_stored{s}") for s in range(2)]
        xn_stored = [sem(f"xn_stored{s}") for s in range(2)]
        xnT_ready = sem("xnT_ready")
        xnT_copied = sem("xnT_copied")
        router_ready = sem("router_ready")
        logits_ready = sem("logits_ready")
        ranks_ready = sem("ranks_ready")
        gexp_ready = sem("gexp_ready")
        gexp_done = sem("gexp_done")
        picks_ready = sem("picks_ready")
        count_ready = sem("count_ready")
        hot_ready = sem("hot_ready")
        hot_used = sem("hot_used")
        routed = sem("routed")
        gidx_ready = sem("gidx_ready")
        pool_turn = sem("pool_turn")
        xg_loaded = [sem(f"xg_loaded{s}") for s in range(2)]
        w1_loaded = [sem(f"w1_loaded{s}") for s in range(2)]
        w3_loaded = [sem(f"w3_loaded{s}") for s in range(2)]
        w2_loaded = [sem(f"w2_loaded{s}") for s in range(2)]
        xgT_ready = sem("xgT_ready")
        xgT_copied = sem("xgT_copied")
        h1_ready = sem("h1_ready")
        h3_ready = sem("h3_ready")
        sil_ready = sem("sil_ready")
        hid_ready = sem("hid_ready")
        hidT_ready = sem("hidT_ready")
        hidT_copied = sem("hidT_copied")
        y_ready = sem("y_ready")
        y_copied = sem("y_copied")
        y_stored = [sem(f"y_stored{s}") for s in range(2)]
        cidx_ready = sem("cidx_ready")
        pair_loaded = [sem(f"pair_loaded{s}") for s in range(2)]
        xc_loaded = [sem(f"xc_loaded{s}") for s in range(2)]
        sum_ready = sem("sum_ready")
        rms3_ready = sem("rms3_ready")
        out_ready = sem("out_ready")
        out_stored = [sem(f"out_stored{s}") for s in range(2)]
        dve_step = sem("dve_step")
        act_step = sem("act_step")
        pool_step = sem("pool_step")

        PROJ = bank[0:3]
        TK, TV, KV, SC, OUT = bank[3:8]
        MS = TV
        CONSTS = 10

        def ge(eng, s, value):
            if not isinstance(value, int) or value > 0:
                eng.wait_ge(s, value)

        class Chain:

            def __init__(self, eng, s):
                self.eng, self.sem, self.base, self.n, self.off, self.per = eng, s, 0, 0, None, 0

            def value(self):
                return self.base + self.n if self.off is None else self.off * self.per + (self.base + self.n)

            def link(self, ins):
                ins.then_inc(self.sem, 1)
                self.n += 1
                self.eng.wait_ge(self.sem, self.value())

            def start(self):
                self.base, self.n = self.base + self.n, 0

            def enter(self, off, per):
                self.start()
                self.off, self.per = off, per

            def leave(self, iterations):
                assert self.n == self.per, (self.n, self.per)
                self.base, self.n, self.off = self.base + self.per * iterations, 0, None

        def heads_loop(eng, chain, body):
            chain.start()
            body(0)
            per = chain.n
            with eng.Fori(1, HEADS - 1) as h:
                chain.enter(h - 1, per)
                body(h)
            chain.leave(HEADS - 2)
            body(HEADS - 1)

        def in_slot(h, n):
            per_head = 16 * sum(3 if STEPS[m][0] == BWD else 2 for m in range(n % 2, NS, 2))
            return h * per_head + 16 * sum(3 if STEPS[m][0] == BWD else 2 for m in range(n % 2, n + 1, 2))

        def unit_number(h, u):
            return h * UNITS + (POOL_UNITS + u)

        def by_dve(u):
            return u // NG in (Q, OG)

        def wait_left_bank(eng, h, u):
            count = sum(by_dve(v) == by_dve(u) for v in range(u + 1))
            per_head = sum(by_dve(v) == by_dve(u) for v in range(UNITS))
            eng.wait_ge(dve_units if by_dve(u) else act_units, h * per_head + (count + (POOL_UNITS if by_dve(u) else 0)))

        block = always.enter_context(nc.Block())

        @block.sync
        def _(sp):
            def load_x(t, s):
                sp.dma_start(xin[:, s, :], x_all[ds(t * P, P), :]).then_inc(x_loaded[s], 16)

            def load_w(column, s):
                sp.dma_start(wsec[:, s, :, :],
                             w_in[:, ds(column, P)].rearrange("(k p) n -> p k n", p=P)).then_inc(w_loaded[s], 16)

            for s in range(2):
                load_x(s, s)
            sp.dma_start(colc[:, :], cols).then_inc(cols_loaded, 16)
            for c in range(POOLS):
                load_w(c * P, c)
            load_w(SECTION_COLUMN[4], 4)
            sp.dma_start(wpool[:, :, :], pool_w.rearrange("g c d -> c g d")).then_inc(wpool_loaded, 16)
            with sp.Fori(1, NT // 2) as i:
                for s in range(2):
                    sp.wait_ge(xs_ready, 2 * i - 1 + s)
                    load_x(2 * i + s, s)
            sp.wait_ge(nT_ready, 2 * NT)
            for c in range(POOLS):
                ge(sp, pooled_ready, c)
                sp.dma_start(pinv, inv_count[c:c + 1, :].to_broadcast([P, POOL_W])).then_inc(inv_loaded, 16)
                sp.wait_ge(gemm_done, (c + 1) * NG)
                load_w(SECTION_COLUMN[c], c)
            for s in range(SECTIONS):
                sp.wait_ge(gemm_done, unit_number(0, (s + 1) * NG))
                load_w(SECTION_COLUMN[s] + P, s)

            def recurrence_loads(h):
                for s in range(3):
                    sp.wait_ge(u_stored[s], h * (16 * SECTIONS) + 16 * SECTIONS)
                for n, (d, g) in enumerate(STEPS):
                    ge(sp, kT_ready, h * NS + (n - 1))
                    for j, sec in enumerate((Q, FF + d, VAL)[:3 if d == BWD else 2]):
                        sp.dma_start(rin[:, n % 2, j, :],
                                     u_dram[ds((h * SECTIONS + sec) * P, P), g * GT:(g + 1) * GT]
                                     ).then_inc(rin_loaded[n % 2], 16)
                    if d == BWD:
                        gg = NG - 1 - g
                        ge(sp, mix_ready, h * NG + (gg + 1 - NG))
                        sp.dma_start(ogate[:, gg, :],
                                     u_dram[ds((h * SECTIONS + OG) * P, P), gg * GT:(gg + 1) * GT]
                                     ).then_inc(ogate_loaded[gg], 16)
                    for sec in (() if isinstance(h, int) and h >= HEADS - 2 else W_LOADS[n]):
                        sp.wait_ge(gemm_done, unit_number(h + 1, (sec + 1) * NG))
                        load_w(h * P + (SECTION_COLUMN[sec] + 2 * P), sec)

            recurrence_loads(0)
            with sp.Fori(1, HEADS - 2) as h:
                recurrence_loads(h)
            recurrence_loads(HEADS - 2)
            recurrence_loads(HEADS - 1)

            sp.wait_ge(y_zeroed, 16)
            for g in range(NG):
                sp.wait_ge(mix_stored[g], 16 * (POOLS + HEADS))
            sp.dma_start(wout[:, :, :], w_out.rearrange("(k p) n -> p k n", p=P)).then_inc(wout_loaded, 16)
            sp.dma_start(rw[:, :, :], router_w.rearrange("(k p) n -> p k n", p=P)).then_inc(wout_loaded, 16)
            sp.dma_start(rowc[:, :], rows).then_inc(wout_loaded, 16)

            def load_tile(t, s):
                sp.dma_start(mixt[:, s, :, :],
                             mix_dram[:, ds(t * P, P)].rearrange("(k p) n -> p k n", p=P)).then_inc(mixt_loaded[s], 16)
                sp.dma_start(xres[:, s, :], x_all[ds(t * P, P), :]).then_inc(xres_loaded[s], 16)

            def store_tile(t, s):
                sp.wait_ge(xn_ready, t + 1)
                sp.dma_start(x1_dram[ds(t * P, P), :], x1t[:, s, :]).then_inc(x1_stored[s], 16)
                sp.dma_start(xn_dram[ds(t * P, P), :], xnt[:, s, :]).then_inc(xn_stored[s], 16)

            load_tile(0, 0)
            load_tile(1, 1)
            with sp.Fori(0, NT // 2 - 1) as i:
                for s in range(2):
                    store_tile(2 * i + s, s)
                    load_tile(2 * i + (s + 2), s)
            for s in range(2):
                store_tile(NT - 2 + s, s)

            sp.wait_ge(routed, 1)
            used = sp.value_load(blocks_over[0:1, 0:1], min_val=0, max_val=MAX_BLOCKS - MIN_BLOCKS) + MIN_BLOCKS

            def load_expert(b, s):
                e = sp.value_load(expert_of[0:1, ds(b, 1)], min_val=0, max_val=NE - 1)
                if not isinstance(b, int):
                    sp.wait_ge(h1_ready, b - 1)
                sp.dma_start(w1t[:, s, :, :], w1[ds(e * D, D), :].rearrange("(k p) n -> p k n", p=P)
                             ).then_inc(w1_loaded[s], 16)
                if not isinstance(b, int):
                    sp.wait_ge(h3_ready, b - 1)
                sp.dma_start(w3t[:, s, :, :], w3[ds(e * D, D), :].rearrange("(k p) n -> p k n", p=P)
                             ).then_inc(w3_loaded[s], 16)
                if not isinstance(b, int):
                    sp.wait_ge(y_ready, 2 * b - 2)
                sp.dma_start(w2t[:, s, :, :], w2[ds(e * FE, FE), :].rearrange("(k p) n -> p k n", p=P)
                             ).then_inc(w2_loaded[s], 16)

            load_expert(0, 0)
            load_expert(1, 1)
            with sp.Fori(1, (MAX_BLOCKS + 1) // 2) as i:
                for s in range(2):
                    with sp.If(2 * i + s < used):
                        load_expert(2 * i + s, s)

            def load_x1(t, s):
                if not isinstance(t, int):
                    sp.wait_ge(out_stored[s], 8 * t - 8 * s)
                sp.dma_start(xg[:, s, :], x1_dram[ds(t * P, P), :]).then_inc(xc_loaded[s], 16)

            sp.wait_ge(y_copied, 2 * used)
            load_x1(0, 0)
            load_x1(1, 1)
            with sp.Fori(1, NT // 2) as i:
                for s in range(2):
                    load_x1(2 * i + s, s)
            for s in range(2):
                sp.wait_ge(x1_stored[s], 8 * NT)
                sp.wait_ge(out_stored[s], 8 * NT)

        @block.gpsimd
        def _(pool):
            n = [0]

            def made(ins):
                ins.then_inc(consts_ready, 1)
                n[0] += 1
                pool.wait_ge(consts_ready, n[0])

            made(pool.memset(ident[:, :], 0.0))
            made(pool.affine_select(out=ident[:, :], in_=ident[:, :], compare_op=ALU.not_equal, fill=1.0,
                                    base=0, pattern=[[-1, P]], channel_multiplier=1))
            made(pool.memset(ones[:, :], 1.0))
            made(pool.memset(eps_col[:, :], EPS))
            made(pool.memset(scan_mask[:, :], 1.0))
            made(pool.memset(scan_mask[:, :].rearrange("p (b c) -> p b c", c=P)[:, :, 0:1], 0.0))
            for d in (FWD, BWD):
                sign = 1 if d == FWD else -1
                made(pool.affine_select(out=tri[d][:, :], in_=ones[:, :], compare_op=ALU.is_ge, fill=0.0,
                                        base=0, pattern=[[sign, P]], channel_multiplier=-sign))
            assert n[0] == CONSTS - 2
            pool.memset(zeros[:, :], 0.0)
            for d in (FWD, BWD):
                pool.memset(scT[d][:, :, :], 0.0)
                made(pool.memset(lev[d][:, :, :], 0.0))

            def store_unit(h, u):
                s, (sec, g) = u % 3, divmod(u, NG)
                wait_left_bank(pool, h, u)
                pool.dma_start(u_dram[ds((h * SECTIONS + sec) * P, P), g * GT:(g + 1) * GT],
                               ustage[:, s, :]).then_inc(u_stored[s], 16)

            def store_mix(row, g):
                pool.dma_start(mix_dram[ds(row, P), g * GT:(g + 1) * GT],
                               mixst[:, g, :]).then_inc(mix_stored[g], 16)

            for c in range(POOLS):
                for g in range(NG):
                    pool.wait_ge(pmix_ready, c * NG + g + 1)
                    store_mix(c * P, g)
                if c == POOLS - 2:
                    for u in range(NG):
                        store_unit(0, u)
            for u in range(NG, UNITS):
                store_unit(0, u)

            def recurrence_stores(h):
                more = not static(h, HEADS - 1)
                for u in range(BEFORE if more else 0):
                    store_unit(h + 1, u)
                for n, (d, g) in enumerate(STEPS):
                    if more:
                        store_unit(h + 1, BEFORE + PER_STEP * n)
                    if n > 0 and STEPS[n - 1][0] == FWD:
                        g1 = STEPS[n - 1][1]
                        pool.wait_ge(mix_ready, h * NG + (g1 + 1))
                        store_mix(h * P + POOLS * P, g1)
                    if more:
                        store_unit(h + 1, BEFORE + PER_STEP * n + 1)
                pool.wait_ge(mix_ready, h * NG + NG)
                store_mix(h * P + POOLS * P, NG - 1)

            recurrence_stores(0)
            with pool.Fori(1, HEADS - 1) as h:
                recurrence_stores(h)
            recurrence_stores(HEADS - 1)
            for g in range(NG):
                pool.wait_ge(mix_stored[g], 16 * (POOLS + HEADS))

            pool.wait_ge(logits_ready, NT)
            for s in range(2):
                pool.wait_ge(x1_stored[s], 8 * NT)
                pool.wait_ge(xn_stored[s], 8 * NT)
            pool.iota(group_rank[:, :], pattern=[[-1, N_GROUPS]], base=N_GROUPS, channel_multiplier=0,
                      allow_small_or_imprecise_dtypes=True)
            pool.iota(expert_rank[:, :], pattern=[[-1, NE]], base=NE, channel_multiplier=0,
                      allow_small_or_imprecise_dtypes=True)
            pool.iota(token_id[:, :], pattern=[[P, NT]], base=0, channel_multiplier=1,
                      allow_small_or_imprecise_dtypes=True)
            pool.iota(lane[:, :], pattern=[[1, P]], base=0, channel_multiplier=0,
                      allow_small_or_imprecise_dtypes=True)
            pool.affine_select(out=before[:, :], in_=ones[:, :], compare_op=ALU.is_gt, fill=0.0,
                               base=0, pattern=[[1, P]], channel_multiplier=-1).then_inc(ranks_ready, 1)

            pool.wait_ge(routed, 1)
            used = pool.value_load(blocks_over[0:1, 0:1], min_val=0, max_val=MAX_BLOCKS - MIN_BLOCKS) + MIN_BLOCKS

            def gather_rows(b, s):
                pool.wait_ge(gidx_ready, b + 1)
                pool.sem_inc(pool_turn, 1)
                pool.indirect_dma_start(out=xg[:, s, :], out_offset=None, in_=xn_dram[:, :],
                                        in_offset=bass.IndirectOffsetOnAxis(ap=gidx[:, s, 0:1], axis=0)
                                        ).then_inc(xg_loaded[s], 16)

            gather_rows(0, 0)
            gather_rows(1, 1)
            with pool.Fori(1, (MAX_BLOCKS + 1) // 2) as i:
                for s in range(2):
                    with pool.If(2 * i + s < used + 1):
                        gather_rows(2 * i + s, s)

            for s in range(2):
                pool.wait_ge(y_stored[s], 16 * ((used + (1 - s)) >> 1))
            pool.sem_inc(pool_turn, 1)

            def gather_pair(t, s):
                pool.wait_ge(cidx_ready, t + 1)
                pool.sem_inc(pool_turn, 1)
                for j in range(2):
                    pool.indirect_dma_start(out=ya[:, s, j, :], out_offset=None, in_=y_dram[:, :],
                                            in_offset=bass.IndirectOffsetOnAxis(ap=gidx[:, s, j:j + 1], axis=0)
                                            ).then_inc(pair_loaded[s], 16)

            with pool.Fori(0, NT // 2) as i:
                for s in range(2):
                    gather_pair(2 * i + s, s)
            pool.wait_ge(y_zeroed, 16)

        @block.scalar
        def _(act):
            chain = Chain(act, act_step)
            act.wait_ge(cols_loaded, 16)
            act.wait_ge(consts_ready, CONSTS)

            def normalise(t, s, i):
                act.wait_ge(x_loaded[s], i * 16 + 16)
                ge(act, xT_ready, 2 * t - 2)
                chain.link(act.activation(xs[:, s, :], xin[:, s, :], ACT.Square, accum_out=ss[:, s:s + 1]))
                act.activation(ss[:, s:s + 1], ss[:, s:s + 1], ACT.Sqrt, bias=eps_col[:, 0:1],
                               scale=1.0 / D).then_inc(rms_ready, 1)
                act.wait_ge(rstd_ready, t + 1)
                act.activation(xs[:, s, :], xin[:, s, :], ACT.Copy, scale=rstd[:, s:s + 1]).then_inc(xs_ready, 1)

            for s in range(2):
                normalise(s, s, 0)
            chain.start()
            with act.Fori(1, NT // 2) as i:
                chain.enter(i - 1, 2)
                for s in range(2):
                    normalise(2 * i + s, s, i)
            chain.leave(NT // 2 - 1)

            act.dma_start(y_dram[MIN_BLOCKS * P:SLOTS, :].rearrange("(b p) d -> p b d", p=P),
                          zeros[:, :].unsqueeze(1).to_broadcast([P, MAX_BLOCKS - MIN_BLOCKS, D])
                          ).then_inc(y_zeroed, 16)
            act.wait_ge(lbw_ready, 1)
            act.activation(lbw[:, :, :, :], lbw[:, :, :, :], ACT.Exp).then_inc(lbexp_ready, 1)

            def pool_outputs(c):
                for g in range(NG):
                    act.wait_ge(py_ready, c * NG + g + 1)
                    ge(act, mix_stored[g], 16 * c)
                    act.activation(mixst[:, g, :], bank[3 + g][:, :], ACT.Copy,
                                   scale=colc[:, C_SCALE + c:C_SCALE + c + 1]).then_inc(pmix_ready, 1)

            def gate_unit(h, u):
                act.wait_ge(gemm_done, unit_number(h, u + 1))
                if by_dve(u):
                    ge(act, dve_units, h * (2 * NG) + (sum(by_dve(v) for v in range(u)) + POOL_UNITS))
                    act.activation(usig[:, :], PROJ[u % 3][:, :], ACT.Sigmoid).then_inc(usig_ready, 1)
                else:
                    ge(act, u_stored[u % 3], h * (16 * SECTIONS) + 16 * (u // 3))
                    act.activation(ustage[:, u % 3, :], PROJ[u % 3][:, :],
                                   ACT.Copy if u // NG == VAL else ACT.Sigmoid).then_inc(act_units, 1)

            def log_forget(h, n):
                d = STEPS[n][0]
                act.wait_ge(rin_loaded[n % 2], in_slot(h, n))
                if n == 0:
                    act.wait_ge(lb_ready, h + 1)
                ge(act, dist_ready, h * NS + n)
                act.activation(logf[:, :], rin[:, n % 2, 1, :], ACT.Ln, scale=lbcur[:, 3 * d + 1:3 * d + 2],
                               bias=lbcur[:, 3 * d:3 * d + 1]).then_inc(logf_ready, 1)

            def exponentials(h, n):
                d = STEPS[n][0]
                sign = 1.0 if d == FWD else -1.0
                act.wait_ge(dist_ready, h * NS + (n + 1))
                act.activation(smalle[:, :, :], small[:, :, :], ACT.Exp)
                act.activation(exk[:, :], dist[:, :], ACT.Exp, scale=-sign)
                act.activation(exq[:, :], dist[:, :], ACT.Exp, scale=sign).then_inc(exps_ready, 1)

            def to_tokens(h, n):
                d, g = STEPS[n]
                act.wait_ge(kT_ready, h * NS + (n + 1))
                if d == BWD:
                    act.activation(vtok[:, g * BG:(g + 1) * BG, :],
                                   TV[:, :].rearrange("p (b c) -> p b c", c=P), ACT.Copy)
                act.activation(ktok[:, :, :], TK[:, :].rearrange("p (b c) -> p b c", c=P),
                               ACT.Copy).then_inc(ktok_ready, 1)

            def inverse_rms(h, k):
                act.wait_ge(ms_ready, h * NG + (k + 1))
                ge(act, mix_ready, h * NG + k)
                chain.link(act.activation(rms[:, :], MS[:, :], ACT.Ln, scale=1.0 / P, bias=eps_col[:, 0:1]))
                act.activation(rms[:, :], rms[:, :], ACT.Exp, scale=-0.5).then_inc(rr_ready, 1)

            def outputs(h, n):
                d, g = STEPS[n]
                if d == BWD:
                    act.wait_ge(o_ready, h * NS + (n + 1))
                    act.activation(obwd[:, g * GT:(g + 1) * GT], OUT[:, :], ACT.Copy).then_inc(ob_ready, 1)
                else:
                    act.wait_ge(osum_ready, h * NG + (g + 1))
                    act.activation(osq[:, :], osum[:, :], ACT.Square).then_inc(osq_ready, 1)

            def recurrence(h):
                more = not static(h, HEADS - 1)
                log_forget(h, 0)
                if more:
                    gate_unit(h + 1, 0)
                exponentials(h, 0)
                if more:
                    gate_unit(h + 1, 1)
                for n, (d, g) in enumerate(STEPS):
                    u = BEFORE + PER_STEP * n
                    if more:
                        gate_unit(h + 1, u - 1)
                    to_tokens(h, n)
                    if more:
                        gate_unit(h + 1, u)
                    if n + 1 < NS:
                        log_forget(h, n + 1)
                    if d == FWD and g > 0:
                        inverse_rms(h, g - 1)
                    if n + 1 < NS:
                        exponentials(h, n + 1)
                    outputs(h, n)
                if more:
                    gate_unit(h + 1, UNITS - 1)
                inverse_rms(h, NG - 1)

            for c in range(POOLS - 1):
                pool_outputs(c)
            for u in range(UNITS):
                gate_unit(0, u)
                if u == NG - 1:
                    pool_outputs(POOLS - 1)
            heads_loop(act, chain, recurrence)

            chain.start()

            def square_sum(done, count, x, junk, signal):
                act.wait_ge(done, count)
                chain.link(act.activation(junk, x, ACT.Square, accum_out=ss[:, 0:1]))
                act.activation(ss[:, 1:2], ss[:, 0:1], ACT.Sqrt, bias=eps_col[:, 0:1],
                               scale=1.0 / D).then_inc(signal, 1)

            def copy_xnT(t):
                for half in range(2):
                    act.wait_ge(xnT_ready, 2 * t + (half + 1))
                    act.activation(xnT[:, half * KT // 2:(half + 1) * KT // 2, :],
                                   bank[4 + half][:, :].rearrange("p (k c) -> p k c", c=P),
                                   ACT.Copy).then_inc(xnT_copied, 1)

            def project(t, s):
                if not isinstance(t, int):
                    act.wait_ge(xn_stored[s], 8 * t - 8 * s)
                    act.wait_ge(xnT_ready, 2 * t - 2)
                square_sum(x1_ready, 2 * t + 2, x1t[:, s, :], xnt[:, s, :], rms2_ready)

            project(0, 0)
            copy_xnT(0)
            project(1, 1)
            chain.start()
            with act.Fori(1, NT // 2) as i:
                chain.enter(i - 1, 2)
                for s in range(2):
                    copy_xnT(2 * i + (s - 1))
                    project(2 * i + s, s)
            chain.leave(NT // 2 - 1)
            copy_xnT(NT - 1)

            act.wait_ge(gexp_ready, 1)
            act.activation(grp[:, :, :], grp[:, :, :], ACT.Exp).then_inc(gexp_done, 1)
            act.wait_ge(gexp_ready, 2)
            act.activation(top[:, 1, :], top[:, 1, :], ACT.Exp).then_inc(gexp_done, 1)

            act.wait_ge(routed, 1)
            used = act.value_load(blocks_over[0:1, 0:1], min_val=0, max_val=MAX_BLOCKS - MIN_BLOCKS) + MIN_BLOCKS

            def copy_xgT(b):
                for half in range(2):
                    act.wait_ge(xgT_ready, 2 * b + (half + 1))
                    act.activation(xgT[:, half * KT // 2:(half + 1) * KT // 2, :],
                                   bank[half][:, :].rearrange("p (k c) -> p k c", c=P),
                                   ACT.Copy).then_inc(xgT_copied, 1)

            def store_y(b, s):
                act.wait_ge(y_copied, 2 * b + 2)
                act.dma_start(y_dram[ds(b * P, P), :], yst[:, s, :]).then_inc(y_stored[s], 16)

            def expert_block(b, s):
                act.wait_ge(h1_ready, b + 1)
                ge(act, hid_ready, b)
                act.activation(sil[:, :], bank[2][:, :], ACT.Silu).then_inc(sil_ready, 1)
                copy_xgT(b + 1)
                if not static(b, 0):
                    store_y(b - 1, 1 - s)

            copy_xgT(0)
            expert_block(0, 0)
            with act.Fori(0, (MAX_BLOCKS - 1) // 2) as i:
                for s in (1, 0):
                    b = 2 * i + (2 - s)
                    with act.If(b < used):
                        expert_block(b, s)
            act.wait_ge(y_copied, 2 * used)
            for s in range(2):
                with act.If(((used + (1 - s)) & 1) < 1):
                    act.dma_start(y_dram[ds((used - 1) * P, P), :], yst[:, s, :]).then_inc(y_stored[s], 16)

            def finish(t, s):
                square_sum(sum_ready, t + 1, xg[:, s, :], ya[:, s, 0, :], rms3_ready)
                act.wait_ge(out_ready, t + 1)
                act.dma_start(out[ds(t * P, P), :], ya[:, s, 1, :]).then_inc(out_stored[s], 16)

            chain.start()
            with act.Fori(0, NT // 2) as i:
                chain.enter(i, 2)
                for s in range(2):
                    finish(2 * i + s, s)
            chain.leave(NT // 2)

        @block.vector
        def _(dve):
            chain = Chain(dve, dve_step)
            link = chain.link
            dve.wait_ge(cols_loaded, 16)
            dve.wait_ge(consts_ready, CONSTS)

            def into_nT(t, s):
                dve.wait_ge(rms_ready, t + 1)
                dve.reciprocal(rstd[:, s:s + 1], ss[:, s:s + 1]).then_inc(rstd_ready, 1)
                for half in range(2):
                    k0 = half * KT // 2
                    dve.wait_ge(xT_ready, 2 * t + half + 1)
                    dve.tensor_tensor(nT[:, k0:k0 + KT // 2, ds(t * P, P)],
                                      bank[half][:, :].rearrange("p (k c) -> p k c", c=P),
                                      colc[:, C_MIX + k0:C_MIX + k0 + KT // 2].unsqueeze(2)
                                      .to_broadcast([P, KT // 2, P]), ALU.mult).then_inc(nT_ready, 1)

            rows2 = colc[:, C_LB:C_N].rearrange("p (d r h) -> p d r h", d=2, r=2)
            link(dve.tensor_tensor(lbx[:, :, :], rows2[:, :, 0, :], rows2[:, :, 1, :], ALU.max))
            dve.tensor_tensor(lbw[:, :, :, :], rows2, lbx[:, :, :].unsqueeze(2).to_broadcast([P, 2, 2, HEADS]),
                              ALU.subtract).then_inc(lbw_ready, 1)
            into_nT(0, 0)
            into_nT(1, 1)
            with dve.Fori(1, NT // 2) as i:
                for s in range(2):
                    into_nT(2 * i + s, s)
            dve.wait_ge(lbexp_ready, 1)
            link(dve.tensor_tensor(lbx[:, :, :], lbw[:, :, 0, :], lbw[:, :, 1, :], ALU.add))
            link(dve.reciprocal(lbx[:, :, :], lbx[:, :, :]))
            for d in (FWD, BWD):
                link(dve.tensor_tensor(lbs[:, :, 3 * d], lbw[:, d, 0, :], lbx[:, d, :], ALU.mult))
                link(dve.tensor_scalar(lbs[:, :, 3 * d + 1], lbs[:, :, 3 * d], -1.0, 1.0, ALU.mult, ALU.add))
                link(dve.tensor_scalar(lbs[:, :, 3 * d + 2], lbs[:, :, 3 * d], -1.0, None, ALU.add))
            dve.wait_ge(xT_ready, 2 * NT)
            for c0 in (0, PAD + T_PROMPT, POOL_W - PAD):
                link(dve.memset(ptok[:, c0:c0 + (2 * PAD if c0 == PAD + T_PROMPT else PAD)], 0.0))

            def pool_group(c):
                for g in range(NG):
                    dve.wait_ge(gemm_done, c * NG + g + 1)
                    c0 = pool_column(g * GT)
                    ins = dve.tensor_copy(ptok[:, c0:c0 + GT], PROJ[g][:, :])
                    ins.then_inc(dve_units, 1)
                dve.wait_ge(dve_units, (c + 1) * NG)
                ge(dve, py_ready, c * NG)
                a, b, lo, hi = ptok, pwin[0], 0, POOL_W
                for i in range(c + 1):
                    back, ahead = (1, 0) if i == 0 else (1 << (i - 1), 1 << (i - 1))
                    lo, hi = lo + back, hi - ahead
                    link(dve.tensor_tensor(b[:, lo:hi], a[:, lo - back:hi - back], a[:, lo + ahead:hi + ahead],
                                           ALU.add))
                    a, b = b, (pwin[1] if b is pwin[0] else pwin[0])
                dve.wait_ge(inv_loaded, 16 * (c + 1))
                span = slice(PAD, POOL_W - PAD)
                link(dve.tensor_tensor(a[:, span], a[:, span], pinv[:, span], ALU.mult))
                dve.tensor_tensor(pooled[:, span], a[:, span], ptok[:, span], ALU.subtract).then_inc(pooled_ready, 1)
                dve.wait_ge(pooled_ready, c + 1)

            def silu_unit(h, u):
                if not by_dve(u):
                    return
                ge(dve, u_stored[u % 3], h * (16 * SECTIONS) + 16 * (u // 3))
                dve.wait_ge(usig_ready, h * (2 * NG) + sum(by_dve(v) for v in range(u + 1)))
                dve.tensor_tensor(ustage[:, u % 3, :], usig[:, :], PROJ[u % 3][:, :],
                                  ALU.mult).then_inc(dve_units, 1)

            def subs(x):
                return x[:, :].rearrange("p (s c) -> p s c", c=SUB)

            def blocks(x):
                return x[:, :].rearrange("p (b s c) -> p b s c", s=NSUB, c=SUB)

            def exponents(h, n):
                d = STEPS[n][0]
                if n == 0:
                    dve.tensor_copy(lbcur[:, :], lbs[:, ds(h, 1), :].rearrange("p o c -> p (o c)")).then_inc(lb_ready, 1)
                    dve.wait_ge(lb_ready, h + 1)
                dve.wait_ge(rin_loaded[n % 2], in_slot(h, n))
                dve.tensor_scalar(keep[:, :], rin[:, n % 2, 1, :], lbcur[:, 3 * d + 2:3 * d + 3],
                                  lbcur[:, 3 * d + 1:3 * d + 2], ALU.mult, ALU.add)
                dve.wait_ge(logf_ready, h * NS + (n + 1))
                link(dve.tensor_tensor_scan(cum[:, :], scan_mask[:, :], logf[:, :], 0.0, ALU.mult, ALU.add))
                c4 = blocks(cum)
                last = c4[:, :, NSUB - 1, SUB - 1:SUB]
                link(dve.tensor_copy(small[:, :, 8:9], last))
                if d == FWD:
                    mid = SUB // 2 - 1
                    ref = c4[:, :, :, mid]
                    dve.tensor_copy(small[:, :, 3:7], ref)
                    dve.tensor_tensor(small[:, :, 7:8], small[:, :, 8:9], ref[:, :, NSUB - 1:NSUB], ALU.subtract)
                else:
                    mid = SUB // 2
                    link(dve.tensor_tensor(cum[:, :], cum[:, :], logf[:, :], ALU.subtract))
                    ref = c4[:, :, :, mid]
                    dve.tensor_tensor(small[:, :, 3:7], small[:, :, 8:9].to_broadcast([P, BG, NSUB]), ref,
                                      ALU.subtract)
                    dve.tensor_copy(small[:, :, 7:8], ref[:, :, 0:1])
                dve.tensor_tensor(small[:, :, 0:3], ref[:, :, 1:NSUB], ref[:, :, 0:NSUB - 1], ALU.subtract)
                x = subs(cum)
                dve.tensor_tensor(subs(dist), x, x[:, :, mid:mid + 1].to_broadcast([P, BG * NSUB, SUB]),
                                  ALU.subtract).then_inc(dist_ready, 1)

            def queries_and_keys(h, n):
                d = STEPS[n][0]
                lv = lev[d]
                dve.wait_ge(exps_ready, h * NS + (n + 1))
                ge(dve, sc_ready, h * NS + n)
                link(dve.tensor_tensor(qs[:, :], rin[:, n % 2, 0, :], exq[:, :], ALU.mult))
                diagonal = lv[:, :, :].rearrange("p b (s c) -> p b s c", c=P + SUB)[:, :, :, 0:SUB]
                link(dve.tensor_tensor(diagonal, blocks(keep), blocks(exk), ALU.mult))
                order = range(1, NSUB) if d == FWD else range(NSUB - 2, -1, -1)
                for j in order:
                    src = j - 1 if d == FWD else j + 1
                    lo, hi = (0, SUB * j) if d == FWD else (SUB * (j + 1), P)
                    f = min(j, src)
                    link(dve.tensor_tensor(lv[:, :, j * P + lo:j * P + hi], lv[:, :, src * P + lo:src * P + hi],
                                           smalle[:, :, f:f + 1].to_broadcast([P, BG, hi - lo]), ALU.mult))
                full = (NSUB - 1) * P if d == FWD else 0
                ge(dve, kT_ready, h * NS + n)
                dve.tensor_tensor(kst[:, :].rearrange("p (b c) -> p b c", c=P), lv[:, :, full:full + P],
                                  smalle[:, :, 7:8].to_broadcast([P, BG, P]), ALU.mult).then_inc(keys_ready, 1)

            def state_queries(h, n):
                ge(dve, o_ready, h * NS + n)
                dve.tensor_tensor(blocks(qint), blocks(qs),
                                  smalle[:, :, 3:7].unsqueeze(3).to_broadcast([P, BG, NSUB, SUB]),
                                  ALU.mult).then_inc(qint_ready, 1)

            def states_and_scores(h, n):
                d, g = STEPS[n]
                first, rest = (0, range(BG)) if d == FWD else (BG, range(BG - 1, -1, -1))
                ge(dve, o_ready, h * NS + n)
                if (d, g) in NEW_SEQUENCE:
                    link(dve.memset(state[:, first, :], 0.0))
                else:
                    link(dve.tensor_copy(state[:, first, :], state[:, BG - first, :]))
                dve.wait_ge(kv_ready, h * NS + (n + 1))
                for b in rest:
                    src, dst = (b, b + 1) if d == FWD else (b + 1, b)
                    if b == rest[-1]:
                        dve.wait_ge(sc_ready, h * NS + (n + 1))
                    ins = dve.scalar_tensor_tensor(out=state[:, dst, :], in0=state[:, src, :],
                                                   scalar=smalle[:, b, 8:9], in1=KV[:, b * P:(b + 1) * P],
                                                   op0=ALU.mult, op1=ALU.add)
                    if b == rest[-1]:
                        ins.then_inc(dve_step, 1)
                        chain.n += 1
                    else:
                        link(ins)
                dve.copy_predicated(scT[d][:, :, :], tri[d][:, :].bitcast(u32).unsqueeze(1).to_broadcast([P, BG, P]),
                                    SC[:, :].rearrange("p (b c) -> p b c", c=P)).then_inc(st_ready, 1)

            def sum_outputs(h, n):
                g = STEPS[n][1]
                dve.wait_ge(o_ready, h * NS + (n + 1))
                dve.wait_ge(ob_ready, h * NG + NG)
                dve.tensor_tensor(osum[:, :], OUT[:, :], obwd[:, g * GT:(g + 1) * GT], ALU.add).then_inc(osum_ready, 1)

            def mixer_output(h, g):
                dve.wait_ge(rr_ready, h * NG + (g + 1))
                dve.wait_ge(mix_stored[g], h * 16 + 16 * POOLS)
                link(dve.scalar_tensor_tensor(out=mixst[:, g, :], in0=osum[:, :], scalar=colc[:, C_GAIN:C_GAIN + 1],
                                              in1=rms[:, :], op0=ALU.mult, op1=ALU.mult))
                dve.wait_ge(ogate_loaded[g], h * 16 + 16)
                dve.tensor_tensor(mixst[:, g, :], mixst[:, g, :], ogate[:, g, :], ALU.mult).then_inc(mix_ready, 1)

            def recurrence(h):
                more = not static(h, HEADS - 1)
                exponents(h, 0)
                if more:
                    silu_unit(h + 1, 0)
                queries_and_keys(h, 0)
                if more:
                    silu_unit(h + 1, 1)
                state_queries(h, 0)
                for n, (d, g) in enumerate(STEPS):
                    u = BEFORE + PER_STEP * n
                    if more:
                        silu_unit(h + 1, u - 1)
                        silu_unit(h + 1, u)
                    states_and_scores(h, n)
                    if n + 1 < NS:
                        exponents(h, n + 1)
                    if d == FWD and g > 0:
                        mixer_output(h, g - 1)
                    if n + 1 < NS:
                        queries_and_keys(h, n + 1)
                        state_queries(h, n + 1)
                    if d == FWD:
                        sum_outputs(h, n)
                if more:
                    silu_unit(h + 1, UNITS - 1)
                mixer_output(h, NG - 1)

            for c in range(POOLS):
                pool_group(c)
            for u in range(UNITS):
                silu_unit(0, u)
            heads_loop(dve, chain, recurrence)

            chain.start()

            def residual(t, s):
                dve.wait_ge(xres_loaded[s], t * 8 + (16 - 8 * s))
                if not isinstance(t, int):
                    dve.wait_ge(x1_stored[s], 8 * t - 8 * s)
                for half in range(2):
                    cs = slice(half * 512, (half + 1) * 512)
                    dve.wait_ge(wo_ready, 2 * t + (half + 1))
                    dve.tensor_tensor(x1t[:, s, cs], bank[2 * s + half][:, :], xres[:, s, cs],
                                      ALU.add).then_inc(x1_ready, 1)
                dve.wait_ge(rms2_ready, t + 1)
                link(dve.reciprocal(rstd[:, 0:1], ss[:, 1:2]))
                dve.scalar_tensor_tensor(out=xnt[:, s, :], in0=x1t[:, s, :], scalar=rstd[:, 0:1],
                                         in1=rowc[:, R_FFN:R_FFN + D], op0=ALU.mult,
                                         op1=ALU.mult).then_inc(xn_ready, 1)

            def add_bias(t):
                dve.wait_ge(router_ready, t + 1)
                dve.tensor_tensor(logits[:, ds(t, 1), :].rearrange("p o c -> p (o c)"), bank[6][:, 0:NLOG],
                                  rowc[:, R_BIAS:R_BIAS + NLOG], ALU.add).then_inc(logits_ready, 1)

            dve.wait_ge(wout_loaded, 48)
            residual(0, 0)
            residual(1, 1)
            add_bias(0)
            chain.start()
            with dve.Fori(1, NT // 2) as i:
                chain.enter(i - 1, 2)
                for s in range(2):
                    residual(2 * i + s, s)
                    add_bias(2 * i + (s - 1))
            chain.leave(NT // 2 - 1)
            add_bias(NT - 1)

            dve.wait_ge(ranks_ready, 1)
            dve.wait_ge(logits_ready, NT)
            dve.wait_ge(xnT_copied, 2 * NT)
            BIG = 1.0e30
            over_tiles = [P, NT, NE]

            def spread(x, n):
                return x.unsqueeze(2).to_broadcast([P, NT, n])

            def first_max(values, rank, n, best, scratch_, chosen):
                ranks = rank.unsqueeze(1).to_broadcast([P, NT, n])
                link(dve.tensor_reduce(best, values, axis=AX.X, op=ALU.max))
                link(dve.tensor_tensor(scratch_, values, spread(best, n), ALU.is_equal))
                link(dve.tensor_tensor(scratch_, scratch_, ranks, ALU.mult))
                link(dve.tensor_reduce(top[:, 3, :], scratch_, axis=AX.X, op=ALU.max))
                link(dve.tensor_tensor(chosen, ranks, spread(top[:, 3, :], n), ALU.is_equal))

            g_logits, e_logits = logits[:, :, 0:N_GROUPS], logits[:, :, N_GROUPS:NLOG]
            group_hot = slots[:, :, 0:N_GROUPS]
            first_max(g_logits, group_rank[:, :], N_GROUPS, top[:, 0, :], grp[:, :, :], group_hot)
            dve.tensor_tensor(grp[:, :, :], g_logits, spread(top[:, 0, :], N_GROUPS),
                              ALU.subtract).then_inc(gexp_ready, 1)
            link(dve.tensor_scalar(masked[:, :, 0:N_GROUPS], group_hot, BIG, -BIG, ALU.mult, ALU.add))
            link(dve.tensor_copy(work[:, :, :].rearrange("p t (g e) -> p t g e", g=N_GROUPS),
                                 masked[:, :, 0:N_GROUPS].unsqueeze(3)
                                 .to_broadcast([P, NT, N_GROUPS, PER_GROUP])))
            link(dve.tensor_tensor(masked[:, :, :], work[:, :, :], e_logits, ALU.add))
            first_max(masked[:, :, :], expert_rank[:, :], NE, top[:, 0, :], work[:, :, :], pick[0][:, :, :])
            link(dve.scalar_tensor_tensor(out=masked[:, :, :], in0=pick[0][:, :, :], scalar=-BIG,
                                          in1=masked[:, :, :], op0=ALU.mult, op1=ALU.add))
            first_max(masked[:, :, :], expert_rank[:, :], NE, top[:, 1, :], work[:, :, :], pick[1][:, :, :])
            dve.tensor_tensor(top[:, 1, :], top[:, 1, :], top[:, 0, :], ALU.subtract).then_inc(gexp_ready, 1)
            dve.tensor_tensor(work[:, :, :], pick[0][:, :, :], pick[1][:, :, :], ALU.add).then_inc(picks_ready, 1)
            dve.wait_ge(gexp_done, 2)
            link(dve.tensor_reduce(top[:, 2, :], grp[:, :, :], axis=AX.X, op=ALU.add))
            link(dve.tensor_scalar(top[:, 3, :], top[:, 1, :], 1.0, None, ALU.add))
            link(dve.tensor_tensor(top[:, 2, :], top[:, 2, :], top[:, 3, :], ALU.mult))
            link(dve.reciprocal(top[:, 2, :], top[:, 2, :]))
            link(dve.tensor_copy(gate[:, :, 0], top[:, 2, :]))
            link(dve.tensor_tensor(gate[:, :, 1], top[:, 2, :], top[:, 1, :], ALU.mult))
            dve.wait_ge(count_ready, 1)
            totals = bank[1][:, 0:NT * NE].rearrange("p (t e) -> p t e", e=NE)
            link(dve.memset(offset[:, 0, :], 0.0))
            for t in range(NT):
                link(dve.tensor_tensor(offset[:, t + 1, :], totals[:, t, :], offset[:, t, :], ALU.add))
            link(dve.memset(bcount[:, :], 0.0))
            for j in range(NT):
                link(dve.scalar_tensor_tensor(out=bcount[:, :], in0=offset[:, NT, :], scalar=float(j * P),
                                              in1=bcount[:, :], op0=ALU.is_gt, op1=ALU.add))
            link(dve.memset(bcmp[:, 0:NE], 1.0))
            link(dve.tensor_tensor_scan(bend[:, :], bcmp[:, 0:NE], bcount[:, :], 0.0, ALU.mult, ALU.add))
            link(dve.tensor_scalar(blocks_over[:, :], bend[:, NE - 1:NE], -float(MIN_BLOCKS), None, ALU.add))
            nb = MAX_BLOCKS + 1
            bc3 = bcmp[:, :].rearrange("p (b e) -> p b e", e=NE)
            link(dve.tensor_tensor(bc3[:, :, :], bend[:, :].unsqueeze(1).to_broadcast([P, nb, NE]),
                                   lane[:, 0:nb].unsqueeze(2).to_broadcast([P, nb, NE]), ALU.is_le))
            link(dve.tensor_reduce(bsum[:, :], bc3[:, :, :], axis=AX.X, op=ALU.add))
            link(dve.tensor_scalar(bsum[:, :], bsum[:, :], float(NE - 1), None, ALU.min))
            link(dve.tensor_copy(expert_of[:, :], bsum[:, :]))
            link(dve.tensor_tensor(bend[:, :], bend[:, :], bcount[:, :], ALU.subtract))
            link(dve.tensor_scalar(bend[:, :], bend[:, :], float(P), None, ALU.mult))
            link(dve.tensor_tensor(slots[:, :, :], bank[0][:, 0:NT * NE].rearrange("p (t e) -> p t e", e=NE),
                                   offset[:, 0:NT, :], ALU.add))
            link(dve.tensor_tensor(slots[:, :, :], slots[:, :, :],
                                   bend[:, :].unsqueeze(1).to_broadcast(over_tiles), ALU.add))
            for j in range(2):
                link(dve.tensor_tensor(masked[:, :, :], pick[j][:, :, :], slots[:, :, :], ALU.mult))
                link(dve.tensor_reduce(where[:, j, :], masked[:, :, :], axis=AX.X, op=ALU.add))
            flat = where[:, :, :].rearrange("p j t -> p (j t)")
            link(dve.tensor_copy(slot_of[:, :, :].rearrange("p j t -> p (j t)"), flat))
            link(dve.tensor_copy(whole[:, 0, :], flat))
            link(dve.tensor_single_scalar(whole[:, 1, :], whole[:, 0, :], 7, ALU.logical_shift_right))
            link(dve.tensor_single_scalar(whole[:, 2, :], whole[:, 0, :], P - 1, ALU.bitwise_and))
            link(dve.tensor_copy(parts[:, :, :], whole[:, 1:3, :]))
            for c in range(2 * NT):
                ge(dve, hot_used, c - 1)
                dve.tensor_scalar(hot[:, c % 2, :], lane[:, :], parts[:, 1, c:c + 1], None, ALU.is_equal)
                dve.tensor_scalar(hotb[:, c % 2, :], lane[:, 0:nb], parts[:, 0, c:c + 1],
                                  token_id[:, c % NT:c % NT + 1], ALU.is_equal, ALU.mult).then_inc(hot_ready, 1)
            dve.wait_ge(hot_used, 2 * NT)
            dve.tensor_copy(token_of[:, :], bank[2][:, 0:nb]).then_inc(routed, 1)
            dve.wait_ge(routed, 1)

            used = dve.value_load(blocks_over[0:1, 0:1], min_val=0, max_val=MAX_BLOCKS - MIN_BLOCKS) + MIN_BLOCKS

            def next_rows(b, s):
                if not isinstance(b, int):
                    dve.wait_ge(xg_loaded[s], b * 8 - 8 * s)
                    dve.wait_ge(xgT_ready, 2 * b - 2)
                dve.tensor_copy(gidx[:, s, 0:1], token_of[:, ds(b, 1)]).then_inc(gidx_ready, 1)

            def hidden(b):
                dve.wait_ge(sil_ready, b + 1)
                dve.wait_ge(h3_ready, b + 1)
                ge(dve, hidT_ready, b)
                dve.tensor_tensor(hid[:, :], sil[:, :], bank[3][:, :], ALU.mult).then_inc(hid_ready, 1)

            def copy_hidT(b):
                dve.wait_ge(hidT_ready, b + 1)
                dve.tensor_copy(hidT[:, :, :], bank[4][:, :].rearrange("p (k c) -> p k c", c=P)
                                ).then_inc(hidT_copied, 1)

            def copy_y(b, s):
                if not (isinstance(b, int) and b < 2):
                    dve.wait_ge(y_stored[s], b * 8 - 8 * s)
                for half in range(2):
                    dve.wait_ge(y_ready, 2 * b + (half + 1))
                    dve.tensor_copy(yst[:, s, half * 512:(half + 1) * 512],
                                    bank[5 + half][:, :]).then_inc(y_copied, 1)

            next_rows(0, 0)
            next_rows(1, 1)
            hidden(0)

            def expert_step(b, s):
                next_rows(b + 1, 1 - s)
                copy_hidT(b - 1)
                hidden(b)
                copy_y(b - 1, 1 - s)

            expert_step(1, 1)
            expert_step(2, 0)
            with dve.Fori(1, (MAX_BLOCKS - 1) // 2) as i:
                for s in (1, 0):
                    b = 2 * i + (2 - s)
                    with dve.If(b < used):
                        expert_step(b, s)
            dve.wait_ge(hidT_ready, used)
            dve.tensor_copy(hidT[:, :, :], bank[4][:, :].rearrange("p (k c) -> p k c", c=P)).then_inc(hidT_copied, 1)
            for s in range(2):
                with dve.If(((used + (1 - s)) & 1) < 1):
                    dve.wait_ge(y_stored[s], (used - 1) * 8 - 8 * s)
                    for half in range(2):
                        dve.wait_ge(y_ready, 2 * used - 1 + half)
                        dve.tensor_copy(yst[:, s, half * 512:(half + 1) * 512],
                                        bank[5 + half][:, :]).then_inc(y_copied, 1)

            def pair_rows(t, s):
                if not isinstance(t, int):
                    dve.wait_ge(pair_loaded[s], 16 * t - 16 * s)
                    dve.wait_ge(out_stored[s], 8 * t - 8 * s)
                dve.tensor_copy(gidx[:, s, :], slot_of[:, :, ds(t, 1)].rearrange("p j o -> p (j o)")
                                ).then_inc(cidx_ready, 1)

            def combine(t, s):
                dve.wait_ge(xc_loaded[s], 8 * t + (16 - 8 * s))
                dve.wait_ge(pair_loaded[s], 16 * t + (32 - 16 * s))
                acc = xg[:, s, :]
                g2 = gate[:, ds(t, 1), :].rearrange("p o j -> p (o j)")
                link(dve.scalar_tensor_tensor(out=acc, in0=ya[:, s, 0, :], scalar=g2[:, 0:1], in1=acc,
                                              op0=ALU.mult, op1=ALU.add))
                dve.scalar_tensor_tensor(out=acc, in0=ya[:, s, 1, :], scalar=g2[:, 1:2], in1=acc,
                                         op0=ALU.mult, op1=ALU.add).then_inc(sum_ready, 1)
                dve.wait_ge(rms3_ready, t + 1)
                link(dve.reciprocal(rstd[:, 0:1], ss[:, 1:2]))
                dve.scalar_tensor_tensor(out=ya[:, s, 1, :], in0=acc, scalar=rstd[:, 0:1],
                                         in1=rowc[:, R_FINAL:R_FINAL + D], op0=ALU.mult,
                                         op1=ALU.mult).then_inc(out_ready, 1)

            for s in range(2):
                dve.wait_ge(xg_loaded[s], 16 * ((used + (2 - s)) >> 1))
                pair_rows(s, s)
            chain.start()
            with dve.Fori(0, NT // 2 - 1) as i:
                chain.enter(i, 4)
                for s in range(2):
                    combine(2 * i + s, s)
                    pair_rows(2 * i + (s + 2), s)
            chain.leave(NT // 2 - 1)
            for s in range(2):
                combine(NT - 2 + s, s)

        @block.tensor
        def _(pe):
            pe.wait_ge(consts_ready, CONSTS)

            def transpose_x(t, s):
                pe.wait_ge(xs_ready, t + 1)
                for half in range(2):
                    ge(pe, nT_ready, 2 * t + (half - 1))
                    for k in range(KT // 2):
                        c0 = (half * KT // 2 + k) * P
                        last = pe.transpose(bank[half][:, k * P:(k + 1) * P], xs[:, s, c0:c0 + P], ident[:, :])
                    last.then_inc(xT_ready, 1)

            transpose_x(0, 0)
            transpose_x(1, 1)
            with pe.Fori(1, NT // 2) as i:
                for s in range(2):
                    transpose_x(2 * i + s, s)

            def product(u, slot, g):
                for k in range(KT):
                    last = pe.matmul(PROJ[u % 3][:, :], wsec[:, slot, k, :], nT[:, k, g * GT:(g + 1) * GT],
                                     start=(k == 0), stop=(k == KT - 1))
                last.then_inc(gemm_done, 1)

            def pool_unit(j):
                c, g = divmod(j, NG)
                if g == 0:
                    pe.wait_ge(w_loaded[c], 16)
                ge(pe, dve_units, j - 2)
                product(j, c, g)

            def unit(h, u):
                sec, g = divmod(u, NG)
                if g == 0:
                    pe.wait_ge(w_loaded[sec], h * 16 + (32 if sec < POOLS else 16))
                if u >= 3:
                    wait_left_bank(pe, h, u - 3)
                elif static(h, 0):
                    pe.wait_ge(dve_units, POOL_UNITS - 2 + u)
                else:
                    wait_left_bank(pe, h - 1, UNITS - 3 + u)
                product(u, sec, g)

            def pool_map(c):
                pe.wait_ge(pooled_ready, c + 1)
                if c == 0:
                    pe.wait_ge(wpool_loaded, 16)
                for g in range(NG):
                    ge(pe, pmix_ready, (c - 1) * NG + g + 1)
                    c0 = pool_column(g * GT)
                    pe.matmul(bank[3 + g][:, :], wpool[:, c, :], pooled[:, c0:c0 + GT],
                              start=True, stop=True).then_inc(py_ready, 1)

            pe.wait_ge(nT_ready, 2 * NT)
            for c in range(POOLS):
                for g in range(NG):
                    pool_unit(c * NG + g)
                if c > 0:
                    pool_map(c - 1)
            for u in range(UNITS):
                unit(0, u)
                if u == NG - 1:
                    pool_map(POOLS - 1)

            def to_tokens(h, n):
                d, g = STEPS[n]
                r = h * NS + n
                pe.wait_ge(keys_ready, r + 1)
                ge(pe, ktok_ready, r)
                if d == BWD:
                    ge(pe, rr_ready, h * NG)
                    pe.wait_ge(rin_loaded[n % 2], in_slot(h, n))
                    for b in range(BG):
                        pe.transpose(TV[:, b * P:(b + 1) * P], rin[:, n % 2, 2, b * P:(b + 1) * P], ident[:, :])
                for b in range(BG):
                    last = pe.transpose(TK[:, b * P:(b + 1) * P], kst[:, b * P:(b + 1) * P], ident[:, :])
                last.then_inc(kT_ready, 1)

            def updates_and_scores(h, n):
                d, g = STEPS[n]
                r = h * NS + n
                pe.wait_ge(ktok_ready, r + 1)
                ge(pe, st_ready, r)
                for b in range(BG):
                    last = pe.matmul(KV[:, b * P:(b + 1) * P], ktok[:, b, :], vtok[:, g * BG + b, :],
                                     start=True, stop=True)
                last.then_inc(kv_ready, 1)
                for b in range(BG):
                    for j in range(NSUB):
                        c0 = b * P + j * SUB
                        last = pe.matmul(SC[:, c0:c0 + SUB], lev[d][:, b, j * P:(j + 1) * P], qs[:, c0:c0 + SUB],
                                         start=True, stop=True)
                last.then_inc(sc_ready, 1)

            def block_outputs(h, n):
                d, g = STEPS[n]
                r = h * NS + n
                pe.wait_ge(st_ready, r + 1)
                pe.wait_ge(qint_ready, r + 1)
                if 1 <= n <= NG:
                    pe.wait_ge(ob_ready, h * NG + n)
                else:
                    ge(pe, osum_ready, h * NG + (n - NG if n else 0))
                for b in range(BG):
                    cs = slice(b * P, (b + 1) * P)
                    pe.matmul(OUT[:, cs], vtok[:, g * BG + b, :], scT[d][:, b, :], start=True, stop=False)
                    last = pe.matmul(OUT[:, cs], state[:, b if d == FWD else b + 1, :], qint[:, cs],
                                     start=False, stop=True)
                last.then_inc(o_ready, 1)

            def mean_square(h, g):
                pe.wait_ge(osq_ready, h * NG + (g + 1))
                if g == 0:
                    pe.wait_ge(ktok_ready, h * NS + NG)
                ge(pe, rr_ready, h * NG + g)
                pe.matmul(MS[:, :], ones[:, :], osq[:, :], start=True, stop=True).then_inc(ms_ready, 1)

            def recurrence(h):
                more = not static(h, HEADS - 1)
                for u in range(BEFORE if more else 0):
                    unit(h + 1, u)
                for n, (d, g) in enumerate(STEPS):
                    u = BEFORE + PER_STEP * n
                    to_tokens(h, n)
                    if more:
                        unit(h + 1, u)
                    updates_and_scores(h, n)
                    if d == FWD and g > 0:
                        mean_square(h, g - 1)
                    if more:
                        unit(h + 1, u + 1)
                    block_outputs(h, n)
                mean_square(h, NG - 1)

            recurrence(0)
            with pe.Fori(1, HEADS - 1) as h:
                recurrence(h)
            recurrence(HEADS - 1)

            pe.wait_ge(wout_loaded, 48)

            def project_half(t, s, half):
                if half == 0:
                    pe.wait_ge(mixt_loaded[s], t * 8 + (16 - 8 * s))
                if not (isinstance(t, int) and t < 2):
                    pe.wait_ge(x1_ready, 2 * t - 3 + half)
                for k in range(KT):
                    last = pe.matmul(bank[2 * s + half][:, :], mixt[:, s, k, :],
                                     wout[:, k, half * 512:(half + 1) * 512], start=(k == 0), stop=(k == KT - 1))
                last.then_inc(wo_ready, 1)

            def transpose_tile(t, s):
                pe.wait_ge(xn_ready, t + 1)
                for half in range(2):
                    ge(pe, xnT_copied, 2 * t + (half - 1))
                    for k in range(KT // 2):
                        c0 = (half * KT // 2 + k) * P
                        last = pe.transpose(bank[4 + half][:, k * P:(k + 1) * P], xnt[:, s, c0:c0 + P], ident[:, :])
                    last.then_inc(xnT_ready, 1)

            def route_tile(t):
                pe.wait_ge(xnT_copied, 2 * t + 2)
                ge(pe, logits_ready, t)
                for k in range(KT):
                    last = pe.matmul(bank[6][:, 0:NLOG], xnT[:, k, :], rw[:, k, :],
                                     start=(k == 0), stop=(k == KT - 1))
                last.then_inc(router_ready, 1)

            for t in range(2):
                project_half(t, t, 0)
                if t:
                    transpose_tile(0, 0)
                project_half(t, t, 1)
                if t:
                    route_tile(0)
            with pe.Fori(1, NT // 2) as i:
                for s in range(2):
                    project_half(2 * i + s, s, 0)
                    transpose_tile(2 * i + (s - 1), 1 - s)
                    project_half(2 * i + s, s, 1)
                    route_tile(2 * i + (s - 1))
            transpose_tile(NT - 1, 1)
            route_tile(NT - 1)

            pe.wait_ge(picks_ready, 1)
            chosen = work[:, :, :].rearrange("p t e -> p (t e)")
            pe.matmul(bank[0][:, 0:NT * NE], before[:, :], chosen, start=True, stop=True)
            pe.matmul(bank[1][:, 0:NT * NE], ones[:, :], chosen, start=True, stop=True).then_inc(count_ready, 1)
            nb = MAX_BLOCKS + 1
            for c in range(2 * NT):
                pe.wait_ge(hot_ready, c + 1)
                pe.matmul(bank[2][:, 0:nb], hot[:, c % 2, :], hotb[:, c % 2, :],
                          start=(c == 0), stop=(c == 2 * NT - 1)).then_inc(hot_used, 1)

            pe.wait_ge(routed, 1)
            used = pe.value_load(blocks_over[0:1, 0:1], min_val=0, max_val=MAX_BLOCKS - MIN_BLOCKS) + MIN_BLOCKS

            def transpose_rows(b, s):
                pe.wait_ge(xg_loaded[s], b * 8 + (16 - 8 * s))
                for half in range(2):
                    ge(pe, xgT_copied, 2 * b + (half - 1))
                    for k in range(KT // 2):
                        c0 = (half * KT // 2 + k) * P
                        last = pe.transpose(bank[half][:, k * P:(k + 1) * P], xg[:, s, c0:c0 + P], ident[:, :])
                    last.then_inc(xgT_ready, 1)

            def up(b, s, weights, loaded, out_bank, free, done):
                pe.wait_ge(loaded[s], b * 8 + (16 - 8 * s))
                ge(pe, free, b)
                for k in range(KT):
                    last = pe.matmul(bank[out_bank][:, :], xgT[:, k, :], weights[:, s, k, :],
                                     start=(k == 0), stop=(k == KT - 1))
                last.then_inc(done, 1)

            def first_up(b, s):
                pe.wait_ge(xgT_copied, 2 * b + 2)
                up(b, s, w1t, w1_loaded, 2, sil_ready, h1_ready)

            def second_up(b, s):
                up(b, s, w3t, w3_loaded, 3, hid_ready, h3_ready)

            def transpose_hidden(b):
                pe.wait_ge(hid_ready, b + 1)
                ge(pe, hidT_copied, b)
                for k in range(FT):
                    last = pe.transpose(bank[4][:, k * P:(k + 1) * P], hid[:, k * P:(k + 1) * P], ident[:, :])
                last.then_inc(hidT_ready, 1)

            def down(b, s):
                pe.wait_ge(w2_loaded[s], b * 8 + (16 - 8 * s))
                pe.wait_ge(hidT_copied, b + 1)
                for half in range(2):
                    ge(pe, y_copied, 2 * b + (half - 1))
                    for k in range(FT):
                        last = pe.matmul(bank[5 + half][:, :], hidT[:, k, :], w2t[:, s, k, half * 512:(half + 1) * 512],
                                         start=(k == 0), stop=(k == FT - 1))
                    last.then_inc(y_ready, 1)

            transpose_rows(0, 0)
            first_up(0, 0)
            second_up(0, 0)
            transpose_rows(1, 1)

            def expert_step(b, s):
                first_up(b, s)
                transpose_hidden(b - 1)
                second_up(b, s)
                transpose_rows(b + 1, 1 - s)
                down(b - 1, 1 - s)

            expert_step(1, 1)
            expert_step(2, 0)
            with pe.Fori(1, (MAX_BLOCKS - 1) // 2) as i:
                for s in (1, 0):
                    b = 2 * i + (2 - s)
                    with pe.If(b < used):
                        expert_step(b, s)
            transpose_hidden(used - 1)
            for s in range(2):
                with pe.If(((used + (1 - s)) & 1) < 1):
                    down(used - 1, s)


def kernel(**inputs):
    import numpy as np
    import concourse.bacc as bacc
    from concourse.bass_utils import run_bass_kernel_spmd as run

    nc = bacc.Bacc("TRN2", target_bir_lowering=False, num_devices=1)
    f32 = mybir.dt.float32
    a = {k: np.ascontiguousarray(v) for k, v in inputs.items()}
    cols = np.concatenate([a["norm_mix"].reshape(KT, P).T, a["pool_scale"].reshape(POOLS, P).T,
                           a["hg_norm_gain"].reshape(1, P).T,
                           a["hg_lb_fwd"].reshape(2 * HEADS, P).T, a["hg_lb_bwd"].reshape(2 * HEADS, P).T], axis=1)
    rows = np.concatenate([a["norm_ffn"].reshape(-1), a["norm_final"].reshape(-1),
                           a["router_group_b"].reshape(-1), a["router_expert_b"].reshape(-1)])
    inv = np.ones((POOLS, POOL_W), np.float32)
    for c, w in enumerate(WINDOWS):
        for start, length in ((0, T_PROMPT), (T_PROMPT, T_SAMPLE)):
            t = np.arange(length)
            count = np.clip(t + w // 2, 0, length) - np.clip(t - w // 2, 0, length)
            inv[c, pool_column(start):pool_column(start) + length] = 1.0 / count
    arrays = {
        "x_all": np.concatenate([a["x_prompt"].reshape(-1, D), a["x_sample"].reshape(-1, D)]),
        "w_in": a["w_in"][0], "w_out": a["w_out"][0], "pool_w": a["pool_w"][0],
        "cols": np.ascontiguousarray(cols), "rows": np.broadcast_to(rows, (P, R_N)).copy(), "inv_count": inv,
        "router_w": np.concatenate([a["router_group_w"][0], a["router_expert_w"][0]], axis=1),
        "w1": a["expert_w1"].reshape(NE * D, FE), "w3": a["expert_w3"].reshape(NE * D, FE),
        "w2": a["expert_w2"].reshape(NE * FE, D),
    }
    args = [nc.dram_tensor(k, v.shape, f32, kind="ExternalInput").ap() for k, v in arrays.items()]
    out = nc.dram_tensor("y", (T, D), f32, kind="ExternalOutput").ap()
    trunk_program(nc, *args, out)
    y = run(nc, [arrays], core_ids=[0]).results[0]["y"]
    return y[:T_PROMPT].reshape(1, T_PROMPT, D), y[T_PROMPT:].reshape(1, T_SAMPLE, D)
```

```python
import concourse.bass as bass
from concourse import mybir
from contextlib import ExitStack

P = 128
D = 1024
KT = D // P
T_PROMPT, T_SAMPLE = 1024, 512
T = T_PROMPT + T_SAMPLE
NT = T // P
GT = 512
NG = T // GT
BG = GT // P
HEADS = 4
SUB = 32
NSUB = P // SUB
WIDTH = 512
Q, FF, FB, OG, VAL = range(5)
SECTION_COLUMN = [1 * WIDTH, 2 * WIDTH, 3 * WIDTH, 5 * WIDTH, 4 * WIDTH]
SECTIONS = len(SECTION_COLUMN)
UNITS = SECTIONS * NG
POOLS = 4
POOL_UNITS = POOLS * NG
WINDOWS = (2, 4, 8, 16)
PAD = 8
POOL_W = T + 4 * PAD
EPS = 1e-6
FWD, BWD = 0, 1
STEPS = [(BWD, 2), (BWD, 1), (BWD, 0), (FWD, 0), (FWD, 1), (FWD, 2)]
NEW_SEQUENCE = {(BWD, 2), (BWD, 1), (FWD, 0), (FWD, 2)}
NS = len(STEPS)
BEFORE, PER_STEP = 3, 2
assert BEFORE + NS * PER_STEP == UNITS

W_LOADS = [(), (0,), (), (1,), (2,), (3, 4)]

PK = POOLS + HEADS - 2
HALF = 512
PARTS = 2 * NT
PARTS_PER_STEP = PARTS // NS

N_GROUPS, PER_GROUP = 4, 8
NE = N_GROUPS * PER_GROUP
NLOG = N_GROUPS + NE
FE = 512
FT = FE // P
MAX_BLOCKS = (2 * T + NE * (P - 1)) // P
MIN_BLOCKS = 2 * T // P
BLOCK_COLUMNS = MAX_BLOCKS + 2
C_MIX, C_SCALE, C_GAIN, C_LB = 0, KT, KT + POOLS, KT + POOLS + 1
C_N = C_LB + 4 * HEADS
R_FFN, R_FINAL, R_BIAS = 0, D, 2 * D
R_N = 2 * D + NLOG


def pool_column(t):
    return PAD + t + (2 * PAD if t >= T_PROMPT else 0)


def static(i, value):
    return isinstance(i, int) and i == value


def trunk_program(nc, x_all, w_in, w_out, pool_w, cols, rows, inv_count, router_w,
                  w1, w3, w2, out):
    f32, i32, u32 = mybir.dt.float32, mybir.dt.int32, mybir.dt.uint32
    ALU, ACT, AX = mybir.AluOpType, mybir.ActivationFunctionType, mybir.AxisListType
    ds = bass.ds

    def scratch(name, shape, dt=f32):
        return nc.dram_tensor(name, shape, dt, kind="Internal").ap()

    u_dram = scratch("u_dram", (HEADS * SECTIONS * P, T))
    mix_dram = scratch("mix_dram", (KT * P, T))
    part_dram = scratch("part_dram", (T, D))
    x1_dram = scratch("x1_dram", (T + P, D))
    xn_dram = scratch("xn_dram", (T + P, D))

    always, mixing = ExitStack(), ExitStack()

    def sb(stack, name, shape, dt=f32):
        return stack.enter_context(nc.sbuf_tensor(name, shape, dt))

    with always:
        def sem(name):
            return always.enter_context(nc.semaphore(name))

        bank = [always.enter_context(nc.psum_tensor(f"bank{i}", [P, 512], f32)) for i in range(8)]
        ident = sb(always, "ident", [P, P])
        ones = sb(always, "ones", [P, P])
        colc = sb(always, "colc", [P, C_N])
        eps_col = sb(always, "eps_col", [P, 1])
        ss = sb(always, "ss", [P, 2])
        rstd = sb(always, "rstd", [P, 2])

        wide = sb(always, "wide", [P, KT * T])
        mid = sb(always, "mid", [P, SECTIONS * KT * P])
        early = sb(always, "early", [P, 4 * POOL_W])

        class Region:

            def __init__(self, tensor):
                self.tensor, self.at = tensor, 0

            def take(self, *dims):
                n = 1
                for d in dims:
                    n *= d
                names = "abcd"[:len(dims)]
                flat = self.tensor[:, self.at:self.at + n]
                self.at += n
                if len(dims) == 1:
                    return flat
                return flat.rearrange(f"p ({' '.join(names)}) -> p {' '.join(names)}",
                                      **{c: d for c, d in zip(names[1:], dims[1:])})

        nT = Region(wide).take(KT, T)
        wsec = Region(mid).take(SECTIONS, KT, P)
        in_early = Region(early).take(4, POOL_W)
        xin = in_early[:, 0:2, 0:D]
        xs = in_early[:, 2:4, 0:D]
        ptok, pwin, pinv = in_early[:, 0, :], [in_early[:, 1, :], in_early[:, 2, :]], in_early[:, 3, :]
        region = Region(wide)
        wout = region.take(KT, D)
        x1t = region.take(2, D)
        xnt = region.take(2, D)
        region = Region(mid)
        mixp = region.take(2, PK, P)
        xp = region.take(2, D)
        mixt = region.take(2, KT - PK, P)
        region = Region(early)
        rowc = region.take(R_N)
        rw = region.take(KT, NLOG)
        xres = region.take(2, D)
        xnT = region.take(KT, P)
        logits = region.take(NT, NLOG)
        w2t = Region(wide).take(2, FT, D)
        region = Region(mid)
        xg = region.take(2, D)
        yst = region.take(2, D)

        ustage = sb(mixing, "ustage", [P, 3, GT])
        usig = sb(mixing, "usig", [P, GT])
        rin = sb(mixing, "rin", [P, 2, 3, GT])
        ogate = sb(mixing, "ogate", [P, NG, GT])
        keep = sb(mixing, "keep", [P, GT])
        logf = sb(mixing, "logf", [P, GT])
        cum = sb(mixing, "cum", [P, GT])
        dist = sb(mixing, "dist", [P, GT])
        exq = sb(mixing, "exq", [P, GT])
        exk = sb(mixing, "exk", [P, GT])
        LW = NSUB * (P + SUB)
        lev = [sb(mixing, f"lev{d}", [P, BG, LW]) for d in (FWD, BWD)]
        small = sb(mixing, "small", [P, BG, 9])
        smalle = sb(mixing, "smalle", [P, BG, 9])
        qs = sb(mixing, "qs", [P, GT])
        qint = sb(mixing, "qint", [P, GT])
        kst = sb(mixing, "kst", [P, GT])
        ktok = sb(mixing, "ktok", [P, BG, P])
        vtok = sb(mixing, "vtok", [P, NT, P])
        scT = [sb(mixing, f"scT{d}", [P, BG, P]) for d in (FWD, BWD)]
        state = sb(mixing, "state", [P, BG + 1, P])
        obwd = sb(mixing, "obwd", [P, T])
        osum = sb(mixing, "osum", [P, GT])
        osq = sb(mixing, "osq", [P, GT])
        rms = sb(mixing, "rms", [P, GT])
        mixst = sb(mixing, "mixst", [P, NG, GT])
        scan_mask = sb(mixing, "scan_mask", [P, GT])
        tri = [sb(mixing, f"tri{d}", [P, P]) for d in (FWD, BWD)]
        lbs = sb(mixing, "lbs", [P, HEADS, 6])
        lbcur = sb(mixing, "lbcur", [P, 6])
        lbw = sb(mixing, "lbw", [P, 2, 2, HEADS])
        lbx = sb(mixing, "lbx", [P, 2, HEADS])
        wpool = sb(mixing, "wpool", [P, POOLS, P])
        zeros = sb(mixing, "zeros", [P, D])
        pooled = rin[:, :, :, :].rearrange("p a b c -> p (a b c)")[:, 0:POOL_W]
        mixing.pop_all().close()

        experts, blockwise = ExitStack(), ExitStack()
        wup = sb(experts, "wup", [P, 2, 2, KT, FE])
        w1t, w3t = wup[:, :, 0, :, :], wup[:, :, 1, :, :]
        final = wup[:, :, :, :, :].rearrange("p s w k n -> p (s w k n)")[:, 0:NT * D].rearrange(
            "p (t d) -> p t d", d=D)
        gate = sb(experts, "gate", [P, NT, 2])
        token_of = sb(experts, "token_of", [P, BLOCK_COLUMNS], i32)
        gate_of = sb(experts, "gate_of", [P, BLOCK_COLUMNS])
        expert_of = sb(experts, "expert_of", [P, BLOCK_COLUMNS], i32)
        blocks_over = sb(experts, "blocks_over", [P, 1], i32)
        group_rank = sb(blockwise, "group_rank", [P, N_GROUPS])
        expert_rank = sb(blockwise, "expert_rank", [P, NE])
        token_id = sb(blockwise, "token_id", [P, NT])
        row_id = sb(blockwise, "row_id", [P, 1])
        lane = sb(blockwise, "lane", [P, P])
        before = sb(blockwise, "before", [P, P])
        masked = sb(blockwise, "masked", [P, NT, NE])
        pick = [sb(blockwise, f"pick{j}", [P, NT, NE]) for j in range(2)]
        work = sb(blockwise, "work", [P, NT, NE])
        slots = sb(blockwise, "slots", [P, NT, NE])
        grp = sb(blockwise, "grp", [P, NT, N_GROUPS])
        top = sb(blockwise, "top", [P, 4, NT])
        offset = sb(blockwise, "offset", [P, NT + 1, NE])
        bcount = sb(blockwise, "bcount", [P, NE])
        bend = sb(blockwise, "bend", [P, NE])
        bcmp = sb(blockwise, "bcmp", [P, BLOCK_COLUMNS * NE])
        bsum = sb(blockwise, "bsum", [P, BLOCK_COLUMNS])
        where = sb(blockwise, "where", [P, 2, NT])
        whole = sb(blockwise, "whole", [P, 3, 2 * NT], i32)
        parts = sb(blockwise, "parts", [P, 2, 2 * NT])
        hot = sb(blockwise, "hot", [P, 2, P])
        hotb = sb(blockwise, "hotb", [P, 2, 2, BLOCK_COLUMNS])
        slot_free = sb(blockwise, "slot_free", [P, BLOCK_COLUMNS])
        gidx = sb(blockwise, "gidx", [P, 2], i32)
        sidx = sb(blockwise, "sidx", [P, 2], i32)
        xgT = sb(blockwise, "xgT", [P, KT, P])
        sil = sb(blockwise, "sil", [P, FE])
        hid = sb(blockwise, "hid", [P, FE])
        hidT = sb(blockwise, "hidT", [P, FT, P])
        junk = sb(blockwise, "junk", [P, D])
        fss = sb(blockwise, "fss", [P, 3, NT])
        blockwise.pop_all().close()
        experts.pop_all().close()

        consts_ready = sem("consts_ready")
        cols_loaded = sem("cols_loaded")
        x_loaded = [sem(f"x_loaded{s}") for s in range(2)]
        tails_zeroed = sem("tails_zeroed")
        rms_ready = sem("rms_ready")
        rstd_ready = sem("rstd_ready")
        xs_ready = sem("xs_ready")
        xT_ready = sem("xT_ready")
        nT_ready = sem("nT_ready")
        w_loaded = [sem(f"w_loaded{s}") for s in range(SECTIONS)]
        gemm_done = sem("gemm_done")
        usig_ready = sem("usig_ready")
        act_units = sem("act_units")
        dve_units = sem("dve_units")
        u_stored = [sem(f"u_stored{s}") for s in range(3)]
        wpool_loaded = sem("wpool_loaded")
        inv_loaded = sem("inv_loaded")
        pooled_ready = sem("pooled_ready")
        py_ready = sem("py_ready")
        pmix_ready = sem("pmix_ready")
        rin_loaded = [sem(f"rin_loaded{s}") for s in range(2)]
        ogate_loaded = [sem(f"ogate_loaded{s}") for s in range(NG)]
        lbw_ready = sem("lbw_ready")
        lbexp_ready = sem("lbexp_ready")
        lb_ready = sem("lb_ready")
        logf_ready = sem("logf_ready")
        dist_ready = sem("dist_ready")
        exps_ready = sem("exps_ready")
        keys_ready = sem("keys_ready")
        qint_ready = sem("qint_ready")
        kT_ready = sem("kT_ready")
        ktok_ready = sem("ktok_ready")
        kv_ready = sem("kv_ready")
        sc_ready = sem("sc_ready")
        st_ready = sem("st_ready")
        o_ready = sem("o_ready")
        ob_ready = sem("ob_ready")
        osum_ready = sem("osum_ready")
        osq_ready = sem("osq_ready")
        ms_ready = sem("ms_ready")
        rr_ready = sem("rr_ready")
        mix_ready = sem("mix_ready")
        mix_stored = [sem(f"mix_stored{s}") for s in range(NG)]
        wout_loaded = sem("wout_loaded")
        wrest_loaded = sem("wrest_loaded")
        mixp_loaded = [sem(f"mixp_loaded{s}") for s in range(2)]
        xp_loaded = [sem(f"xp_loaded{s}") for s in range(2)]
        part_done = sem("part_done")
        part_ready = sem("part_ready")
        part_stored = [sem(f"part_stored{s}") for s in range(3)]
        mixt_loaded = [sem(f"mixt_loaded{s}") for s in range(2)]
        xres_loaded = [sem(f"xres_loaded{s}") for s in range(2)]
        wo_ready = sem("wo_ready")
        x1_ready = sem("x1_ready")
        rms2_ready = sem("rms2_ready")
        xn_ready = sem("xn_ready")
        x1_stored = [sem(f"x1_stored{s}") for s in range(2)]
        xn_stored = [sem(f"xn_stored{s}") for s in range(2)]
        xnT_ready = sem("xnT_ready")
        xnT_copied = sem("xnT_copied")
        router_ready = sem("router_ready")
        logits_ready = sem("logits_ready")
        ranks_ready = sem("ranks_ready")
        gexp_ready = sem("gexp_ready")
        gexp_done = sem("gexp_done")
        picks_ready = sem("picks_ready")
        count_ready = sem("count_ready")
        hot_ready = sem("hot_ready")
        hot_used = sem("hot_used")
        routed = sem("routed")
        gidx_ready = sem("gidx_ready")
        pool_turn = sem("pool_turn")
        xg_loaded = [sem(f"xg_loaded{s}") for s in range(2)]
        w1_loaded = [sem(f"w1_loaded{s}") for s in range(2)]
        w3_loaded = [sem(f"w3_loaded{s}") for s in range(2)]
        w2_loaded = [sem(f"w2_loaded{s}") for s in range(2)]
        xgT_ready = sem("xgT_ready")
        xgT_copied = sem("xgT_copied")
        h1_ready = sem("h1_ready")
        h3_ready = sem("h3_ready")
        sil_ready = sem("sil_ready")
        hid_ready = sem("hid_ready")
        hidT_ready = sem("hidT_ready")
        hidT_copied = sem("hidT_copied")
        y_ready = sem("y_ready")
        y_copied = sem("y_copied")
        y_added = [sem(f"y_added{s}") for s in range(2)]
        final_loaded = [sem(f"final_loaded{i}") for i in range(NT // 2)]
        rms3_ready = sem("rms3_ready")
        gain_ready = sem("gain_ready")
        out_ready = sem("out_ready")
        out_stored = sem("out_stored")
        dve_step = sem("dve_step")
        act_step = sem("act_step")
        pool_step = sem("pool_step")

        PROJ = bank[0:3]
        TK, TV, KV, SC, OUT = bank[3:8]
        MS = TV
        CONSTS = 10

        def ge(eng, s, value):
            if not isinstance(value, int) or value > 0:
                eng.wait_ge(s, value)

        class Chain:

            def __init__(self, eng, s):
                self.eng, self.sem, self.base, self.n, self.off, self.per = eng, s, 0, 0, None, 0

            def value(self):
                return self.base + self.n if self.off is None else self.off * self.per + (self.base + self.n)

            def link(self, ins):
                ins.then_inc(self.sem, 1)
                self.n += 1
                self.eng.wait_ge(self.sem, self.value())

            def start(self):
                self.base, self.n = self.base + self.n, 0

            def enter(self, off, per):
                self.start()
                self.off, self.per = off, per

            def leave(self, iterations):
                assert self.n == self.per, (self.n, self.per)
                self.base, self.n, self.off = self.base + self.per * iterations, 0, None

        def heads_loop(eng, chain, body):
            chain.start()
            body(0)
            per = chain.n
            with eng.Fori(1, HEADS - 1) as h:
                chain.enter(h - 1, per)
                body(h)
            chain.leave(HEADS - 2)
            body(HEADS - 1)

        def in_slot(h, n):
            per_head = 16 * sum(3 if STEPS[m][0] == BWD else 2 for m in range(n % 2, NS, 2))
            return h * per_head + 16 * sum(3 if STEPS[m][0] == BWD else 2 for m in range(n % 2, n + 1, 2))

        def unit_number(h, u):
            return h * UNITS + (POOL_UNITS + u)

        def by_dve(u):
            return u // NG in (Q, OG)

        def wait_left_bank(eng, h, u):
            count = sum(by_dve(v) == by_dve(u) for v in range(u + 1))
            per_head = sum(by_dve(v) == by_dve(u) for v in range(UNITS))
            eng.wait_ge(dve_units if by_dve(u) else act_units, h * per_head + (count + (POOL_UNITS if by_dve(u) else 0)))

        block = always.enter_context(nc.Block())

        @block.sync
        def _(sp):
            def load_x(t, s):
                sp.dma_start(xin[:, s, :], x_all[ds(t * P, P), :]).then_inc(x_loaded[s], 16)

            def load_w(column, s):
                sp.dma_start(wsec[:, s, :, :],
                             w_in[:, ds(column, P)].rearrange("(k p) n -> p k n", p=P)).then_inc(w_loaded[s], 16)

            for s in range(2):
                load_x(s, s)
            sp.dma_start(colc[:, :], cols).then_inc(cols_loaded, 16)
            for c in range(POOLS):
                load_w(c * P, c)
            load_w(SECTION_COLUMN[4], 4)
            sp.dma_start(wpool[:, :, :], pool_w.rearrange("g c d -> c g d")).then_inc(wpool_loaded, 16)
            with sp.Fori(1, NT // 2) as i:
                for s in range(2):
                    sp.wait_ge(xs_ready, 2 * i - 1 + s)
                    load_x(2 * i + s, s)
            sp.wait_ge(nT_ready, 2 * NT)
            for c in range(POOLS):
                ge(sp, pooled_ready, c)
                sp.dma_start(pinv, inv_count[c:c + 1, :].to_broadcast([P, POOL_W])).then_inc(inv_loaded, 16)
                sp.wait_ge(gemm_done, (c + 1) * NG)
                load_w(SECTION_COLUMN[c], c)
            for s in range(SECTIONS):
                sp.wait_ge(gemm_done, unit_number(0, (s + 1) * NG))
                load_w(SECTION_COLUMN[s] + P, s)

            def load_part(t):
                ge(sp, part_ready, 2 * t - 2)
                sp.dma_start(mixp[:, t % 2, :, :],
                             mix_dram[0:PK * P, t * P:(t + 1) * P].rearrange("(k p) n -> p k n", p=P)
                             ).then_inc(mixp_loaded[t % 2], 16)
                sp.dma_start(xp[:, t % 2, :], x_all[t * P:(t + 1) * P, :]).then_inc(xp_loaded[t % 2], 16)

            def load_wout(k0, k1, signal):
                sp.dma_start(wout[:, k0:k1, :],
                             w_out[k0 * P:k1 * P, :].rearrange("(k p) n -> p k n", p=P)).then_inc(signal, 16)

            def recurrence_loads(h):
                for s in range(3):
                    sp.wait_ge(u_stored[s], h * (16 * SECTIONS) + 16 * SECTIONS)
                for n, (d, g) in enumerate(STEPS):
                    if static(h, HEADS - 1) and n == 1:
                        sp.wait_ge(gemm_done, unit_number(HEADS - 1, UNITS))
                        for j in range(NG):
                            sp.wait_ge(mix_stored[j], 16 * PK)
                        load_part(0)
                        load_part(1)
                        load_wout(0, PK, wout_loaded)
                    if static(h, HEADS - 1) and n >= 2:
                        load_part(2 * n - 2)
                        load_part(2 * n - 1)
                    ge(sp, kT_ready, h * NS + (n - 1))
                    for j, sec in enumerate((Q, FF + d, VAL)[:3 if d == BWD else 2]):
                        sp.dma_start(rin[:, n % 2, j, :],
                                     u_dram[ds((h * SECTIONS + sec) * P, P), g * GT:(g + 1) * GT]
                                     ).then_inc(rin_loaded[n % 2], 16)
                    if d == BWD:
                        gg = NG - 1 - g
                        ge(sp, mix_ready, h * NG + (gg + 1 - NG))
                        sp.dma_start(ogate[:, gg, :],
                                     u_dram[ds((h * SECTIONS + OG) * P, P), gg * GT:(gg + 1) * GT]
                                     ).then_inc(ogate_loaded[gg], 16)
                    for sec in (() if isinstance(h, int) and h >= HEADS - 2 else W_LOADS[n]):
                        sp.wait_ge(gemm_done, unit_number(h + 1, (sec + 1) * NG))
                        load_w(h * P + (SECTION_COLUMN[sec] + 2 * P), sec)

            recurrence_loads(0)
            with sp.Fori(1, HEADS - 2) as h:
                recurrence_loads(h)
            recurrence_loads(HEADS - 2)
            recurrence_loads(HEADS - 1)

            load_part(NT - 2)
            load_part(NT - 1)
            load_wout(PK, KT, wrest_loaded)
            sp.dma_start(rw[:, :, :], router_w.rearrange("(k p) n -> p k n", p=P)).then_inc(wrest_loaded, 16)
            sp.dma_start(rowc, rows).then_inc(wrest_loaded, 16)

            def load_tile(t, s):
                sp.dma_start(mixt[:, s, :, :],
                             mix_dram[PK * P:KT * P, ds(t * P, P)].rearrange("(k p) n -> p k n", p=P)).then_inc(mixt_loaded[s], 16)
                sp.dma_start(xres[:, s, :], part_dram[ds(t * P, P), :]).then_inc(xres_loaded[s], 16)

            def store_tile(t, s):
                sp.wait_ge(xn_ready, t + 1)
                sp.dma_start(x1_dram[ds(t * P, P), :], x1t[:, s, :]).then_inc(x1_stored[s], 16)
                sp.dma_start(xn_dram[ds(t * P, P), :], xnt[:, s, :]).then_inc(xn_stored[s], 16)

            for s in range(3):
                sp.wait_ge(part_stored[s], 16 * PARTS // 3)
            for g in range(NG):
                sp.wait_ge(mix_stored[g], 16 * (POOLS + HEADS))
            load_tile(0, 0)
            load_tile(1, 1)
            with sp.Fori(0, NT // 2 - 1) as i:
                for s in range(2):
                    store_tile(2 * i + s, s)
                    load_tile(2 * i + (s + 2), s)
            for s in range(2):
                store_tile(NT - 2 + s, s)

            sp.wait_ge(tails_zeroed, 32)
            sp.wait_ge(routed, 1)
            used = sp.value_load(blocks_over[0:1, 0:1], min_val=0, max_val=MAX_BLOCKS - MIN_BLOCKS) + MIN_BLOCKS

            def load_expert(b, s):
                e = sp.value_load(expert_of[0:1, ds(b, 1)], min_val=0, max_val=NE - 1)
                if not isinstance(b, int):
                    sp.wait_ge(h1_ready, b - 1)
                sp.dma_start(w1t[:, s, :, :], w1[ds(e * D, D), :].rearrange("(k p) n -> p k n", p=P)
                             ).then_inc(w1_loaded[s], 16)
                if not isinstance(b, int):
                    sp.wait_ge(h3_ready, b - 1)
                sp.dma_start(w3t[:, s, :, :], w3[ds(e * D, D), :].rearrange("(k p) n -> p k n", p=P)
                             ).then_inc(w3_loaded[s], 16)
                if not isinstance(b, int):
                    sp.wait_ge(y_ready, 2 * b - 2)
                sp.dma_start(w2t[:, s, :, :], w2[ds(e * FE, FE), :].rearrange("(k p) n -> p k n", p=P)
                             ).then_inc(w2_loaded[s], 16)

            load_expert(0, 0)
            load_expert(1, 1)
            with sp.Fori(1, (MAX_BLOCKS + 1) // 2) as i:
                for s in range(2):
                    with sp.If(2 * i + s < used):
                        load_expert(2 * i + s, s)

            for s in range(2):
                sp.wait_ge(y_added[s], 16 * ((used + (1 - s)) >> 1))
            for i in range(NT // 2):
                sp.dma_start(final[:, 2 * i:2 * i + 2, :], x1_dram[2 * i * P:(2 * i + 2) * P, :].rearrange(
                    "(t p) d -> p t d", p=P)).then_inc(final_loaded[i], 16)
            with sp.Fori(0, NT) as t:
                sp.wait_ge(out_ready, 2 * t + 2)
                sp.dma_start(out[ds(t * P, P), :], final[:, ds(t, 1), :].rearrange("p o d -> p (o d)")
                             ).then_inc(out_stored, 16)
            for s in range(2):
                sp.wait_ge(x1_stored[s], 8 * NT)
            sp.wait_ge(out_stored, 16 * NT)

        @block.gpsimd
        def _(pool):
            n = [0]

            def made(ins):
                ins.then_inc(consts_ready, 1)
                n[0] += 1
                pool.wait_ge(consts_ready, n[0])

            made(pool.memset(ident[:, :], 0.0))
            made(pool.affine_select(out=ident[:, :], in_=ident[:, :], compare_op=ALU.not_equal, fill=1.0,
                                    base=0, pattern=[[-1, P]], channel_multiplier=1))
            made(pool.memset(ones[:, :], 1.0))
            made(pool.memset(eps_col[:, :], EPS))
            made(pool.memset(scan_mask[:, :], 1.0))
            made(pool.memset(scan_mask[:, :].rearrange("p (b c) -> p b c", c=P)[:, :, 0:1], 0.0))
            for d in (FWD, BWD):
                sign = 1 if d == FWD else -1
                made(pool.affine_select(out=tri[d][:, :], in_=ones[:, :], compare_op=ALU.is_ge, fill=0.0,
                                        base=0, pattern=[[sign, P]], channel_multiplier=-sign))
            assert n[0] == CONSTS - 2
            pool.memset(zeros[:, :], 0.0)
            for d in (FWD, BWD):
                pool.memset(scT[d][:, :, :], 0.0)
                made(pool.memset(lev[d][:, :, :], 0.0))

            def store_unit(h, u):
                s, (sec, g) = u % 3, divmod(u, NG)
                wait_left_bank(pool, h, u)
                pool.dma_start(u_dram[ds((h * SECTIONS + sec) * P, P), g * GT:(g + 1) * GT],
                               ustage[:, s, :]).then_inc(u_stored[s], 16)

            def store_mix(row, g):
                pool.dma_start(mix_dram[ds(row, P), g * GT:(g + 1) * GT],
                               mixst[:, g, :]).then_inc(mix_stored[g], 16)

            for c in range(POOLS):
                for g in range(NG):
                    pool.wait_ge(pmix_ready, c * NG + g + 1)
                    store_mix(c * P, g)
                if c == POOLS - 2:
                    for u in range(NG):
                        store_unit(0, u)
            for u in range(NG, UNITS):
                store_unit(0, u)

            def store_part(v):
                t, half = divmod(v, 2)
                pool.wait_ge(part_ready, v + 1)
                pool.dma_start(part_dram[t * P:(t + 1) * P, half * HALF:(half + 1) * HALF],
                               ustage[:, v % 3, :]).then_inc(part_stored[v % 3], 16)

            def recurrence_stores(h):
                more = not static(h, HEADS - 1)
                for u in range(BEFORE if more else 0):
                    store_unit(h + 1, u)
                for n, (d, g) in enumerate(STEPS):
                    if more:
                        store_unit(h + 1, BEFORE + PER_STEP * n)
                    else:
                        store_part(PARTS_PER_STEP * n)
                        store_part(PARTS_PER_STEP * n + 1)
                    if n > 0 and STEPS[n - 1][0] == FWD:
                        g1 = STEPS[n - 1][1]
                        pool.wait_ge(mix_ready, h * NG + (g1 + 1))
                        store_mix(h * P + POOLS * P, g1)
                    if more:
                        store_unit(h + 1, BEFORE + PER_STEP * n + 1)
                    else:
                        store_part(PARTS_PER_STEP * n + 2)
                        store_part(PARTS_PER_STEP * n + 3)
                pool.wait_ge(mix_ready, h * NG + NG)
                store_mix(h * P + POOLS * P, NG - 1)

            recurrence_stores(0)
            with pool.Fori(1, HEADS - 1) as h:
                recurrence_stores(h)
            recurrence_stores(HEADS - 1)
            for g in range(NG):
                pool.wait_ge(mix_stored[g], 16 * (POOLS + HEADS))

            pool.wait_ge(tails_zeroed, 32)
            pool.iota(group_rank[:, :], pattern=[[-1, N_GROUPS]], base=N_GROUPS, channel_multiplier=0,
                      allow_small_or_imprecise_dtypes=True)
            pool.iota(expert_rank[:, :], pattern=[[-1, NE]], base=NE, channel_multiplier=0,
                      allow_small_or_imprecise_dtypes=True)
            pool.iota(token_id[:, :], pattern=[[P, NT]], base=-T, channel_multiplier=1,
                      allow_small_or_imprecise_dtypes=True)
            pool.iota(lane[:, :], pattern=[[1, P]], base=0, channel_multiplier=0,
                      allow_small_or_imprecise_dtypes=True)
            pool.iota(row_id[:, :], pattern=[[0, 1]], base=0, channel_multiplier=1,
                      allow_small_or_imprecise_dtypes=True)
            pool.affine_select(out=before[:, :], in_=ones[:, :], compare_op=ALU.is_gt, fill=0.0,
                               base=0, pattern=[[1, P]], channel_multiplier=-1).then_inc(ranks_ready, 1)

            pool.wait_ge(routed, 1)
            for s in range(2):
                pool.wait_ge(xn_stored[s], 8 * NT)
                pool.wait_ge(x1_stored[s], 8 * NT)
            used = pool.value_load(blocks_over[0:1, 0:1], min_val=0, max_val=MAX_BLOCKS - MIN_BLOCKS) + MIN_BLOCKS

            def gather_rows(b, s):
                pool.wait_ge(gidx_ready, b + 1)
                pool.sem_inc(pool_turn, 1)
                pool.indirect_dma_start(out=xg[:, s, :], out_offset=None, in_=xn_dram[:, :],
                                        in_offset=bass.IndirectOffsetOnAxis(ap=gidx[:, s:s + 1], axis=0)
                                        ).then_inc(xg_loaded[s], 16)

            def add_outputs(b, s):
                pool.wait_ge(y_copied, 2 * b + 2)
                if not static(b, 0):
                    pool.wait_ge(y_added[1 - s], 8 * b + (8 * s))
                pool.sem_inc(pool_turn, 1)
                pool.indirect_dma_start(out=x1_dram[:, :],
                                        out_offset=bass.IndirectOffsetOnAxis(ap=sidx[:, s:s + 1], axis=0),
                                        in_=yst[:, s, :], in_offset=None, compute_op=ALU.add
                                        ).then_inc(y_added[s], 16)

            for b in range(3):
                gather_rows(b, b % 2)
            gather_rows(3, 1)
            add_outputs(0, 0)
            gather_rows(4, 0)
            add_outputs(1, 1)
            with pool.Fori(1, (MAX_BLOCKS - 1) // 2) as i:
                for s in (1, 0):
                    b = 2 * i + (2 - s)
                    with pool.If(b < used):
                        gather_rows(b + 2, s)
                        add_outputs(b - 1, 1 - s)
            for s in range(2):
                with pool.If(((used + (1 - s)) & 1) < 1):
                    add_outputs(used - 1, s)
            for s in range(2):
                pool.wait_ge(xg_loaded[s], 16 * ((used + (3 - s)) >> 1))

        @block.scalar
        def _(act):
            chain = Chain(act, act_step)
            act.wait_ge(cols_loaded, 16)
            act.wait_ge(consts_ready, CONSTS)

            def normalise(t, s, i):
                act.wait_ge(x_loaded[s], i * 16 + 16)
                ge(act, xT_ready, 2 * t - 2)
                chain.link(act.activation(xs[:, s, :], xin[:, s, :], ACT.Square, accum_out=ss[:, s:s + 1]))
                act.activation(ss[:, s:s + 1], ss[:, s:s + 1], ACT.Sqrt, bias=eps_col[:, 0:1],
                               scale=1.0 / D).then_inc(rms_ready, 1)
                act.wait_ge(rstd_ready, t + 1)
                act.activation(xs[:, s, :], xin[:, s, :], ACT.Copy, scale=rstd[:, s:s + 1]).then_inc(xs_ready, 1)

            for s in range(2):
                normalise(s, s, 0)
            chain.start()
            with act.Fori(1, NT // 2) as i:
                chain.enter(i - 1, 2)
                for s in range(2):
                    normalise(2 * i + s, s, i)
            chain.leave(NT // 2 - 1)

            for x in (x1_dram, xn_dram):
                act.dma_start(x[T:T + P, :], zeros[:, :]).then_inc(tails_zeroed, 16)
            act.wait_ge(lbw_ready, 1)
            act.activation(lbw[:, :, :, :], lbw[:, :, :, :], ACT.Exp).then_inc(lbexp_ready, 1)

            def pool_outputs(c):
                for g in range(NG):
                    act.wait_ge(py_ready, c * NG + g + 1)
                    ge(act, mix_stored[g], 16 * c)
                    act.activation(mixst[:, g, :], bank[3 + g][:, :], ACT.Copy,
                                   scale=colc[:, C_SCALE + c:C_SCALE + c + 1]).then_inc(pmix_ready, 1)

            def gate_unit(h, u):
                act.wait_ge(gemm_done, unit_number(h, u + 1))
                if by_dve(u):
                    ge(act, dve_units, h * (2 * NG) + (sum(by_dve(v) for v in range(u)) + POOL_UNITS))
                    act.activation(usig[:, :], PROJ[u % 3][:, :], ACT.Sigmoid).then_inc(usig_ready, 1)
                else:
                    ge(act, u_stored[u % 3], h * (16 * SECTIONS) + 16 * (u // 3))
                    act.activation(ustage[:, u % 3, :], PROJ[u % 3][:, :],
                                   ACT.Copy if u // NG == VAL else ACT.Sigmoid).then_inc(act_units, 1)

            def log_forget(h, n):
                d = STEPS[n][0]
                act.wait_ge(rin_loaded[n % 2], in_slot(h, n))
                if n == 0:
                    act.wait_ge(lb_ready, h + 1)
                ge(act, dist_ready, h * NS + n)
                act.activation(logf[:, :], rin[:, n % 2, 1, :], ACT.Ln, scale=lbcur[:, 3 * d + 1:3 * d + 2],
                               bias=lbcur[:, 3 * d:3 * d + 1]).then_inc(logf_ready, 1)

            def exponentials(h, n):
                d = STEPS[n][0]
                sign = 1.0 if d == FWD else -1.0
                act.wait_ge(dist_ready, h * NS + (n + 1))
                act.activation(smalle[:, :, :], small[:, :, :], ACT.Exp)
                act.activation(exk[:, :], dist[:, :], ACT.Exp, scale=-sign)
                act.activation(exq[:, :], dist[:, :], ACT.Exp, scale=sign).then_inc(exps_ready, 1)

            def to_tokens(h, n):
                d, g = STEPS[n]
                act.wait_ge(kT_ready, h * NS + (n + 1))
                if d == BWD:
                    act.activation(vtok[:, g * BG:(g + 1) * BG, :],
                                   TV[:, :].rearrange("p (b c) -> p b c", c=P), ACT.Copy)
                act.activation(ktok[:, :, :], TK[:, :].rearrange("p (b c) -> p b c", c=P),
                               ACT.Copy).then_inc(ktok_ready, 1)

            def inverse_rms(h, k):
                act.wait_ge(ms_ready, h * NG + (k + 1))
                ge(act, mix_ready, h * NG + k)
                chain.link(act.activation(rms[:, :], MS[:, :], ACT.Ln, scale=1.0 / P, bias=eps_col[:, 0:1]))
                act.activation(rms[:, :], rms[:, :], ACT.Exp, scale=-0.5).then_inc(rr_ready, 1)

            def outputs(h, n):
                d, g = STEPS[n]
                if d == BWD:
                    act.wait_ge(o_ready, h * NS + (n + 1))
                    act.activation(obwd[:, g * GT:(g + 1) * GT], OUT[:, :], ACT.Copy).then_inc(ob_ready, 1)
                else:
                    act.wait_ge(osum_ready, h * NG + (g + 1))
                    act.activation(osq[:, :], osum[:, :], ACT.Square).then_inc(osq_ready, 1)

            def recurrence(h):
                more = not static(h, HEADS - 1)
                log_forget(h, 0)
                if more:
                    gate_unit(h + 1, 0)
                exponentials(h, 0)
                if more:
                    gate_unit(h + 1, 1)
                for n, (d, g) in enumerate(STEPS):
                    u = BEFORE + PER_STEP * n
                    if more:
                        gate_unit(h + 1, u - 1)
                    to_tokens(h, n)
                    if more:
                        gate_unit(h + 1, u)
                    if n + 1 < NS:
                        log_forget(h, n + 1)
                    if d == FWD and g > 0:
                        inverse_rms(h, g - 1)
                    if n + 1 < NS:
                        exponentials(h, n + 1)
                    outputs(h, n)
                if more:
                    gate_unit(h + 1, UNITS - 1)
                inverse_rms(h, NG - 1)

            for c in range(POOLS - 1):
                pool_outputs(c)
            for u in range(UNITS):
                gate_unit(0, u)
                if u == NG - 1:
                    pool_outputs(POOLS - 1)
            heads_loop(act, chain, recurrence)

            chain.start()

            def square_sum(done, count, x, junk, signal):
                act.wait_ge(done, count)
                chain.link(act.activation(junk, x, ACT.Square, accum_out=ss[:, 0:1]))
                act.activation(ss[:, 1:2], ss[:, 0:1], ACT.Sqrt, bias=eps_col[:, 0:1],
                               scale=1.0 / D).then_inc(signal, 1)

            def copy_xnT(t):
                for half in range(2):
                    act.wait_ge(xnT_ready, 2 * t + (half + 1))
                    act.activation(xnT[:, half * KT // 2:(half + 1) * KT // 2, :],
                                   bank[4 + half][:, :].rearrange("p (k c) -> p k c", c=P),
                                   ACT.Copy).then_inc(xnT_copied, 1)

            def project(t, s):
                if not isinstance(t, int):
                    act.wait_ge(xn_stored[s], 8 * t - 8 * s)
                    act.wait_ge(xnT_ready, 2 * t - 2)
                square_sum(x1_ready, 2 * t + 2, x1t[:, s, :], xnt[:, s, :], rms2_ready)

            project(0, 0)
            copy_xnT(0)
            project(1, 1)
            chain.start()
            with act.Fori(1, NT // 2) as i:
                chain.enter(i - 1, 2)
                for s in range(2):
                    copy_xnT(2 * i + (s - 1))
                    project(2 * i + s, s)
            chain.leave(NT // 2 - 1)
            copy_xnT(NT - 1)

            act.wait_ge(gexp_ready, 1)
            act.activation(grp[:, :, :], grp[:, :, :], ACT.Exp).then_inc(gexp_done, 1)
            act.wait_ge(gexp_ready, 2)
            act.activation(top[:, 1, :], top[:, 1, :], ACT.Exp).then_inc(gexp_done, 1)

            act.wait_ge(routed, 1)
            used = act.value_load(blocks_over[0:1, 0:1], min_val=0, max_val=MAX_BLOCKS - MIN_BLOCKS) + MIN_BLOCKS

            def copy_xgT(b):
                for half in range(2):
                    act.wait_ge(xgT_ready, 2 * b + (half + 1))
                    act.activation(xgT[:, half * KT // 2:(half + 1) * KT // 2, :],
                                   bank[half][:, :].rearrange("p (k c) -> p k c", c=P),
                                   ACT.Copy).then_inc(xgT_copied, 1)

            def expert_block(b, s):
                act.wait_ge(h1_ready, b + 1)
                ge(act, hid_ready, b)
                act.activation(sil[:, :], bank[2][:, :], ACT.Silu).then_inc(sil_ready, 1)
                copy_xgT(b + 1)

            copy_xgT(0)
            expert_block(0, 0)
            with act.Fori(0, (MAX_BLOCKS - 1) // 2) as i:
                for s in (1, 0):
                    b = 2 * i + (2 - s)
                    with act.If(b < used):
                        expert_block(b, s)

            chain.start()
            act.wait_ge(y_copied, 2 * used)
            for t in range(NT):
                if t % 2 == 0:
                    act.wait_ge(final_loaded[t // 2], 16)
                chain.link(act.activation(junk[:, :], final[:, t, :], ACT.Square, accum_out=fss[:, 0, t:t + 1]))
                act.activation(fss[:, 1, t:t + 1], fss[:, 0, t:t + 1], ACT.Sqrt, bias=eps_col[:, 0:1],
                               scale=1.0 / D).then_inc(rms3_ready, 1)

        @block.vector
        def _(dve):
            chain = Chain(dve, dve_step)
            link = chain.link
            dve.wait_ge(cols_loaded, 16)
            dve.wait_ge(consts_ready, CONSTS)

            def into_nT(t, s):
                dve.wait_ge(rms_ready, t + 1)
                dve.reciprocal(rstd[:, s:s + 1], ss[:, s:s + 1]).then_inc(rstd_ready, 1)
                for half in range(2):
                    k0 = half * KT // 2
                    dve.wait_ge(xT_ready, 2 * t + half + 1)
                    dve.tensor_tensor(nT[:, k0:k0 + KT // 2, ds(t * P, P)],
                                      bank[half][:, :].rearrange("p (k c) -> p k c", c=P),
                                      colc[:, C_MIX + k0:C_MIX + k0 + KT // 2].unsqueeze(2)
                                      .to_broadcast([P, KT // 2, P]), ALU.mult).then_inc(nT_ready, 1)

            rows2 = colc[:, C_LB:C_N].rearrange("p (d r h) -> p d r h", d=2, r=2)
            link(dve.tensor_tensor(lbx[:, :, :], rows2[:, :, 0, :], rows2[:, :, 1, :], ALU.max))
            dve.tensor_tensor(lbw[:, :, :, :], rows2, lbx[:, :, :].unsqueeze(2).to_broadcast([P, 2, 2, HEADS]),
                              ALU.subtract).then_inc(lbw_ready, 1)
            into_nT(0, 0)
            into_nT(1, 1)
            with dve.Fori(1, NT // 2) as i:
                for s in range(2):
                    into_nT(2 * i + s, s)
            dve.wait_ge(lbexp_ready, 1)
            link(dve.tensor_tensor(lbx[:, :, :], lbw[:, :, 0, :], lbw[:, :, 1, :], ALU.add))
            link(dve.reciprocal(lbx[:, :, :], lbx[:, :, :]))
            for d in (FWD, BWD):
                link(dve.tensor_tensor(lbs[:, :, 3 * d], lbw[:, d, 0, :], lbx[:, d, :], ALU.mult))
                link(dve.tensor_scalar(lbs[:, :, 3 * d + 1], lbs[:, :, 3 * d], -1.0, 1.0, ALU.mult, ALU.add))
                link(dve.tensor_scalar(lbs[:, :, 3 * d + 2], lbs[:, :, 3 * d], -1.0, None, ALU.add))
            dve.wait_ge(xT_ready, 2 * NT)
            for c0 in (0, PAD + T_PROMPT, POOL_W - PAD):
                link(dve.memset(ptok[:, c0:c0 + (2 * PAD if c0 == PAD + T_PROMPT else PAD)], 0.0))

            def pool_group(c):
                for g in range(NG):
                    dve.wait_ge(gemm_done, c * NG + g + 1)
                    c0 = pool_column(g * GT)
                    ins = dve.tensor_copy(ptok[:, c0:c0 + GT], PROJ[g][:, :])
                    ins.then_inc(dve_units, 1)
                dve.wait_ge(dve_units, (c + 1) * NG)
                ge(dve, py_ready, c * NG)
                a, b, lo, hi = ptok, pwin[0], 0, POOL_W
                for i in range(c + 1):
                    back, ahead = (1, 0) if i == 0 else (1 << (i - 1), 1 << (i - 1))
                    lo, hi = lo + back, hi - ahead
                    link(dve.tensor_tensor(b[:, lo:hi], a[:, lo - back:hi - back], a[:, lo + ahead:hi + ahead],
                                           ALU.add))
                    a, b = b, (pwin[1] if b is pwin[0] else pwin[0])
                dve.wait_ge(inv_loaded, 16 * (c + 1))
                span = slice(PAD, POOL_W - PAD)
                link(dve.tensor_tensor(a[:, span], a[:, span], pinv[:, span], ALU.mult))
                dve.tensor_tensor(pooled[:, span], a[:, span], ptok[:, span], ALU.subtract).then_inc(pooled_ready, 1)
                dve.wait_ge(pooled_ready, c + 1)

            def silu_unit(h, u):
                if not by_dve(u):
                    return
                ge(dve, u_stored[u % 3], h * (16 * SECTIONS) + 16 * (u // 3))
                dve.wait_ge(usig_ready, h * (2 * NG) + sum(by_dve(v) for v in range(u + 1)))
                dve.tensor_tensor(ustage[:, u % 3, :], usig[:, :], PROJ[u % 3][:, :],
                                  ALU.mult).then_inc(dve_units, 1)

            def subs(x):
                return x[:, :].rearrange("p (s c) -> p s c", c=SUB)

            def blocks(x):
                return x[:, :].rearrange("p (b s c) -> p b s c", s=NSUB, c=SUB)

            def exponents(h, n):
                d = STEPS[n][0]
                if n == 0:
                    dve.tensor_copy(lbcur[:, :], lbs[:, ds(h, 1), :].rearrange("p o c -> p (o c)")).then_inc(lb_ready, 1)
                    dve.wait_ge(lb_ready, h + 1)
                dve.wait_ge(rin_loaded[n % 2], in_slot(h, n))
                dve.tensor_scalar(keep[:, :], rin[:, n % 2, 1, :], lbcur[:, 3 * d + 2:3 * d + 3],
                                  lbcur[:, 3 * d + 1:3 * d + 2], ALU.mult, ALU.add)
                dve.wait_ge(logf_ready, h * NS + (n + 1))
                link(dve.tensor_tensor_scan(cum[:, :], scan_mask[:, :], logf[:, :], 0.0, ALU.mult, ALU.add))
                c4 = blocks(cum)
                last = c4[:, :, NSUB - 1, SUB - 1:SUB]
                link(dve.tensor_copy(small[:, :, 8:9], last))
                if d == FWD:
                    mid = SUB // 2 - 1
                    ref = c4[:, :, :, mid]
                    dve.tensor_copy(small[:, :, 3:7], ref)
                    dve.tensor_tensor(small[:, :, 7:8], small[:, :, 8:9], ref[:, :, NSUB - 1:NSUB], ALU.subtract)
                else:
                    mid = SUB // 2
                    link(dve.tensor_tensor(cum[:, :], cum[:, :], logf[:, :], ALU.subtract))
                    ref = c4[:, :, :, mid]
                    dve.tensor_tensor(small[:, :, 3:7], small[:, :, 8:9].to_broadcast([P, BG, NSUB]), ref,
                                      ALU.subtract)
                    dve.tensor_copy(small[:, :, 7:8], ref[:, :, 0:1])
                dve.tensor_tensor(small[:, :, 0:3], ref[:, :, 1:NSUB], ref[:, :, 0:NSUB - 1], ALU.subtract)
                x = subs(cum)
                dve.tensor_tensor(subs(dist), x, x[:, :, mid:mid + 1].to_broadcast([P, BG * NSUB, SUB]),
                                  ALU.subtract).then_inc(dist_ready, 1)

            def queries_and_keys(h, n):
                d = STEPS[n][0]
                lv = lev[d]
                dve.wait_ge(exps_ready, h * NS + (n + 1))
                ge(dve, sc_ready, h * NS + n)
                link(dve.tensor_tensor(qs[:, :], rin[:, n % 2, 0, :], exq[:, :], ALU.mult))
                diagonal = lv[:, :, :].rearrange("p b (s c) -> p b s c", c=P + SUB)[:, :, :, 0:SUB]
                link(dve.tensor_tensor(diagonal, blocks(keep), blocks(exk), ALU.mult))
                order = range(1, NSUB) if d == FWD else range(NSUB - 2, -1, -1)
                for j in order:
                    src = j - 1 if d == FWD else j + 1
                    lo, hi = (0, SUB * j) if d == FWD else (SUB * (j + 1), P)
                    f = min(j, src)
                    link(dve.tensor_tensor(lv[:, :, j * P + lo:j * P + hi], lv[:, :, src * P + lo:src * P + hi],
                                           smalle[:, :, f:f + 1].to_broadcast([P, BG, hi - lo]), ALU.mult))
                full = (NSUB - 1) * P if d == FWD else 0
                ge(dve, kT_ready, h * NS + n)
                dve.tensor_tensor(kst[:, :].rearrange("p (b c) -> p b c", c=P), lv[:, :, full:full + P],
                                  smalle[:, :, 7:8].to_broadcast([P, BG, P]), ALU.mult).then_inc(keys_ready, 1)

            def state_queries(h, n):
                ge(dve, o_ready, h * NS + n)
                dve.tensor_tensor(blocks(qint), blocks(qs),
                                  smalle[:, :, 3:7].unsqueeze(3).to_broadcast([P, BG, NSUB, SUB]),
                                  ALU.mult).then_inc(qint_ready, 1)

            def states_and_scores(h, n):
                d, g = STEPS[n]
                first, rest = (0, range(BG)) if d == FWD else (BG, range(BG - 1, -1, -1))
                ge(dve, o_ready, h * NS + n)
                if (d, g) in NEW_SEQUENCE:
                    link(dve.memset(state[:, first, :], 0.0))
                else:
                    link(dve.tensor_copy(state[:, first, :], state[:, BG - first, :]))
                dve.wait_ge(kv_ready, h * NS + (n + 1))
                for b in rest:
                    src, dst = (b, b + 1) if d == FWD else (b + 1, b)
                    if b == rest[-1]:
                        dve.wait_ge(sc_ready, h * NS + (n + 1))
                    ins = dve.scalar_tensor_tensor(out=state[:, dst, :], in0=state[:, src, :],
                                                   scalar=smalle[:, b, 8:9], in1=KV[:, b * P:(b + 1) * P],
                                                   op0=ALU.mult, op1=ALU.add)
                    if b == rest[-1]:
                        ins.then_inc(dve_step, 1)
                        chain.n += 1
                    else:
                        link(ins)
                dve.copy_predicated(scT[d][:, :, :], tri[d][:, :].bitcast(u32).unsqueeze(1).to_broadcast([P, BG, P]),
                                    SC[:, :].rearrange("p (b c) -> p b c", c=P)).then_inc(st_ready, 1)

            def sum_outputs(h, n):
                g = STEPS[n][1]
                dve.wait_ge(o_ready, h * NS + (n + 1))
                dve.wait_ge(ob_ready, h * NG + NG)
                dve.tensor_tensor(osum[:, :], OUT[:, :], obwd[:, g * GT:(g + 1) * GT], ALU.add).then_inc(osum_ready, 1)

            def mixer_output(h, g):
                dve.wait_ge(rr_ready, h * NG + (g + 1))
                dve.wait_ge(mix_stored[g], h * 16 + 16 * POOLS)
                link(dve.scalar_tensor_tensor(out=mixst[:, g, :], in0=osum[:, :], scalar=colc[:, C_GAIN:C_GAIN + 1],
                                              in1=rms[:, :], op0=ALU.mult, op1=ALU.mult))
                dve.wait_ge(ogate_loaded[g], h * 16 + 16)
                dve.tensor_tensor(mixst[:, g, :], mixst[:, g, :], ogate[:, g, :], ALU.mult).then_inc(mix_ready, 1)

            def add_part(v):
                t, half = divmod(v, 2)
                if half == 0:
                    dve.wait_ge(xp_loaded[t % 2], 16 * (t // 2) + 16)
                if v < 3:
                    dve.wait_ge(u_stored[v % 3], HEADS * 16 * SECTIONS)
                else:
                    dve.wait_ge(part_stored[v % 3], 16 * (v // 3))
                dve.wait_ge(part_done, v + 1)
                dve.tensor_tensor(ustage[:, v % 3, :], PROJ[v % 3][:, :],
                                  xp[:, t % 2, half * HALF:(half + 1) * HALF], ALU.add).then_inc(part_ready, 1)

            def recurrence(h):
                more = not static(h, HEADS - 1)
                exponents(h, 0)
                if more:
                    silu_unit(h + 1, 0)
                queries_and_keys(h, 0)
                if more:
                    silu_unit(h + 1, 1)
                state_queries(h, 0)
                for n, (d, g) in enumerate(STEPS):
                    u = BEFORE + PER_STEP * n
                    if more:
                        silu_unit(h + 1, u - 1)
                        silu_unit(h + 1, u)
                    else:
                        add_part(PARTS_PER_STEP * n)
                        add_part(PARTS_PER_STEP * n + 1)
                    states_and_scores(h, n)
                    if n + 1 < NS:
                        exponents(h, n + 1)
                    if d == FWD and g > 0:
                        mixer_output(h, g - 1)
                    if n + 1 < NS:
                        queries_and_keys(h, n + 1)
                    if not more:
                        add_part(PARTS_PER_STEP * n + 2)
                        add_part(PARTS_PER_STEP * n + 3)
                    if n + 1 < NS:
                        state_queries(h, n + 1)
                    if d == FWD:
                        sum_outputs(h, n)
                if more:
                    silu_unit(h + 1, UNITS - 1)
                mixer_output(h, NG - 1)

            for c in range(POOLS):
                pool_group(c)
            for u in range(UNITS):
                silu_unit(0, u)
            heads_loop(dve, chain, recurrence)

            chain.start()

            def residual(t, s):
                dve.wait_ge(xres_loaded[s], t * 8 + (16 - 8 * s))
                if not isinstance(t, int):
                    dve.wait_ge(x1_stored[s], 8 * t - 8 * s)
                for half in range(2):
                    cs = slice(half * 512, (half + 1) * 512)
                    dve.wait_ge(wo_ready, 2 * t + (half + 1))
                    dve.tensor_tensor(x1t[:, s, cs], bank[2 * s + half][:, :], xres[:, s, cs],
                                      ALU.add).then_inc(x1_ready, 1)
                dve.wait_ge(rms2_ready, t + 1)
                link(dve.reciprocal(rstd[:, 0:1], ss[:, 1:2]))
                dve.scalar_tensor_tensor(out=xnt[:, s, :], in0=x1t[:, s, :], scalar=rstd[:, 0:1],
                                         in1=rowc[:, R_FFN:R_FFN + D], op0=ALU.mult,
                                         op1=ALU.mult).then_inc(xn_ready, 1)

            def add_bias(t):
                dve.wait_ge(router_ready, t + 1)
                dve.tensor_tensor(logits[:, ds(t, 1), :].rearrange("p o c -> p (o c)"), bank[6][:, 0:NLOG],
                                  rowc[:, R_BIAS:R_BIAS + NLOG], ALU.add).then_inc(logits_ready, 1)

            dve.wait_ge(wrest_loaded, 48)
            residual(0, 0)
            residual(1, 1)
            add_bias(0)
            chain.start()
            with dve.Fori(1, NT // 2) as i:
                chain.enter(i - 1, 2)
                for s in range(2):
                    residual(2 * i + s, s)
                    add_bias(2 * i + (s - 1))
            chain.leave(NT // 2 - 1)
            add_bias(NT - 1)

            dve.wait_ge(ranks_ready, 1)
            dve.wait_ge(logits_ready, NT)
            dve.wait_ge(xnT_copied, 2 * NT)
            BIG = 1.0e30
            over_tiles = [P, NT, NE]

            def spread(x, n):
                return x.unsqueeze(2).to_broadcast([P, NT, n])

            def first_max(values, rank, n, best, scratch_, chosen):
                ranks = rank.unsqueeze(1).to_broadcast([P, NT, n])
                link(dve.tensor_reduce(best, values, axis=AX.X, op=ALU.max))
                link(dve.tensor_tensor(scratch_, values, spread(best, n), ALU.is_equal))
                link(dve.tensor_tensor(scratch_, scratch_, ranks, ALU.mult))
                link(dve.tensor_reduce(top[:, 3, :], scratch_, axis=AX.X, op=ALU.max))
                link(dve.tensor_tensor(chosen, ranks, spread(top[:, 3, :], n), ALU.is_equal))

            g_logits, e_logits = logits[:, :, 0:N_GROUPS], logits[:, :, N_GROUPS:NLOG]
            group_hot = slots[:, :, 0:N_GROUPS]
            first_max(g_logits, group_rank[:, :], N_GROUPS, top[:, 0, :], grp[:, :, :], group_hot)
            dve.tensor_tensor(grp[:, :, :], g_logits, spread(top[:, 0, :], N_GROUPS),
                              ALU.subtract).then_inc(gexp_ready, 1)
            link(dve.tensor_scalar(masked[:, :, 0:N_GROUPS], group_hot, BIG, -BIG, ALU.mult, ALU.add))
            link(dve.tensor_copy(work[:, :, :].rearrange("p t (g e) -> p t g e", g=N_GROUPS),
                                 masked[:, :, 0:N_GROUPS].unsqueeze(3)
                                 .to_broadcast([P, NT, N_GROUPS, PER_GROUP])))
            link(dve.tensor_tensor(masked[:, :, :], work[:, :, :], e_logits, ALU.add))
            first_max(masked[:, :, :], expert_rank[:, :], NE, top[:, 0, :], work[:, :, :], pick[0][:, :, :])
            link(dve.scalar_tensor_tensor(out=masked[:, :, :], in0=pick[0][:, :, :], scalar=-BIG,
                                          in1=masked[:, :, :], op0=ALU.mult, op1=ALU.add))
            first_max(masked[:, :, :], expert_rank[:, :], NE, top[:, 1, :], work[:, :, :], pick[1][:, :, :])
            dve.tensor_tensor(top[:, 1, :], top[:, 1, :], top[:, 0, :], ALU.subtract).then_inc(gexp_ready, 1)
            dve.tensor_tensor(work[:, :, :], pick[0][:, :, :], pick[1][:, :, :], ALU.add).then_inc(picks_ready, 1)
            dve.wait_ge(gexp_done, 2)
            link(dve.tensor_reduce(top[:, 2, :], grp[:, :, :], axis=AX.X, op=ALU.add))
            link(dve.tensor_scalar(top[:, 3, :], top[:, 1, :], 1.0, None, ALU.add))
            link(dve.tensor_tensor(top[:, 2, :], top[:, 2, :], top[:, 3, :], ALU.mult))
            link(dve.reciprocal(top[:, 2, :], top[:, 2, :]))
            link(dve.tensor_copy(gate[:, :, 0], top[:, 2, :]))
            link(dve.tensor_tensor(gate[:, :, 1], top[:, 2, :], top[:, 1, :], ALU.mult))
            dve.wait_ge(count_ready, 1)
            totals = bank[1][:, 0:NT * NE].rearrange("p (t e) -> p t e", e=NE)
            link(dve.memset(offset[:, 0, :], 0.0))
            for t in range(NT):
                link(dve.tensor_tensor(offset[:, t + 1, :], totals[:, t, :], offset[:, t, :], ALU.add))
            link(dve.memset(bcount[:, :], 0.0))
            for j in range(NT):
                link(dve.scalar_tensor_tensor(out=bcount[:, :], in0=offset[:, NT, :], scalar=float(j * P),
                                              in1=bcount[:, :], op0=ALU.is_gt, op1=ALU.add))
            link(dve.memset(bcmp[:, 0:NE], 1.0))
            link(dve.tensor_tensor_scan(bend[:, :], bcmp[:, 0:NE], bcount[:, :], 0.0, ALU.mult, ALU.add))
            link(dve.tensor_scalar(blocks_over[:, :], bend[:, NE - 1:NE], -float(MIN_BLOCKS), None, ALU.add))
            nb = BLOCK_COLUMNS
            bc3 = bcmp[:, :].rearrange("p (b e) -> p b e", e=NE)
            link(dve.tensor_tensor(bc3[:, :, :], bend[:, :].unsqueeze(1).to_broadcast([P, nb, NE]),
                                   lane[:, 0:nb].unsqueeze(2).to_broadcast([P, nb, NE]), ALU.is_le))
            link(dve.tensor_reduce(bsum[:, :], bc3[:, :, :], axis=AX.X, op=ALU.add))
            link(dve.tensor_scalar(bsum[:, :], bsum[:, :], float(NE - 1), None, ALU.min))
            link(dve.tensor_copy(expert_of[:, :], bsum[:, :]))
            link(dve.tensor_tensor(bend[:, :], bend[:, :], bcount[:, :], ALU.subtract))
            link(dve.tensor_scalar(bend[:, :], bend[:, :], float(P), None, ALU.mult))
            link(dve.tensor_tensor(slots[:, :, :], bank[0][:, 0:NT * NE].rearrange("p (t e) -> p t e", e=NE),
                                   offset[:, 0:NT, :], ALU.add))
            link(dve.tensor_tensor(slots[:, :, :], slots[:, :, :],
                                   bend[:, :].unsqueeze(1).to_broadcast(over_tiles), ALU.add))
            for j in range(2):
                link(dve.tensor_tensor(masked[:, :, :], pick[j][:, :, :], slots[:, :, :], ALU.mult))
                link(dve.tensor_reduce(where[:, j, :], masked[:, :, :], axis=AX.X, op=ALU.add))
            flat = where[:, :, :].rearrange("p j t -> p (j t)")
            link(dve.tensor_copy(whole[:, 0, :], flat))
            link(dve.tensor_single_scalar(whole[:, 1, :], whole[:, 0, :], 7, ALU.logical_shift_right))
            link(dve.tensor_single_scalar(whole[:, 2, :], whole[:, 0, :], P - 1, ALU.bitwise_and))
            link(dve.tensor_copy(parts[:, :, :], whole[:, 1:3, :]))
            for c in range(2 * NT):
                ge(dve, hot_used, c - 1)
                j, t = divmod(c, NT)
                dve.tensor_scalar(hot[:, c % 2, :], lane[:, :], parts[:, 1, c:c + 1], None, ALU.is_equal)
                dve.tensor_scalar(hotb[:, c % 2, 0, :], lane[:, 0:nb], parts[:, 0, c:c + 1],
                                  token_id[:, t:t + 1], ALU.is_equal, ALU.mult)
                dve.tensor_scalar(hotb[:, c % 2, 1, :], lane[:, 0:nb], parts[:, 0, c:c + 1],
                                  gate[:, t, j:j + 1], ALU.is_equal, ALU.mult).then_inc(hot_ready, 1)
            dve.wait_ge(hot_used, 2 * NT)
            link(dve.tensor_scalar(slot_free[:, :], bank[2][:, 0:nb], 0.0, row_id[:, 0:1], ALU.is_equal, ALU.mult))
            link(dve.scalar_tensor_tensor(out=slot_free[:, :], in0=bank[2][:, 0:nb], scalar=float(T),
                                          in1=slot_free[:, :], op0=ALU.add, op1=ALU.add))
            dve.tensor_copy(gate_of[:, :], bank[2][:, nb:2 * nb])
            dve.tensor_copy(token_of[:, :], slot_free[:, :]).then_inc(routed, 1)
            dve.wait_ge(routed, 1)

            used = dve.value_load(blocks_over[0:1, 0:1], min_val=0, max_val=MAX_BLOCKS - MIN_BLOCKS) + MIN_BLOCKS

            def next_rows(b, s):
                if not (isinstance(b, int) and b < 2):
                    dve.wait_ge(xg_loaded[s], b * 8 - 8 * s)
                    dve.wait_ge(xgT_ready, 2 * b - 2)
                dve.tensor_copy(gidx[:, s:s + 1], token_of[:, ds(b, 1)]).then_inc(gidx_ready, 1)

            def hidden(b):
                dve.wait_ge(sil_ready, b + 1)
                dve.wait_ge(h3_ready, b + 1)
                ge(dve, hidT_ready, b)
                dve.tensor_tensor(hid[:, :], sil[:, :], bank[3][:, :], ALU.mult).then_inc(hid_ready, 1)

            def copy_hidT(b):
                dve.wait_ge(hidT_ready, b + 1)
                dve.tensor_copy(hidT[:, :, :], bank[4][:, :].rearrange("p (k c) -> p k c", c=P)
                                ).then_inc(hidT_copied, 1)

            def copy_y(b, s):
                if not (isinstance(b, int) and b < 2):
                    dve.wait_ge(y_added[s], b * 8 - 8 * s)
                dve.tensor_copy(sidx[:, s:s + 1], token_of[:, ds(b, 1)])
                for half in range(2):
                    dve.wait_ge(y_ready, 2 * b + (half + 1))
                    dve.tensor_scalar(yst[:, s, half * 512:(half + 1) * 512], bank[5 + half][:, :],
                                      gate_of[:, ds(b, 1)], None, ALU.mult).then_inc(y_copied, 1)

            next_rows(0, 0)
            next_rows(1, 1)
            next_rows(2, 0)
            hidden(0)

            def expert_step(b, s):
                next_rows(b + 2, s)
                copy_hidT(b - 1)
                hidden(b)
                copy_y(b - 1, 1 - s)

            expert_step(1, 1)
            expert_step(2, 0)
            with dve.Fori(1, (MAX_BLOCKS - 1) // 2) as i:
                for s in (1, 0):
                    b = 2 * i + (2 - s)
                    with dve.If(b < used):
                        expert_step(b, s)
            dve.wait_ge(hidT_ready, used)
            dve.tensor_copy(hidT[:, :, :], bank[4][:, :].rearrange("p (k c) -> p k c", c=P)).then_inc(hidT_copied, 1)
            for s in range(2):
                with dve.If(((used + (1 - s)) & 1) < 1):
                    copy_y(used - 1, s)

            dve.wait_ge(xgT_copied, 2 * used + 2)
            for half in range(2):
                dve.tensor_copy(bank[half][:, :], rowc[:, R_FINAL + half * 512:R_FINAL + (half + 1) * 512]
                                ).then_inc(gain_ready, 1)
            dve.wait_ge(gain_ready, 2)
            chain.start()
            with dve.Fori(0, NT) as t:
                chain.enter(t, 1)
                dve.wait_ge(rms3_ready, t + 1)
                link(dve.reciprocal(fss[:, 2, ds(t, 1)], fss[:, 1, ds(t, 1)]))
                for half in range(2):
                    x = final[:, ds(t, 1), half * 512:(half + 1) * 512].rearrange("p o d -> p (o d)")
                    dve.scalar_tensor_tensor(out=x, in0=x, scalar=fss[:, 2, ds(t, 1)], in1=bank[half][:, :],
                                             op0=ALU.mult, op1=ALU.mult).then_inc(out_ready, 1)
            chain.leave(NT)

        @block.tensor
        def _(pe):
            pe.wait_ge(consts_ready, CONSTS)

            def transpose_x(t, s):
                pe.wait_ge(xs_ready, t + 1)
                for half in range(2):
                    ge(pe, nT_ready, 2 * t + (half - 1))
                    for k in range(KT // 2):
                        c0 = (half * KT // 2 + k) * P
                        last = pe.transpose(bank[half][:, k * P:(k + 1) * P], xs[:, s, c0:c0 + P], ident[:, :])
                    last.then_inc(xT_ready, 1)

            transpose_x(0, 0)
            transpose_x(1, 1)
            with pe.Fori(1, NT // 2) as i:
                for s in range(2):
                    transpose_x(2 * i + s, s)

            def product(u, slot, g):
                for k in range(KT):
                    last = pe.matmul(PROJ[u % 3][:, :], wsec[:, slot, k, :], nT[:, k, g * GT:(g + 1) * GT],
                                     start=(k == 0), stop=(k == KT - 1))
                last.then_inc(gemm_done, 1)

            def pool_unit(j):
                c, g = divmod(j, NG)
                if g == 0:
                    pe.wait_ge(w_loaded[c], 16)
                ge(pe, dve_units, j - 2)
                product(j, c, g)

            def unit(h, u):
                sec, g = divmod(u, NG)
                if g == 0:
                    pe.wait_ge(w_loaded[sec], h * 16 + (32 if sec < POOLS else 16))
                if u >= 3:
                    wait_left_bank(pe, h, u - 3)
                elif static(h, 0):
                    pe.wait_ge(dve_units, POOL_UNITS - 2 + u)
                else:
                    wait_left_bank(pe, h - 1, UNITS - 3 + u)
                product(u, sec, g)

            def pool_map(c):
                pe.wait_ge(pooled_ready, c + 1)
                if c == 0:
                    pe.wait_ge(wpool_loaded, 16)
                for g in range(NG):
                    ge(pe, pmix_ready, (c - 1) * NG + g + 1)
                    c0 = pool_column(g * GT)
                    pe.matmul(bank[3 + g][:, :], wpool[:, c, :], pooled[:, c0:c0 + GT],
                              start=True, stop=True).then_inc(py_ready, 1)

            pe.wait_ge(nT_ready, 2 * NT)
            for c in range(POOLS):
                for g in range(NG):
                    pool_unit(c * NG + g)
                if c > 0:
                    pool_map(c - 1)
            for u in range(UNITS):
                unit(0, u)
                if u == NG - 1:
                    pool_map(POOLS - 1)

            def to_tokens(h, n):
                d, g = STEPS[n]
                r = h * NS + n
                pe.wait_ge(keys_ready, r + 1)
                ge(pe, ktok_ready, r)
                if d == BWD:
                    ge(pe, rr_ready, h * NG)
                    pe.wait_ge(rin_loaded[n % 2], in_slot(h, n))
                    for b in range(BG):
                        pe.transpose(TV[:, b * P:(b + 1) * P], rin[:, n % 2, 2, b * P:(b + 1) * P], ident[:, :])
                for b in range(BG):
                    last = pe.transpose(TK[:, b * P:(b + 1) * P], kst[:, b * P:(b + 1) * P], ident[:, :])
                last.then_inc(kT_ready, 1)

            def updates_and_scores(h, n):
                d, g = STEPS[n]
                r = h * NS + n
                pe.wait_ge(ktok_ready, r + 1)
                ge(pe, st_ready, r)
                for b in range(BG):
                    last = pe.matmul(KV[:, b * P:(b + 1) * P], ktok[:, b, :], vtok[:, g * BG + b, :],
                                     start=True, stop=True)
                last.then_inc(kv_ready, 1)
                for b in range(BG):
                    for j in range(NSUB):
                        c0 = b * P + j * SUB
                        last = pe.matmul(SC[:, c0:c0 + SUB], lev[d][:, b, j * P:(j + 1) * P], qs[:, c0:c0 + SUB],
                                         start=True, stop=True)
                last.then_inc(sc_ready, 1)

            def block_outputs(h, n):
                d, g = STEPS[n]
                r = h * NS + n
                pe.wait_ge(st_ready, r + 1)
                pe.wait_ge(qint_ready, r + 1)
                if 1 <= n <= NG:
                    pe.wait_ge(ob_ready, h * NG + n)
                else:
                    ge(pe, osum_ready, h * NG + (n - NG if n else 0))
                for b in range(BG):
                    cs = slice(b * P, (b + 1) * P)
                    pe.matmul(OUT[:, cs], vtok[:, g * BG + b, :], scT[d][:, b, :], start=True, stop=False)
                    last = pe.matmul(OUT[:, cs], state[:, b if d == FWD else b + 1, :], qint[:, cs],
                                     start=False, stop=True)
                last.then_inc(o_ready, 1)

            def mean_square(h, g):
                pe.wait_ge(osq_ready, h * NG + (g + 1))
                if g == 0:
                    pe.wait_ge(ktok_ready, h * NS + NG)
                ge(pe, rr_ready, h * NG + g)
                pe.matmul(MS[:, :], ones[:, :], osq[:, :], start=True, stop=True).then_inc(ms_ready, 1)

            def first_part(t):
                if t == 0:
                    pe.wait_ge(wout_loaded, 16)
                pe.wait_ge(mixp_loaded[t % 2], 16 * (t // 2) + 16)
                for half in range(2):
                    v = 2 * t + half
                    if v < 3:
                        wait_left_bank(pe, HEADS - 1, UNITS - 3 + v)
                    else:
                        pe.wait_ge(part_ready, v - 2)
                    for k in range(PK):
                        last = pe.matmul(PROJ[v % 3][:, :], mixp[:, t % 2, k, :],
                                         wout[:, k, half * HALF:(half + 1) * HALF],
                                         start=(k == 0), stop=(k == PK - 1))
                    last.then_inc(part_done, 1)

            def recurrence(h):
                more = not static(h, HEADS - 1)
                for u in range(BEFORE if more else 0):
                    unit(h + 1, u)
                for n, (d, g) in enumerate(STEPS):
                    u = BEFORE + PER_STEP * n
                    to_tokens(h, n)
                    if more:
                        unit(h + 1, u)
                    else:
                        first_part(2 * n)
                    updates_and_scores(h, n)
                    if d == FWD and g > 0:
                        mean_square(h, g - 1)
                    if more:
                        unit(h + 1, u + 1)
                    else:
                        first_part(2 * n + 1)
                    block_outputs(h, n)
                mean_square(h, NG - 1)

            recurrence(0)
            with pe.Fori(1, HEADS - 1) as h:
                recurrence(h)
            recurrence(HEADS - 1)

            pe.wait_ge(wrest_loaded, 48)
            pe.wait_ge(part_ready, PARTS)
            pe.wait_ge(rr_ready, HEADS * NG)

            def project_half(t, s, half):
                if half == 0:
                    pe.wait_ge(mixt_loaded[s], t * 8 + (16 - 8 * s))
                if not (isinstance(t, int) and t < 2):
                    pe.wait_ge(x1_ready, 2 * t - 3 + half)
                for k in range(PK, KT):
                    last = pe.matmul(bank[2 * s + half][:, :], mixt[:, s, k - PK, :],
                                     wout[:, k, half * HALF:(half + 1) * HALF], start=(k == PK), stop=(k == KT - 1))
                last.then_inc(wo_ready, 1)

            def transpose_tile(t, s):
                pe.wait_ge(xn_ready, t + 1)
                for half in range(2):
                    ge(pe, xnT_copied, 2 * t + (half - 1))
                    for k in range(KT // 2):
                        c0 = (half * KT // 2 + k) * P
                        last = pe.transpose(bank[4 + half][:, k * P:(k + 1) * P], xnt[:, s, c0:c0 + P], ident[:, :])
                    last.then_inc(xnT_ready, 1)

            def route_tile(t):
                pe.wait_ge(xnT_copied, 2 * t + 2)
                ge(pe, logits_ready, t)
                for k in range(KT):
                    last = pe.matmul(bank[6][:, 0:NLOG], xnT[:, k, :], rw[:, k, :],
                                     start=(k == 0), stop=(k == KT - 1))
                last.then_inc(router_ready, 1)

            for t in range(2):
                project_half(t, t, 0)
                if t:
                    transpose_tile(0, 0)
                project_half(t, t, 1)
                if t:
                    route_tile(0)
            with pe.Fori(1, NT // 2) as i:
                for s in range(2):
                    project_half(2 * i + s, s, 0)
                    transpose_tile(2 * i + (s - 1), 1 - s)
                    project_half(2 * i + s, s, 1)
                    route_tile(2 * i + (s - 1))
            transpose_tile(NT - 1, 1)
            route_tile(NT - 1)

            pe.wait_ge(picks_ready, 1)
            chosen = work[:, :, :].rearrange("p t e -> p (t e)")
            pe.matmul(bank[0][:, 0:NT * NE], before[:, :], chosen, start=True, stop=True)
            pe.matmul(bank[1][:, 0:NT * NE], ones[:, :], chosen, start=True, stop=True).then_inc(count_ready, 1)
            nb = BLOCK_COLUMNS
            for c in range(2 * NT):
                pe.wait_ge(hot_ready, c + 1)
                pe.matmul(bank[2][:, 0:2 * nb], hot[:, c % 2, :], hotb[:, c % 2, :, :].rearrange("p j b -> p (j b)"),
                          start=(c == 0), stop=(c == 2 * NT - 1)).then_inc(hot_used, 1)

            pe.wait_ge(routed, 1)
            used = pe.value_load(blocks_over[0:1, 0:1], min_val=0, max_val=MAX_BLOCKS - MIN_BLOCKS) + MIN_BLOCKS

            def transpose_rows(b, s):
                pe.wait_ge(xg_loaded[s], b * 8 + (16 - 8 * s))
                for half in range(2):
                    ge(pe, xgT_copied, 2 * b + (half - 1))
                    for k in range(KT // 2):
                        c0 = (half * KT // 2 + k) * P
                        last = pe.transpose(bank[half][:, k * P:(k + 1) * P], xg[:, s, c0:c0 + P], ident[:, :])
                    last.then_inc(xgT_ready, 1)

            def up(b, s, weights, loaded, out_bank, free, done):
                pe.wait_ge(loaded[s], b * 8 + (16 - 8 * s))
                ge(pe, free, b)
                for k in range(KT):
                    last = pe.matmul(bank[out_bank][:, :], xgT[:, k, :], weights[:, s, k, :],
                                     start=(k == 0), stop=(k == KT - 1))
                last.then_inc(done, 1)

            def first_up(b, s):
                pe.wait_ge(xgT_copied, 2 * b + 2)
                up(b, s, w1t, w1_loaded, 2, sil_ready, h1_ready)

            def second_up(b, s):
                up(b, s, w3t, w3_loaded, 3, hid_ready, h3_ready)

            def transpose_hidden(b):
                pe.wait_ge(hid_ready, b + 1)
                ge(pe, hidT_copied, b)
                for k in range(FT):
                    last = pe.transpose(bank[4][:, k * P:(k + 1) * P], hid[:, k * P:(k + 1) * P], ident[:, :])
                last.then_inc(hidT_ready, 1)

            def down(b, s):
                pe.wait_ge(w2_loaded[s], b * 8 + (16 - 8 * s))
                pe.wait_ge(hidT_copied, b + 1)
                for half in range(2):
                    ge(pe, y_copied, 2 * b + (half - 1))
                    for k in range(FT):
                        last = pe.matmul(bank[5 + half][:, :], hidT[:, k, :], w2t[:, s, k, half * 512:(half + 1) * 512],
                                         start=(k == 0), stop=(k == FT - 1))
                    last.then_inc(y_ready, 1)

            transpose_rows(0, 0)
            first_up(0, 0)
            second_up(0, 0)
            transpose_rows(1, 1)

            def expert_step(b, s):
                first_up(b, s)
                transpose_hidden(b - 1)
                second_up(b, s)
                transpose_rows(b + 1, 1 - s)
                down(b - 1, 1 - s)

            expert_step(1, 1)
            expert_step(2, 0)
            with pe.Fori(1, (MAX_BLOCKS - 1) // 2) as i:
                for s in (1, 0):
                    b = 2 * i + (2 - s)
                    with pe.If(b < used):
                        expert_step(b, s)
            transpose_hidden(used - 1)
            for s in range(2):
                with pe.If(((used + (1 - s)) & 1) < 1):
                    down(used - 1, s)


def kernel(**inputs):
    import numpy as np
    import concourse.bacc as bacc
    from concourse.bass_utils import run_bass_kernel_spmd as run

    nc = bacc.Bacc("TRN2", target_bir_lowering=False, num_devices=1)
    f32 = mybir.dt.float32
    a = {k: np.ascontiguousarray(v) for k, v in inputs.items()}
    cols = np.concatenate([a["norm_mix"].reshape(KT, P).T, a["pool_scale"].reshape(POOLS, P).T,
                           a["hg_norm_gain"].reshape(1, P).T,
                           a["hg_lb_fwd"].reshape(2 * HEADS, P).T, a["hg_lb_bwd"].reshape(2 * HEADS, P).T], axis=1)
    rows = np.concatenate([a["norm_ffn"].reshape(-1), a["norm_final"].reshape(-1),
                           a["router_group_b"].reshape(-1), a["router_expert_b"].reshape(-1)])
    inv = np.ones((POOLS, POOL_W), np.float32)
    for c, w in enumerate(WINDOWS):
        for start, length in ((0, T_PROMPT), (T_PROMPT, T_SAMPLE)):
            t = np.arange(length)
            count = np.clip(t + w // 2, 0, length) - np.clip(t - w // 2, 0, length)
            inv[c, pool_column(start):pool_column(start) + length] = 1.0 / count
    arrays = {
        "x_all": np.concatenate([a["x_prompt"].reshape(-1, D), a["x_sample"].reshape(-1, D)]),
        "w_in": a["w_in"][0], "w_out": a["w_out"][0], "pool_w": a["pool_w"][0],
        "cols": np.ascontiguousarray(cols), "rows": np.broadcast_to(rows, (P, R_N)).copy(), "inv_count": inv,
        "router_w": np.concatenate([a["router_group_w"][0], a["router_expert_w"][0]], axis=1),
        "w1": a["expert_w1"].reshape(NE * D, FE), "w3": a["expert_w3"].reshape(NE * D, FE),
        "w2": a["expert_w2"].reshape(NE * FE, D),
    }
    args = [nc.dram_tensor(k, v.shape, f32, kind="ExternalInput").ap() for k, v in arrays.items()]
    out = nc.dram_tensor("y", (T, D), f32, kind="ExternalOutput").ap()
    trunk_program(nc, *args, out)
    y = run(nc, [arrays], core_ids=[0]).results[0]["y"]
    return y[:T_PROMPT].reshape(1, T_PROMPT, D), y[T_PROMPT:].reshape(1, T_SAMPLE, D)
```

```python
import concourse.bass as bass
from concourse import mybir
from contextlib import ExitStack

P = 128
D = 1024
KT = D // P
T_PROMPT, T_SAMPLE = 1024, 512
T = T_PROMPT + T_SAMPLE
NT = T // P
GT = 512
NG = T // GT
BG = GT // P
HEADS = 4
SUB = 32
NSUB = P // SUB
WIDTH = 512
Q, FF, FB, OG, VAL = range(5)
SECTION_COLUMN = [1 * WIDTH, 2 * WIDTH, 3 * WIDTH, 5 * WIDTH, 4 * WIDTH]
SECTIONS = len(SECTION_COLUMN)
UNITS = SECTIONS * NG
POOLS = 4
POOL_UNITS = POOLS * NG
WINDOWS = (2, 4, 8, 16)
PAD = 8
POOL_W = T + 4 * PAD
XIN = 4
EPS = 1e-6
FWD, BWD = 0, 1
STEPS = [(BWD, 2), (BWD, 1), (BWD, 0), (FWD, 0), (FWD, 1), (FWD, 2)]
NEW_SEQUENCE = {(BWD, 2), (BWD, 1), (FWD, 0), (FWD, 2)}
NS = len(STEPS)
BEFORE, PER_STEP = 3, 2
assert BEFORE + NS * PER_STEP == UNITS

W_LOADS = [(), (0,), (), (1,), (2,), (3, 4)]

PK = POOLS + HEADS - 2
HALF = 512
PARTS = 2 * NT
PARTS_PER_STEP = PARTS // NS

N_GROUPS, PER_GROUP = 4, 8
NE = N_GROUPS * PER_GROUP
NLOG = N_GROUPS + NE
FE = 512
FT = FE // P
MAX_BLOCKS = (2 * T + NE * (P - 1)) // P
MIN_BLOCKS = 2 * T // P
EIGHT = 8
BLOCK_COLUMNS = MAX_BLOCKS + 2
C_MIX, C_SCALE, C_GAIN, C_LB = 0, KT, KT + POOLS, KT + POOLS + 1
C_N = C_LB + 4 * HEADS
R_FFN, R_FINAL, R_BIAS = 0, D, 2 * D
R_N = 2 * D + NLOG


def pool_column(t):
    return PAD + t + (2 * PAD if t >= T_PROMPT else 0)


def static(i, value):
    return isinstance(i, int) and i == value


def trunk_program(nc, x_all, w_in, w_out, pool_w, cols, rows, inv_count, router_w,
                  w1, w3, w2, out):
    f32, i32, u32 = mybir.dt.float32, mybir.dt.int32, mybir.dt.uint32
    ALU, ACT, AX = mybir.AluOpType, mybir.ActivationFunctionType, mybir.AxisListType
    ds = bass.ds

    def scratch(name, shape, dt=f32):
        return nc.dram_tensor(name, shape, dt, kind="Internal").ap()

    u_dram = scratch("u_dram", (HEADS * SECTIONS * P, T))
    mix_dram = scratch("mix_dram", (KT * P, T))
    part_dram = scratch("part_dram", (T, D))
    x1_dram = scratch("x1_dram", (T + P, D))
    xn_dram = scratch("xn_dram", (T + P, D))

    always, mixing = ExitStack(), ExitStack()

    def sb(stack, name, shape, dt=f32):
        return stack.enter_context(nc.sbuf_tensor(name, shape, dt))

    with always:
        def sem(name):
            return always.enter_context(nc.semaphore(name))

        bank = [always.enter_context(nc.psum_tensor(f"bank{i}", [P, 512], f32)) for i in range(8)]
        ident = sb(always, "ident", [P, P])
        ones = sb(always, "ones", [P, P])
        colc = sb(always, "colc", [P, C_N])
        eps_col = sb(always, "eps_col", [P, 1])
        ss = sb(always, "ss", [P, 2])
        rstd = sb(always, "rstd", [P, 2])

        wide = sb(always, "wide", [P, KT * T])
        mid = sb(always, "mid", [P, SECTIONS * KT * P])
        early = sb(always, "early", [P, 4 * POOL_W])

        class Region:

            def __init__(self, tensor):
                self.tensor, self.at = tensor, 0

            def take(self, *dims):
                n = 1
                for d in dims:
                    n *= d
                names = "abcd"[:len(dims)]
                flat = self.tensor[:, self.at:self.at + n]
                self.at += n
                if len(dims) == 1:
                    return flat
                return flat.rearrange(f"p ({' '.join(names)}) -> p {' '.join(names)}",
                                      **{c: d for c, d in zip(names[1:], dims[1:])})

        nT = Region(wide).take(KT, T)
        wsec = Region(mid).take(SECTIONS, KT, P)
        region = Region(early)
        xin = region.take(XIN, D)
        xs = region.take(2, D)
        in_early = Region(early).take(4, POOL_W)
        ptok, pwin, pinv = in_early[:, 0, :], [in_early[:, 1, :], in_early[:, 2, :]], in_early[:, 3, :]
        wfirst = Region(early).take(PK, D)
        region = Region(mid)
        mixp = region.take(2, PK, P)
        xp = region.take(2, D)
        mixt = region.take(2, KT - PK, P)
        region = Region(wide)
        wrest = region.take(KT - PK, D)
        x1t = region.take(2, D)
        xnt = region.take(2, D)
        xres = region.take(2, D)
        assert region.at >= 2 * FT * D
        rowc = region.take(R_N)
        rw = region.take(KT, NLOG)
        xnT = region.take(KT, P)
        logits = region.take(NT, NLOG)
        w2t = Region(wide).take(2, FT, D)
        region = Region(mid)
        xg = region.take(2, D)
        yst = region.take(2, D)

        region = Region(early)
        hot = region.take(2 * NT, P)
        hotb = region.take(2 * NT, BLOCK_COLUMNS)
        hotg = region.take(2 * NT, BLOCK_COLUMNS)

        ustage = sb(mixing, "ustage", [P, 3, GT])
        usig = sb(mixing, "usig", [P, GT])
        rin = sb(mixing, "rin", [P, 2, 3, GT])
        ogate = sb(mixing, "ogate", [P, NG, GT])
        keep = sb(mixing, "keep", [P, GT])
        logf = sb(mixing, "logf", [P, GT])
        cum = sb(mixing, "cum", [P, GT])
        dist = sb(mixing, "dist", [P, GT])
        exq = sb(mixing, "exq", [P, GT])
        exk = sb(mixing, "exk", [P, GT])
        LW = NSUB * (P + SUB)
        lev = [sb(mixing, f"lev{d}", [P, BG, LW]) for d in (FWD, BWD)]
        edges = sb(mixing, "edges", [P, BG, 9])
        edges_exp = sb(mixing, "edges_exp", [P, 2, BG, 9])
        qs = sb(mixing, "qs", [P, GT])
        qint = sb(mixing, "qint", [P, GT])
        kst = sb(mixing, "kst", [P, GT])
        ktok = sb(mixing, "ktok", [P, BG, P])
        vtok = sb(mixing, "vtok", [P, NT, P])
        scT = [sb(mixing, f"scT{d}", [P, BG, P]) for d in (FWD, BWD)]
        state = sb(mixing, "state", [P, BG + 1, P])
        obwd = sb(mixing, "obwd", [P, T])
        osum = sb(mixing, "osum", [P, GT])
        osq = sb(mixing, "osq", [P, GT])
        rms = sb(mixing, "rms", [P, GT])
        mixst = sb(mixing, "mixst", [P, NG, GT])
        scan_mask = sb(mixing, "scan_mask", [P, GT])
        tri = [sb(mixing, f"tri{d}", [P, P]) for d in (FWD, BWD)]
        lbs = sb(mixing, "lbs", [P, HEADS, 6])
        lbcur = sb(mixing, "lbcur", [P, 6])
        lbw = sb(mixing, "lbw", [P, 2, 2, HEADS])
        lbx = sb(mixing, "lbx", [P, 2, HEADS])
        wpool = sb(mixing, "wpool", [P, POOLS, P])
        zeros = sb(mixing, "zeros", [P, D])
        pooled = rin[:, :, :, :].rearrange("p a b c -> p (a b c)")[:, 0:POOL_W]
        mixing.pop_all().close()

        experts, blockwise = ExitStack(), ExitStack()
        wup = sb(experts, "wup", [P, 2, 2, KT, FE])
        w1t, w3t = wup[:, :, 0, :, :], wup[:, :, 1, :, :]
        final = wup[:, :, :, :, :].rearrange("p s w k n -> p (s w k n)")[:, 0:NT * D].rearrange(
            "p (t d) -> p t d", d=D)
        gate = sb(experts, "gate", [P, NT, 2])
        token_of = sb(experts, "token_of", [P, BLOCK_COLUMNS], i32)
        gate_of = sb(experts, "gate_of", [P, BLOCK_COLUMNS])
        expert_of = sb(experts, "expert_of", [P, BLOCK_COLUMNS], i32)
        blocks_over = sb(experts, "blocks_over", [P, 1], i32)
        group_rank = sb(blockwise, "group_rank", [P, N_GROUPS])
        expert_rank = sb(blockwise, "expert_rank", [P, NE])
        token_id = sb(blockwise, "token_id", [P, NT])
        row_id = sb(blockwise, "row_id", [P, 1])
        lane = sb(blockwise, "lane", [P, P])
        before = sb(blockwise, "before", [P, P])
        masked = sb(blockwise, "masked", [P, NT, NE])
        pick = [sb(blockwise, f"pick{j}", [P, NT, NE]) for j in range(2)]
        work = sb(blockwise, "work", [P, NT, NE])
        slots = sb(blockwise, "slots", [P, NT, NE])
        grp = sb(blockwise, "grp", [P, NT, N_GROUPS])
        top = sb(blockwise, "top", [P, 4, NT])
        offset = sb(blockwise, "offset", [P, NT + 1, NE])
        tokens_up = sb(blockwise, "tokens_up", [P, NE], i32)
        bcount = sb(blockwise, "bcount", [P, NE])
        bend = sb(blockwise, "bend", [P, NE])
        bcmp = sb(blockwise, "bcmp", [P, NE])
        bsum = sb(blockwise, "bsum", [P, 1])
        where = sb(blockwise, "where", [P, 2, NT])
        whole = sb(blockwise, "whole", [P, 3, 2 * NT], i32)
        parts = sb(blockwise, "parts", [P, 2, 2 * NT])
        slot_free = sb(blockwise, "slot_free", [P, BLOCK_COLUMNS])
        gidx = sb(blockwise, "gidx", [P, 2], i32)
        sidx = sb(blockwise, "sidx", [P, 2], i32)
        xgT = sb(blockwise, "xgT", [P, KT, P])
        sil = sb(blockwise, "sil", [P, FE])
        hid = sb(blockwise, "hid", [P, FE])
        hidT = sb(blockwise, "hidT", [P, FT, P])
        junk = sb(blockwise, "junk", [P, D])
        fss = sb(blockwise, "fss", [P, 3, NT])
        blockwise.pop_all().close()
        experts.pop_all().close()

        consts_ready = sem("consts_ready")
        cols_loaded = sem("cols_loaded")
        x_loaded = [sem(f"x_loaded{s}") for s in range(XIN)]
        tails_zeroed = sem("tails_zeroed")
        rms_ready = sem("rms_ready")
        rstd_ready = sem("rstd_ready")
        xs_ready = sem("xs_ready")
        xs2_ready = sem("xs2_ready")
        xT_ready = sem("xT_ready")
        nT_ready = sem("nT_ready")
        w_loaded = [sem(f"w_loaded{s}") for s in range(SECTIONS)]
        gemm_done = sem("gemm_done")
        usig_ready = sem("usig_ready")
        act_units = sem("act_units")
        dve_units = sem("dve_units")
        u_stored = [sem(f"u_stored{s}") for s in range(3)]
        wpool_loaded = sem("wpool_loaded")
        inv_loaded = sem("inv_loaded")
        pooled_ready = sem("pooled_ready")
        py_ready = sem("py_ready")
        pmix_ready = sem("pmix_ready")
        rin_loaded = [sem(f"rin_loaded{s}") for s in range(2)]
        ogate_loaded = [sem(f"ogate_loaded{s}") for s in range(NG)]
        lbw_ready = sem("lbw_ready")
        lbexp_ready = sem("lbexp_ready")
        lb_ready = sem("lb_ready")
        logf_ready = sem("logf_ready")
        dist_ready = sem("dist_ready")
        exps_ready = sem("exps_ready")
        keys_ready = sem("keys_ready")
        qint_ready = sem("qint_ready")
        kT_ready = sem("kT_ready")
        ktok_ready = sem("ktok_ready")
        kv_ready = sem("kv_ready")
        sc_ready = sem("sc_ready")
        st_ready = sem("st_ready")
        o_ready = sem("o_ready")
        ob_ready = sem("ob_ready")
        osum_ready = sem("osum_ready")
        osq_ready = sem("osq_ready")
        ms_ready = sem("ms_ready")
        rr_ready = sem("rr_ready")
        mix_ready = sem("mix_ready")
        mix_stored = [sem(f"mix_stored{s}") for s in range(NG)]
        wout_loaded = sem("wout_loaded")
        wrest_loaded = sem("wrest_loaded")
        mixp_loaded = [sem(f"mixp_loaded{s}") for s in range(2)]
        xp_loaded = [sem(f"xp_loaded{s}") for s in range(2)]
        part_done = sem("part_done")
        part_ready = sem("part_ready")
        part_stored = [sem(f"part_stored{s}") for s in range(3)]
        mixt_loaded = [sem(f"mixt_loaded{s}") for s in range(2)]
        xres_loaded = [sem(f"xres_loaded{s}") for s in range(2)]
        wo_ready = sem("wo_ready")
        x1_ready = sem("x1_ready")
        rms2_ready = sem("rms2_ready")
        xn_ready = sem("xn_ready")
        x1_stored = [sem(f"x1_stored{s}") for s in range(2)]
        xn_stored = [sem(f"xn_stored{s}") for s in range(2)]
        xnT_ready = sem("xnT_ready")
        xnT_copied = sem("xnT_copied")
        router_ready = sem("router_ready")
        logits_ready = sem("logits_ready")
        ranks_ready = sem("ranks_ready")
        gexp_ready = sem("gexp_ready")
        gexp_done = sem("gexp_done")
        picks_ready = sem("picks_ready")
        count_ready = sem("count_ready")
        parts_ready = sem("parts_ready")
        hot_ready = sem("hot_ready")
        hotrow_ready = sem("hotrow_ready")
        tokens_summed = sem("tokens_summed")
        hotg_ready = sem("hotg_ready")
        gates_summed = sem("gates_summed")
        gates_known = sem("gates_known")
        bexp_ready = sem("bexp_ready")
        bexp_turned = sem("bexp_turned")
        blocks_known = sem("blocks_known")
        routed = sem("routed")
        gidx_ready = sem("gidx_ready")
        pool_turn = sem("pool_turn")
        xg_loaded = [sem(f"xg_loaded{s}") for s in range(2)]
        w1_loaded = [sem(f"w1_loaded{s}") for s in range(2)]
        w3_loaded = [sem(f"w3_loaded{s}") for s in range(2)]
        w2_loaded = [sem(f"w2_loaded{s}") for s in range(2)]
        xgT_ready = sem("xgT_ready")
        xgT_copied = sem("xgT_copied")
        h1_ready = sem("h1_ready")
        h3_ready = sem("h3_ready")
        sil_ready = sem("sil_ready")
        hid_ready = sem("hid_ready")
        hidT_ready = sem("hidT_ready")
        hidT_copied = sem("hidT_copied")
        y_ready = sem("y_ready")
        y_copied = sem("y_copied")
        y_added = [sem(f"y_added{s}") for s in range(2)]
        final_loaded = [sem(f"final_loaded{i}") for i in range(NT // 2)]
        rms3_ready = sem("rms3_ready")
        gain_ready = sem("gain_ready")
        out_ready = sem("out_ready")
        out_stored = sem("out_stored")
        dve_step = sem("dve_step")
        act_step = sem("act_step")

        PROJ = bank[0:3]
        TK, TV, KV, SC, OUT = bank[3:8]
        XT = bank[3:5]
        MS = TV
        FIRST_CONSTS, CONSTS = 4, 10

        def ge(eng, s, value):
            if not isinstance(value, int) or value > 0:
                eng.wait_ge(s, value)

        class Chain:

            def __init__(self, eng, s):
                self.eng, self.sem, self.base, self.n, self.off, self.per = eng, s, 0, 0, None, 0

            def value(self):
                return self.base + self.n if self.off is None else self.off * self.per + (self.base + self.n)

            def link(self, ins):
                ins.then_inc(self.sem, 1)
                self.n += 1
                self.eng.wait_ge(self.sem, self.value())

            def start(self):
                self.base, self.n = self.base + self.n, 0

            def enter(self, off, per):
                self.start()
                self.off, self.per = off, per

            def leave(self, iterations):
                assert self.n == self.per, (self.n, self.per)
                self.base, self.n, self.off = self.base + self.per * iterations, 0, None

        def heads_loop(eng, chain, body):
            chain.start()
            body(0)
            per = chain.n
            with eng.Fori(1, HEADS - 1) as h:
                chain.enter(h - 1, per)
                body(h)
            chain.leave(HEADS - 2)
            body(HEADS - 1)

        def in_slot(h, n):
            per_head = 16 * sum(3 if STEPS[m][0] == BWD else 2 for m in range(n % 2, NS, 2))
            return h * per_head + 16 * sum(3 if STEPS[m][0] == BWD else 2 for m in range(n % 2, n + 1, 2))

        def unit_number(h, u):
            return h * UNITS + (POOL_UNITS + u)

        def by_dve(u):
            return u // NG in (Q, OG)

        def wait_left_bank(eng, h, u):
            count = sum(by_dve(v) == by_dve(u) for v in range(u + 1))
            per_head = sum(by_dve(v) == by_dve(u) for v in range(UNITS))
            eng.wait_ge(dve_units if by_dve(u) else act_units, h * per_head + (count + (POOL_UNITS if by_dve(u) else 0)))

        def blocks_loop(eng, first, used, body):
            pairs = (MIN_BLOCKS - first) // 2
            with eng.Fori(0, pairs) as i:
                for j in range(2):
                    body(2 * i + (first + j), (first + j) % 2)
            rest = first + 2 * pairs
            with eng.Fori(0, -(-(MAX_BLOCKS - rest) // EIGHT)) as k:
                with eng.If(k * EIGHT + rest < used):
                    with eng.Fori(0, EIGHT // 2) as i:
                        for j in range(2):
                            with eng.If(k * EIGHT + 2 * i + (rest + j) < used):
                                body(k * EIGHT + 2 * i + (rest + j), (first + j) % 2)

        block = always.enter_context(nc.Block())

        @block.sync
        def _(sp):
            def load_x(t, s):
                sp.dma_start(xin[:, s, :], x_all[ds(t * P, P), :]).then_inc(x_loaded[s], 16)

            def load_w(column, s):
                sp.dma_start(wsec[:, s, :, :],
                             w_in[:, ds(column, P)].rearrange("(k p) n -> p k n", p=P)).then_inc(w_loaded[s], 16)

            load_x(0, 0)
            sp.dma_start(colc[:, :], cols).then_inc(cols_loaded, 16)
            for s in range(1, XIN):
                load_x(s, s)
            load_w(0, 0)
            with sp.Fori(1, NT // XIN) as i:
                for s in range(XIN):
                    sp.wait_ge(xs_ready, XIN * i + (s + 1 - XIN))
                    sp.wait_ge(xs2_ready, XIN * i + (s + 1 - XIN))
                    load_x(XIN * i + s, s)
            for c in range(1, POOLS):
                load_w(c * P, c)
            load_w(SECTION_COLUMN[4], 4)
            sp.dma_start(wpool[:, :, :], pool_w.rearrange("g c d -> c g d")).then_inc(wpool_loaded, 16)
            sp.wait_ge(nT_ready, 2 * NT)
            for c in range(POOLS):
                ge(sp, pooled_ready, c)
                sp.dma_start(pinv, inv_count[c:c + 1, :].to_broadcast([P, POOL_W])).then_inc(inv_loaded, 16)
                sp.wait_ge(gemm_done, (c + 1) * NG)
                load_w(SECTION_COLUMN[c], c)
            for s in range(SECTIONS):
                sp.wait_ge(gemm_done, unit_number(0, (s + 1) * NG))
                load_w(SECTION_COLUMN[s] + P, s)

            def load_part(t):
                ge(sp, part_ready, 2 * t - 2)
                sp.dma_start(mixp[:, t % 2, :, :],
                             mix_dram[0:PK * P, t * P:(t + 1) * P].rearrange("(k p) n -> p k n", p=P)
                             ).then_inc(mixp_loaded[t % 2], 16)
                sp.dma_start(xp[:, t % 2, :], x_all[t * P:(t + 1) * P, :]).then_inc(xp_loaded[t % 2], 16)

            def load_wout(target, k0, k1, signal):
                sp.dma_start(target[:, :, :],
                             w_out[k0 * P:k1 * P, :].rearrange("(k p) n -> p k n", p=P)).then_inc(signal, 16)

            def recurrence_loads(h):
                if static(h, HEADS - 1):
                    sp.wait_ge(gemm_done, unit_number(HEADS - 1, UNITS))
                    for j in range(NG):
                        sp.wait_ge(mix_stored[j], 16 * PK)
                    load_part(0)
                    load_part(1)
                for s in range(3):
                    sp.wait_ge(u_stored[s], h * (16 * SECTIONS) + 16 * SECTIONS)
                for n, (d, g) in enumerate(STEPS):
                    if static(h, HEADS - 1) and n >= 2:
                        load_part(2 * n - 2)
                        load_part(2 * n - 1)
                    ge(sp, kT_ready, h * NS + (n - 1))
                    for j, sec in enumerate((Q, FF + d, VAL)[:3 if d == BWD else 2]):
                        sp.dma_start(rin[:, n % 2, j, :],
                                     u_dram[ds((h * SECTIONS + sec) * P, P), g * GT:(g + 1) * GT]
                                     ).then_inc(rin_loaded[n % 2], 16)
                    if d == BWD:
                        gg = NG - 1 - g
                        ge(sp, mix_ready, h * NG + (gg + 1 - NG))
                        sp.dma_start(ogate[:, gg, :],
                                     u_dram[ds((h * SECTIONS + OG) * P, P), gg * GT:(gg + 1) * GT]
                                     ).then_inc(ogate_loaded[gg], 16)
                    for sec in (() if isinstance(h, int) and h >= HEADS - 2 else W_LOADS[n]):
                        sp.wait_ge(gemm_done, unit_number(h + 1, (sec + 1) * NG))
                        load_w(h * P + (SECTION_COLUMN[sec] + 2 * P), sec)

            recurrence_loads(0)
            with sp.Fori(1, HEADS - 2) as h:
                recurrence_loads(h)
            recurrence_loads(HEADS - 2)
            load_wout(wfirst, 0, PK, wout_loaded)
            recurrence_loads(HEADS - 1)

            load_part(NT - 2)
            load_part(NT - 1)
            load_wout(wrest, PK, KT, wrest_loaded)
            sp.dma_start(rw[:, :, :], router_w.rearrange("(k p) n -> p k n", p=P)).then_inc(wrest_loaded, 16)
            sp.dma_start(rowc, rows).then_inc(wrest_loaded, 16)

            def load_tile(t, s):
                sp.dma_start(mixt[:, s, :, :],
                             mix_dram[PK * P:KT * P, ds(t * P, P)].rearrange("(k p) n -> p k n", p=P)).then_inc(mixt_loaded[s], 16)
                sp.dma_start(xres[:, s, :], part_dram[ds(t * P, P), :]).then_inc(xres_loaded[s], 16)

            def store_tile(t, s):
                sp.wait_ge(xn_ready, t + 1)
                sp.dma_start(x1_dram[ds(t * P, P), :], x1t[:, s, :]).then_inc(x1_stored[s], 16)
                sp.dma_start(xn_dram[ds(t * P, P), :], xnt[:, s, :]).then_inc(xn_stored[s], 16)

            sp.wait_ge(mix_stored[0], 16 * (POOLS + HEADS))
            for s in range(3):
                sp.wait_ge(part_stored[s], 16 * (2 * BG // 3 + 1))
            load_tile(0, 0)
            load_tile(1, 1)
            for t in range(2):
                sp.wait_ge(x1_ready, 2 * t + 2)
                load_tile(t + 2, t)
                store_tile(t, t)
            for s in range(3):
                sp.wait_ge(part_stored[s], 16 * PARTS // 3)
            for g in range(1, NG):
                sp.wait_ge(mix_stored[g], 16 * (POOLS + HEADS))
            with sp.Fori(1, NT // 2 - 1) as i:
                for s in range(2):
                    sp.wait_ge(x1_ready, 4 * i + (2 * s + 2))
                    load_tile(2 * i + (s + 2), s)
                    store_tile(2 * i + s, s)
            for s in range(2):
                store_tile(NT - 2 + s, s)

            sp.wait_ge(tails_zeroed, 32)
            for s in range(2):
                sp.wait_ge(x1_stored[s], 8 * NT)
                sp.wait_ge(xn_stored[s], 8 * NT)
            sp.wait_ge(blocks_known, 1)
            used = sp.value_load(blocks_over[0:1, 0:1], min_val=0, max_val=MAX_BLOCKS - MIN_BLOCKS) + MIN_BLOCKS

            def load_expert(b, s):
                e = sp.value_load(expert_of[0:1, ds(b, 1)], min_val=0, max_val=NE - 1)
                if not isinstance(b, int):
                    sp.wait_ge(h1_ready, b - 1)
                sp.dma_start(w1t[:, s, :, :], w1[ds(e * D, D), :].rearrange("(k p) n -> p k n", p=P)
                             ).then_inc(w1_loaded[s], 16)
                if not isinstance(b, int):
                    sp.wait_ge(h3_ready, b - 1)
                sp.dma_start(w3t[:, s, :, :], w3[ds(e * D, D), :].rearrange("(k p) n -> p k n", p=P)
                             ).then_inc(w3_loaded[s], 16)
                if not isinstance(b, int):
                    sp.wait_ge(y_ready, 2 * b - 2)
                elif b == 0:
                    sp.wait_ge(xg_loaded[0], 16)
                sp.dma_start(w2t[:, s, :, :], w2[ds(e * FE, FE), :].rearrange("(k p) n -> p k n", p=P)
                             ).then_inc(w2_loaded[s], 16)

            load_expert(0, 0)
            load_expert(1, 1)
            blocks_loop(sp, 2, used, load_expert)

            for s in range(2):
                sp.wait_ge(y_added[s], 16 * ((used + (1 - s)) >> 1))
            for i in range(NT // 2):
                sp.dma_start(final[:, 2 * i:2 * i + 2, :], x1_dram[2 * i * P:(2 * i + 2) * P, :].rearrange(
                    "(t p) d -> p t d", p=P)).then_inc(final_loaded[i], 16)
            with sp.Fori(0, NT) as t:
                sp.wait_ge(out_ready, 2 * t + 2)
                sp.dma_start(out[ds(t * P, P), :], final[:, ds(t, 1), :].rearrange("p o d -> p (o d)")
                             ).then_inc(out_stored, 16)
            sp.wait_ge(out_stored, 16 * NT)

        @block.gpsimd
        def _(pool):
            n = [0]

            def made(ins):
                ins.then_inc(consts_ready, 1)
                n[0] += 1
                pool.wait_ge(consts_ready, n[0])

            made(pool.memset(ident[:, :], 0.0))
            made(pool.affine_select(out=ident[:, :], in_=ident[:, :], compare_op=ALU.not_equal, fill=1.0,
                                    base=0, pattern=[[-1, P]], channel_multiplier=1))
            made(pool.memset(ones[:, :], 1.0))
            made(pool.memset(eps_col[:, :], EPS))
            made(pool.memset(scan_mask[:, :], 1.0))
            made(pool.memset(scan_mask[:, :].rearrange("p (b c) -> p b c", c=P)[:, :, 0:1], 0.0))
            for d in (FWD, BWD):
                sign = 1 if d == FWD else -1
                made(pool.affine_select(out=tri[d][:, :], in_=ones[:, :], compare_op=ALU.is_ge, fill=0.0,
                                        base=0, pattern=[[sign, P]], channel_multiplier=-sign))
            assert n[0] == CONSTS - 2
            pool.memset(zeros[:, :], 0.0)
            for d in (FWD, BWD):
                pool.memset(scT[d][:, :, :], 0.0)
                made(pool.memset(lev[d][:, :, :], 0.0))

            def store_unit(h, u):
                s, (sec, g) = u % 3, divmod(u, NG)
                wait_left_bank(pool, h, u)
                pool.dma_start(u_dram[ds((h * SECTIONS + sec) * P, P), g * GT:(g + 1) * GT],
                               ustage[:, s, :]).then_inc(u_stored[s], 16)

            def store_mix(row, g):
                pool.dma_start(mix_dram[ds(row, P), g * GT:(g + 1) * GT],
                               mixst[:, g, :]).then_inc(mix_stored[g], 16)

            for c in range(POOLS):
                for g in range(NG):
                    pool.wait_ge(pmix_ready, c * NG + g + 1)
                    store_mix(c * P, g)
                if c == POOLS - 2:
                    for u in range(NG):
                        store_unit(0, u)
            for u in range(NG, UNITS):
                store_unit(0, u)

            def store_part(v):
                t, half = divmod(v, 2)
                pool.wait_ge(part_ready, v + 1)
                pool.dma_start(part_dram[t * P:(t + 1) * P, half * HALF:(half + 1) * HALF],
                               ustage[:, v % 3, :]).then_inc(part_stored[v % 3], 16)

            def recurrence_stores(h):
                more = not static(h, HEADS - 1)
                for u in range(BEFORE if more else 0):
                    store_unit(h + 1, u)
                if not more:
                    store_part(0)
                    store_part(1)
                for n, (d, g) in enumerate(STEPS):
                    if more:
                        store_unit(h + 1, BEFORE + PER_STEP * n)
                    else:
                        store_part(PARTS_PER_STEP * n + 2)
                        store_part(PARTS_PER_STEP * n + 3)
                    if n > 0 and STEPS[n - 1][0] == FWD:
                        g1 = STEPS[n - 1][1]
                        pool.wait_ge(mix_ready, h * NG + (g1 + 1))
                        store_mix(h * P + POOLS * P, g1)
                    if more:
                        store_unit(h + 1, BEFORE + PER_STEP * n + 1)
                    elif n + 1 < NS:
                        store_part(PARTS_PER_STEP * n + 4)
                        store_part(PARTS_PER_STEP * n + 5)
                pool.wait_ge(mix_ready, h * NG + NG)
                store_mix(h * P + POOLS * P, NG - 1)

            recurrence_stores(0)
            with pool.Fori(1, HEADS - 1) as h:
                recurrence_stores(h)
            recurrence_stores(HEADS - 1)
            for g in range(NG):
                pool.wait_ge(mix_stored[g], 16 * (POOLS + HEADS))

            pool.wait_ge(tails_zeroed, 32)
            pool.iota(group_rank[:, :], pattern=[[-1, N_GROUPS]], base=N_GROUPS, channel_multiplier=0,
                      allow_small_or_imprecise_dtypes=True)
            pool.iota(expert_rank[:, :], pattern=[[-1, NE]], base=NE, channel_multiplier=0,
                      allow_small_or_imprecise_dtypes=True)
            pool.iota(token_id[:, :], pattern=[[P, NT]], base=-T, channel_multiplier=1,
                      allow_small_or_imprecise_dtypes=True)
            pool.iota(lane[:, :], pattern=[[1, P]], base=0, channel_multiplier=0,
                      allow_small_or_imprecise_dtypes=True)
            pool.iota(row_id[:, :], pattern=[[0, 1]], base=0, channel_multiplier=1,
                      allow_small_or_imprecise_dtypes=True)
            pool.affine_select(out=before[:, :], in_=ones[:, :], compare_op=ALU.is_gt, fill=0.0,
                               base=0, pattern=[[1, P]], channel_multiplier=-1).then_inc(ranks_ready, 1)

            pool.wait_ge(parts_ready, 1)
            for c in range(0, 2 * NT, 2):
                pool.tensor_scalar(hot[:, c, :], lane[:, :], parts[:, 1, c:c + 1], None,
                                   ALU.is_equal).then_inc(hotrow_ready, 1)

            pool.wait_ge(routed, 1)
            for s in range(2):
                pool.wait_ge(xn_stored[s], 8 * NT)
                pool.wait_ge(x1_stored[s], 8 * NT)
            used = pool.value_load(blocks_over[0:1, 0:1], min_val=0, max_val=MAX_BLOCKS - MIN_BLOCKS) + MIN_BLOCKS

            def gather_rows(b, s):
                pool.wait_ge(gidx_ready, b + 1)
                pool.sem_inc(pool_turn, 1)
                pool.indirect_dma_start(out=xg[:, s, :], out_offset=None, in_=xn_dram[:, :],
                                        in_offset=bass.IndirectOffsetOnAxis(ap=gidx[:, s:s + 1], axis=0)
                                        ).then_inc(xg_loaded[s], 16)

            def add_outputs(b, s):
                pool.wait_ge(y_copied, 2 * b + 2)
                if not static(b, 0):
                    pool.wait_ge(y_added[1 - s], 8 * b + (8 * s))
                pool.sem_inc(pool_turn, 1)
                pool.indirect_dma_start(out=x1_dram[:, :],
                                        out_offset=bass.IndirectOffsetOnAxis(ap=sidx[:, s:s + 1], axis=0),
                                        in_=yst[:, s, :], in_offset=None, compute_op=ALU.add
                                        ).then_inc(y_added[s], 16)

            for b in range(3):
                gather_rows(b, b % 2)
            gather_rows(3, 1)
            add_outputs(0, 0)
            gather_rows(4, 0)
            add_outputs(1, 1)
            def rows_in_and_out(b, s):
                gather_rows(b + 2, s)
                add_outputs(b - 1, 1 - s)

            blocks_loop(pool, 3, used, rows_in_and_out)
            for s in range(2):
                with pool.If(((used + (1 - s)) & 1) < 1):
                    add_outputs(used - 1, s)
            for s in range(2):
                pool.wait_ge(xg_loaded[s], 16 * ((used + (3 - s)) >> 1))

        @block.scalar
        def _(act):
            chain = Chain(act, act_step)
            act.wait_ge(consts_ready, FIRST_CONSTS)
            act.activation(rstd[:, 0:1], eps_col[:, 0:1], ACT.Sqrt)

            def normalise(t, x, i):
                s = x % 2
                act.wait_ge(x_loaded[x], i * 16 + 16)
                ge(act, xT_ready, 2 * t - 2)
                chain.link(act.activation(xs[:, s, :], xin[:, x, :], ACT.Square, accum_out=ss[:, s:s + 1]))
                act.activation(ss[:, s:s + 1], ss[:, s:s + 1], ACT.Sqrt, bias=eps_col[:, 0:1],
                               scale=1.0 / D).then_inc(rms_ready, 1)
                act.wait_ge(rstd_ready, t + 1)
                act.activation(xs[:, s, 0:D // 2], xin[:, x, 0:D // 2], ACT.Copy,
                               scale=rstd[:, s:s + 1]).then_inc(xs_ready, 1)

            for x in range(XIN):
                normalise(x, x, 0)
            chain.start()
            with act.Fori(1, NT // XIN) as i:
                chain.enter(i - 1, XIN)
                for x in range(XIN):
                    normalise(XIN * i + x, x, i)
            chain.leave(NT // XIN - 1)
            act.wait_ge(cols_loaded, 16)
            act.wait_ge(consts_ready, CONSTS)

            for x in (x1_dram, xn_dram):
                act.dma_start(x[T:T + P, :], zeros[:, :]).then_inc(tails_zeroed, 16)
            act.wait_ge(lbw_ready, 1)
            act.activation(lbw[:, :, :, :], lbw[:, :, :, :], ACT.Exp).then_inc(lbexp_ready, 1)

            def pool_outputs(c):
                for g in range(NG):
                    act.wait_ge(py_ready, c * NG + g + 1)
                    ge(act, mix_stored[g], 16 * c)
                    act.activation(mixst[:, g, :], bank[3 + g][:, :], ACT.Copy,
                                   scale=colc[:, C_SCALE + c:C_SCALE + c + 1]).then_inc(pmix_ready, 1)

            def gate_unit(h, u):
                act.wait_ge(gemm_done, unit_number(h, u + 1))
                if by_dve(u):
                    ge(act, dve_units, h * (2 * NG) + (sum(by_dve(v) for v in range(u)) + POOL_UNITS))
                    act.activation(usig[:, :], PROJ[u % 3][:, :], ACT.Sigmoid).then_inc(usig_ready, 1)
                else:
                    ge(act, u_stored[u % 3], h * (16 * SECTIONS) + 16 * (u // 3))
                    act.activation(ustage[:, u % 3, :], PROJ[u % 3][:, :],
                                   ACT.Copy if u // NG == VAL else ACT.Sigmoid).then_inc(act_units, 1)

            def log_forget(h, n):
                d = STEPS[n][0]
                act.wait_ge(rin_loaded[n % 2], in_slot(h, n))
                if n == 0:
                    act.wait_ge(lb_ready, h + 1)
                ge(act, dist_ready, h * NS + n)
                act.activation(logf[:, :], rin[:, n % 2, 1, :], ACT.Ln, scale=lbcur[:, 3 * d + 1:3 * d + 2],
                               bias=lbcur[:, 3 * d:3 * d + 1]).then_inc(logf_ready, 1)

            def exponentials(h, n):
                d = STEPS[n][0]
                sign = 1.0 if d == FWD else -1.0
                act.wait_ge(dist_ready, h * NS + (n + 1))
                act.activation(edges_exp[:, n % 2, :, :], edges[:, :, :], ACT.Exp)
                act.activation(exk[:, :], dist[:, :], ACT.Exp, scale=-sign)
                act.activation(exq[:, :], dist[:, :], ACT.Exp, scale=sign).then_inc(exps_ready, 1)

            def to_tokens(h, n):
                d, g = STEPS[n]
                act.wait_ge(kT_ready, h * NS + (n + 1))
                if d == BWD:
                    act.activation(vtok[:, g * BG:(g + 1) * BG, :],
                                   TV[:, :].rearrange("p (b c) -> p b c", c=P), ACT.Copy)
                act.activation(ktok[:, :, :], TK[:, :].rearrange("p (b c) -> p b c", c=P),
                               ACT.Copy).then_inc(ktok_ready, 1)

            def inverse_rms(h, k):
                act.wait_ge(ms_ready, h * NG + (k + 1))
                ge(act, mix_ready, h * NG + k)
                chain.link(act.activation(rms[:, :], MS[:, :], ACT.Ln, scale=1.0 / P, bias=eps_col[:, 0:1]))
                act.activation(rms[:, :], rms[:, :], ACT.Exp, scale=-0.5).then_inc(rr_ready, 1)

            def outputs(h, n):
                d, g = STEPS[n]
                if d == BWD:
                    act.wait_ge(o_ready, h * NS + (n + 1))
                    act.activation(obwd[:, g * GT:(g + 1) * GT], OUT[:, :], ACT.Copy).then_inc(ob_ready, 1)
                else:
                    act.wait_ge(osum_ready, h * NG + (g + 1))
                    act.activation(osq[:, :], osum[:, :], ACT.Square).then_inc(osq_ready, 1)

            def recurrence(h):
                more = not static(h, HEADS - 1)
                log_forget(h, 0)
                if more:
                    gate_unit(h + 1, 0)
                exponentials(h, 0)
                log_forget(h, 1)
                if more:
                    gate_unit(h + 1, 1)
                for n, (d, g) in enumerate(STEPS):
                    u = BEFORE + PER_STEP * n
                    to_tokens(h, n)
                    if more:
                        gate_unit(h + 1, u - 1)
                    if n + 1 < NS:
                        exponentials(h, n + 1)
                    if n + 2 < NS:
                        log_forget(h, n + 2)
                    if more:
                        gate_unit(h + 1, u)
                    if d == FWD and g > 0:
                        inverse_rms(h, g - 1)
                    outputs(h, n)
                if more:
                    gate_unit(h + 1, UNITS - 1)
                inverse_rms(h, NG - 1)

            for c in range(POOLS - 1):
                pool_outputs(c)
            for u in range(UNITS):
                gate_unit(0, u)
                if u == NG - 1:
                    pool_outputs(POOLS - 1)
            heads_loop(act, chain, recurrence)

            chain.start()

            def square_sum(done, count, x, junk, signal):
                act.wait_ge(done, count)
                chain.link(act.activation(junk, x, ACT.Square, accum_out=ss[:, 0:1]))
                act.activation(ss[:, 1:2], ss[:, 0:1], ACT.Sqrt, bias=eps_col[:, 0:1],
                               scale=1.0 / D).then_inc(signal, 1)

            def copy_xnT(t):
                for half in range(2):
                    act.wait_ge(xnT_ready, 2 * t + (half + 1))
                    act.activation(xnT[:, half * KT // 2:(half + 1) * KT // 2, :],
                                   bank[4 + half][:, :].rearrange("p (k c) -> p k c", c=P),
                                   ACT.Copy).then_inc(xnT_copied, 1)

            def project(t, s):
                if not isinstance(t, int):
                    act.wait_ge(xn_stored[s], 8 * t - 8 * s)
                    act.wait_ge(xnT_ready, 2 * t - 2)
                square_sum(x1_ready, 2 * t + 2, x1t[:, s, :], xnt[:, s, :], rms2_ready)

            project(0, 0)
            project(1, 1)
            chain.start()
            with act.Fori(1, NT // 2) as i:
                chain.enter(i - 1, 2)
                for s in range(2):
                    copy_xnT(2 * i + (s - 2))
                    project(2 * i + s, s)
            chain.leave(NT // 2 - 1)
            copy_xnT(NT - 2)
            copy_xnT(NT - 1)

            act.wait_ge(gexp_ready, 1)
            act.activation(grp[:, :, :], grp[:, :, :], ACT.Exp).then_inc(gexp_done, 1)
            act.wait_ge(gexp_ready, 2)
            act.activation(top[:, 1, :], top[:, 1, :], ACT.Exp).then_inc(gexp_done, 1)

            act.wait_ge(routed, 1)
            used = act.value_load(blocks_over[0:1, 0:1], min_val=0, max_val=MAX_BLOCKS - MIN_BLOCKS) + MIN_BLOCKS

            def copy_xgT(b):
                for half in range(2):
                    act.wait_ge(xgT_ready, 2 * b + (half + 1))
                    act.activation(xgT[:, half * KT // 2:(half + 1) * KT // 2, :],
                                   bank[half][:, :].rearrange("p (k c) -> p k c", c=P),
                                   ACT.Copy).then_inc(xgT_copied, 1)

            def expert_block(b, s):
                act.wait_ge(h1_ready, b + 1)
                ge(act, hid_ready, b)
                act.activation(sil[:, :], bank[2][:, :], ACT.Silu).then_inc(sil_ready, 1)
                copy_xgT(b + 1)

            copy_xgT(0)
            expert_block(0, 0)
            blocks_loop(act, 1, used, expert_block)

            chain.start()
            act.wait_ge(y_copied, 2 * used)
            for t in range(NT):
                if t % 2 == 0:
                    act.wait_ge(final_loaded[t // 2], 16)
                chain.link(act.activation(junk[:, :], final[:, t, :], ACT.Square, accum_out=fss[:, 0, t:t + 1]))
                act.activation(fss[:, 1, t:t + 1], fss[:, 0, t:t + 1], ACT.Sqrt, bias=eps_col[:, 0:1],
                               scale=1.0 / D).then_inc(rms3_ready, 1)

        @block.vector
        def _(dve):
            chain = Chain(dve, dve_step)
            link = chain.link
            dve.wait_ge(cols_loaded, 16)

            def scale_tile(t, x):
                s = x % 2
                dve.wait_ge(rms_ready, t + 1)
                dve.reciprocal(rstd[:, s:s + 1], ss[:, s:s + 1]).then_inc(rstd_ready, 1)
                dve.wait_ge(rstd_ready, t + 1)
                dve.tensor_scalar(xs[:, s, D // 2:D], xin[:, x, D // 2:D], rstd[:, s:s + 1], None,
                                  ALU.mult).then_inc(xs2_ready, 1)

            def into_nT(t):
                for half in range(2):
                    k0 = half * KT // 2
                    dve.wait_ge(xT_ready, 2 * t + half + 1)
                    dve.tensor_tensor(nT[:, k0:k0 + KT // 2, ds(t * P, P)],
                                      XT[half][:, :].rearrange("p (k c) -> p k c", c=P),
                                      colc[:, C_MIX + k0:C_MIX + k0 + KT // 2].unsqueeze(2)
                                      .to_broadcast([P, KT // 2, P]), ALU.mult).then_inc(nT_ready, 1)

            rows2 = colc[:, C_LB:C_N].rearrange("p (d r h) -> p d r h", d=2, r=2)
            link(dve.tensor_tensor(lbx[:, :, :], rows2[:, :, 0, :], rows2[:, :, 1, :], ALU.max))
            dve.tensor_tensor(lbw[:, :, :, :], rows2, lbx[:, :, :].unsqueeze(2).to_broadcast([P, 2, 2, HEADS]),
                              ALU.subtract).then_inc(lbw_ready, 1)
            scale_tile(0, 0)
            for x in range(1, XIN):
                scale_tile(x, x)
                into_nT(x - 1)
            with dve.Fori(1, NT // XIN) as i:
                for x in range(XIN):
                    scale_tile(XIN * i + x, x)
                    into_nT(XIN * i + (x - 1))
            into_nT(NT - 1)
            dve.wait_ge(consts_ready, CONSTS)
            dve.wait_ge(lbexp_ready, 1)
            link(dve.tensor_tensor(lbx[:, :, :], lbw[:, :, 0, :], lbw[:, :, 1, :], ALU.add))
            link(dve.reciprocal(lbx[:, :, :], lbx[:, :, :]))
            for d in (FWD, BWD):
                link(dve.tensor_tensor(lbs[:, :, 3 * d], lbw[:, d, 0, :], lbx[:, d, :], ALU.mult))
                link(dve.tensor_scalar(lbs[:, :, 3 * d + 1], lbs[:, :, 3 * d], -1.0, 1.0, ALU.mult, ALU.add))
                link(dve.tensor_scalar(lbs[:, :, 3 * d + 2], lbs[:, :, 3 * d], -1.0, None, ALU.add))
            dve.wait_ge(xT_ready, 2 * NT)
            for c0 in (0, PAD + T_PROMPT, POOL_W - PAD):
                link(dve.memset(ptok[:, c0:c0 + (2 * PAD if c0 == PAD + T_PROMPT else PAD)], 0.0))

            def pool_group(c):
                for g in range(NG):
                    dve.wait_ge(gemm_done, c * NG + g + 1)
                    c0 = pool_column(g * GT)
                    ins = dve.tensor_copy(ptok[:, c0:c0 + GT], PROJ[g][:, :])
                    ins.then_inc(dve_units, 1)
                dve.wait_ge(dve_units, (c + 1) * NG)
                ge(dve, py_ready, c * NG)
                a, b, lo, hi = ptok, pwin[0], 0, POOL_W
                for i in range(c + 1):
                    back, ahead = (1, 0) if i == 0 else (1 << (i - 1), 1 << (i - 1))
                    lo, hi = lo + back, hi - ahead
                    link(dve.tensor_tensor(b[:, lo:hi], a[:, lo - back:hi - back], a[:, lo + ahead:hi + ahead],
                                           ALU.add))
                    a, b = b, (pwin[1] if b is pwin[0] else pwin[0])
                dve.wait_ge(inv_loaded, 16 * (c + 1))
                span = slice(PAD, POOL_W - PAD)
                link(dve.tensor_tensor(a[:, span], a[:, span], pinv[:, span], ALU.mult))
                dve.tensor_tensor(pooled[:, span], a[:, span], ptok[:, span], ALU.subtract).then_inc(pooled_ready, 1)
                dve.wait_ge(pooled_ready, c + 1)

            def silu_unit(h, u):
                if not by_dve(u):
                    return
                ge(dve, u_stored[u % 3], h * (16 * SECTIONS) + 16 * (u // 3))
                dve.wait_ge(usig_ready, h * (2 * NG) + sum(by_dve(v) for v in range(u + 1)))
                dve.tensor_tensor(ustage[:, u % 3, :], usig[:, :], PROJ[u % 3][:, :],
                                  ALU.mult).then_inc(dve_units, 1)

            def subs(x):
                return x[:, :].rearrange("p (s c) -> p s c", c=SUB)

            def blocks(x):
                return x[:, :].rearrange("p (b s c) -> p b s c", s=NSUB, c=SUB)

            def exponents(h, n):
                d = STEPS[n][0]
                if n == 0:
                    dve.tensor_copy(lbcur[:, :], lbs[:, ds(h, 1), :].rearrange("p o c -> p (o c)")).then_inc(lb_ready, 1)
                    dve.wait_ge(lb_ready, h + 1)
                dve.wait_ge(rin_loaded[n % 2], in_slot(h, n))
                dve.tensor_scalar(keep[:, :], rin[:, n % 2, 1, :], lbcur[:, 3 * d + 2:3 * d + 3],
                                  lbcur[:, 3 * d + 1:3 * d + 2], ALU.mult, ALU.add)
                dve.wait_ge(logf_ready, h * NS + (n + 1))
                link(dve.tensor_tensor_scan(cum[:, :], scan_mask[:, :], logf[:, :], 0.0, ALU.mult, ALU.add))
                c4 = blocks(cum)
                last = c4[:, :, NSUB - 1, SUB - 1:SUB]
                link(dve.tensor_copy(edges[:, :, 8:9], last))
                if d == FWD:
                    mid = SUB // 2 - 1
                    ref = c4[:, :, :, mid]
                    dve.tensor_copy(edges[:, :, 3:7], ref)
                    dve.tensor_tensor(edges[:, :, 7:8], edges[:, :, 8:9], ref[:, :, NSUB - 1:NSUB], ALU.subtract)
                else:
                    mid = SUB // 2
                    link(dve.tensor_tensor(cum[:, :], cum[:, :], logf[:, :], ALU.subtract))
                    ref = c4[:, :, :, mid]
                    dve.tensor_tensor(edges[:, :, 3:7], edges[:, :, 8:9].to_broadcast([P, BG, NSUB]), ref,
                                      ALU.subtract)
                    dve.tensor_copy(edges[:, :, 7:8], ref[:, :, 0:1])
                dve.tensor_tensor(edges[:, :, 0:3], ref[:, :, 1:NSUB], ref[:, :, 0:NSUB - 1], ALU.subtract)
                x = subs(cum)
                dve.tensor_tensor(subs(dist), x, x[:, :, mid:mid + 1].to_broadcast([P, BG * NSUB, SUB]),
                                  ALU.subtract).then_inc(dist_ready, 1)

            def queries_and_keys(h, n):
                d = STEPS[n][0]
                lv = lev[d]
                dve.wait_ge(exps_ready, h * NS + (n + 1))
                ge(dve, sc_ready, h * NS + n)
                link(dve.tensor_tensor(qs[:, :], rin[:, n % 2, 0, :], exq[:, :], ALU.mult))
                diagonal = lv[:, :, :].rearrange("p b (s c) -> p b s c", c=P + SUB)[:, :, :, 0:SUB]
                link(dve.tensor_tensor(diagonal, blocks(keep), blocks(exk), ALU.mult))
                order = range(1, NSUB) if d == FWD else range(NSUB - 2, -1, -1)
                for j in order:
                    src = j - 1 if d == FWD else j + 1
                    lo, hi = (0, SUB * j) if d == FWD else (SUB * (j + 1), P)
                    f = min(j, src)
                    link(dve.tensor_tensor(lv[:, :, j * P + lo:j * P + hi], lv[:, :, src * P + lo:src * P + hi],
                                           edges_exp[:, n % 2, :, f:f + 1].to_broadcast([P, BG, hi - lo]), ALU.mult))
                full = (NSUB - 1) * P if d == FWD else 0
                ge(dve, kT_ready, h * NS + n)
                dve.tensor_tensor(kst[:, :].rearrange("p (b c) -> p b c", c=P), lv[:, :, full:full + P],
                                  edges_exp[:, n % 2, :, 7:8].to_broadcast([P, BG, P]), ALU.mult).then_inc(keys_ready, 1)

            def state_queries(h, n):
                ge(dve, o_ready, h * NS + n)
                dve.tensor_tensor(blocks(qint), blocks(qs),
                                  edges_exp[:, n % 2, :, 3:7].unsqueeze(3).to_broadcast([P, BG, NSUB, SUB]),
                                  ALU.mult).then_inc(qint_ready, 1)

            def states_and_scores(h, n):
                d, g = STEPS[n]
                first, rest = (0, range(BG)) if d == FWD else (BG, range(BG - 1, -1, -1))
                ge(dve, o_ready, h * NS + n)
                if (d, g) in NEW_SEQUENCE:
                    link(dve.memset(state[:, first, :], 0.0))
                else:
                    link(dve.tensor_copy(state[:, first, :], state[:, BG - first, :]))
                dve.wait_ge(kv_ready, h * NS + (n + 1))
                for b in rest:
                    src, dst = (b, b + 1) if d == FWD else (b + 1, b)
                    if b == rest[-1]:
                        dve.wait_ge(sc_ready, h * NS + (n + 1))
                    ins = dve.scalar_tensor_tensor(out=state[:, dst, :], in0=state[:, src, :],
                                                   scalar=edges_exp[:, n % 2, b, 8:9], in1=KV[:, b * P:(b + 1) * P],
                                                   op0=ALU.mult, op1=ALU.add)
                    if b == rest[-1]:
                        ins.then_inc(dve_step, 1)
                        chain.n += 1
                    else:
                        link(ins)
                dve.copy_predicated(scT[d][:, :, :], tri[d][:, :].bitcast(u32).unsqueeze(1).to_broadcast([P, BG, P]),
                                    SC[:, :].rearrange("p (b c) -> p b c", c=P)).then_inc(st_ready, 1)

            def sum_outputs(h, n):
                g = STEPS[n][1]
                dve.wait_ge(o_ready, h * NS + (n + 1))
                dve.wait_ge(ob_ready, h * NG + NG)
                dve.tensor_tensor(osum[:, :], OUT[:, :], obwd[:, g * GT:(g + 1) * GT], ALU.add).then_inc(osum_ready, 1)

            def mixer_output(h, g):
                dve.wait_ge(rr_ready, h * NG + (g + 1))
                dve.wait_ge(mix_stored[g], h * 16 + 16 * POOLS)
                link(dve.scalar_tensor_tensor(out=mixst[:, g, :], in0=osum[:, :], scalar=colc[:, C_GAIN:C_GAIN + 1],
                                              in1=rms[:, :], op0=ALU.mult, op1=ALU.mult))
                dve.wait_ge(ogate_loaded[g], h * 16 + 16)
                dve.tensor_tensor(mixst[:, g, :], mixst[:, g, :], ogate[:, g, :], ALU.mult).then_inc(mix_ready, 1)

            def add_part(v):
                t, half = divmod(v, 2)
                if half == 0:
                    dve.wait_ge(xp_loaded[t % 2], 16 * (t // 2) + 16)
                if v < 3:
                    dve.wait_ge(u_stored[v % 3], HEADS * 16 * SECTIONS)
                else:
                    dve.wait_ge(part_stored[v % 3], 16 * (v // 3))
                dve.wait_ge(part_done, v + 1)
                dve.tensor_tensor(ustage[:, v % 3, :], PROJ[v % 3][:, :],
                                  xp[:, t % 2, half * HALF:(half + 1) * HALF], ALU.add).then_inc(part_ready, 1)

            def recurrence(h):
                more = not static(h, HEADS - 1)
                exponents(h, 0)
                if more:
                    silu_unit(h + 1, 0)
                queries_and_keys(h, 0)
                if more:
                    silu_unit(h + 1, 1)
                else:
                    add_part(0)
                    add_part(1)
                state_queries(h, 0)
                for n, (d, g) in enumerate(STEPS):
                    u = BEFORE + PER_STEP * n
                    if more:
                        silu_unit(h + 1, u - 1)
                    if n + 1 < NS:
                        exponents(h, n + 1)
                    states_and_scores(h, n)
                    if n + 1 < NS:
                        queries_and_keys(h, n + 1)
                    if more:
                        silu_unit(h + 1, u)
                    else:
                        add_part(PARTS_PER_STEP * n + 2)
                        add_part(PARTS_PER_STEP * n + 3)
                    if d == FWD and g > 0:
                        mixer_output(h, g - 1)
                    if not more and n + 1 < NS:
                        add_part(PARTS_PER_STEP * n + 4)
                        add_part(PARTS_PER_STEP * n + 5)
                    if n + 1 < NS:
                        state_queries(h, n + 1)
                    if d == FWD:
                        sum_outputs(h, n)
                if more:
                    silu_unit(h + 1, UNITS - 1)
                mixer_output(h, NG - 1)

            for c in range(POOLS):
                pool_group(c)
            for u in range(UNITS):
                silu_unit(0, u)
            heads_loop(dve, chain, recurrence)

            chain.start()

            def residual(t, s):
                dve.wait_ge(xres_loaded[s], t * 8 + (16 - 8 * s))
                if not isinstance(t, int):
                    dve.wait_ge(x1_stored[s], 8 * t - 8 * s)
                for half in range(2):
                    cs = slice(half * 512, (half + 1) * 512)
                    dve.wait_ge(wo_ready, 2 * t + (half + 1))
                    dve.tensor_tensor(x1t[:, s, cs], bank[2 * s + half][:, :], xres[:, s, cs],
                                      ALU.add).then_inc(x1_ready, 1)
                dve.wait_ge(rms2_ready, t + 1)
                link(dve.reciprocal(rstd[:, 0:1], ss[:, 1:2]))
                dve.scalar_tensor_tensor(out=xnt[:, s, :], in0=x1t[:, s, :], scalar=rstd[:, 0:1],
                                         in1=rowc[:, R_FFN:R_FFN + D], op0=ALU.mult,
                                         op1=ALU.mult).then_inc(xn_ready, 1)

            def add_bias(t):
                dve.wait_ge(router_ready, t + 1)
                dve.tensor_tensor(logits[:, ds(t, 1), :].rearrange("p o c -> p (o c)"), bank[6][:, 0:NLOG],
                                  rowc[:, R_BIAS:R_BIAS + NLOG], ALU.add).then_inc(logits_ready, 1)

            dve.wait_ge(wrest_loaded, 48)
            residual(0, 0)
            residual(1, 1)
            chain.start()
            with dve.Fori(1, NT // 2) as i:
                chain.enter(i - 1, 2)
                for s in range(2):
                    residual(2 * i + s, s)
                    add_bias(2 * i + (s - 2))
            chain.leave(NT // 2 - 1)
            add_bias(NT - 2)
            add_bias(NT - 1)

            dve.wait_ge(ranks_ready, 1)
            dve.wait_ge(logits_ready, NT)
            dve.wait_ge(xnT_copied, 2 * NT)
            BIG = 1.0e30
            over_tiles = [P, NT, NE]

            def spread(x, n):
                return x.unsqueeze(2).to_broadcast([P, NT, n])

            def first_max(values, rank, n, best, scratch_, chosen):
                ranks = rank.unsqueeze(1).to_broadcast([P, NT, n])
                link(dve.tensor_reduce(best, values, axis=AX.X, op=ALU.max))
                link(dve.tensor_tensor(scratch_, values, spread(best, n), ALU.is_equal))
                link(dve.tensor_tensor(scratch_, scratch_, ranks, ALU.mult))
                link(dve.tensor_reduce(top[:, 3, :], scratch_, axis=AX.X, op=ALU.max))
                link(dve.tensor_tensor(chosen, ranks, spread(top[:, 3, :], n), ALU.is_equal))

            g_logits, e_logits = logits[:, :, 0:N_GROUPS], logits[:, :, N_GROUPS:NLOG]
            group_hot = slots[:, :, 0:N_GROUPS]
            first_max(g_logits, group_rank[:, :], N_GROUPS, top[:, 0, :], grp[:, :, :], group_hot)
            dve.tensor_tensor(grp[:, :, :], g_logits, spread(top[:, 0, :], N_GROUPS),
                              ALU.subtract).then_inc(gexp_ready, 1)
            link(dve.tensor_scalar(masked[:, :, 0:N_GROUPS], group_hot, BIG, -BIG, ALU.mult, ALU.add))
            link(dve.tensor_copy(work[:, :, :].rearrange("p t (g e) -> p t g e", g=N_GROUPS),
                                 masked[:, :, 0:N_GROUPS].unsqueeze(3)
                                 .to_broadcast([P, NT, N_GROUPS, PER_GROUP])))
            link(dve.tensor_tensor(masked[:, :, :], work[:, :, :], e_logits, ALU.add))
            first_max(masked[:, :, :], expert_rank[:, :], NE, top[:, 0, :], work[:, :, :], pick[0][:, :, :])
            link(dve.scalar_tensor_tensor(out=masked[:, :, :], in0=pick[0][:, :, :], scalar=-BIG,
                                          in1=masked[:, :, :], op0=ALU.mult, op1=ALU.add))
            first_max(masked[:, :, :], expert_rank[:, :], NE, top[:, 1, :], work[:, :, :], pick[1][:, :, :])
            dve.tensor_tensor(top[:, 1, :], top[:, 1, :], top[:, 0, :], ALU.subtract).then_inc(gexp_ready, 1)
            dve.tensor_tensor(work[:, :, :], pick[0][:, :, :], pick[1][:, :, :], ALU.add).then_inc(picks_ready, 1)
            dve.wait_ge(gexp_done, 2)
            link(dve.tensor_reduce(top[:, 2, :], grp[:, :, :], axis=AX.X, op=ALU.add))
            link(dve.tensor_scalar(top[:, 3, :], top[:, 1, :], 1.0, None, ALU.add))
            link(dve.tensor_tensor(top[:, 2, :], top[:, 2, :], top[:, 3, :], ALU.mult))
            link(dve.reciprocal(top[:, 2, :], top[:, 2, :]))
            link(dve.tensor_copy(gate[:, :, 0], top[:, 2, :]))
            link(dve.tensor_tensor(gate[:, :, 1], top[:, 2, :], top[:, 1, :], ALU.mult))
            dve.wait_ge(count_ready, 1)
            totals = bank[1][:, 0:NT * NE].rearrange("p (t e) -> p t e", e=NE)
            link(dve.memset(offset[:, 0, :], 0.0))
            for t in range(NT):
                link(dve.tensor_tensor(offset[:, t + 1, :], totals[:, t, :], offset[:, t, :], ALU.add))
            link(dve.tensor_scalar(tokens_up[:, :], offset[:, NT, :], float(P - 1), None, ALU.add))
            link(dve.tensor_single_scalar(tokens_up[:, :], tokens_up[:, :], 7, ALU.logical_shift_right))
            link(dve.tensor_copy(bcount[:, :], tokens_up[:, :]))
            link(dve.memset(bcmp[:, 0:NE], 1.0))
            link(dve.tensor_tensor_scan(bend[:, :], bcmp[:, 0:NE], bcount[:, :], 0.0, ALU.mult, ALU.add))
            link(dve.tensor_scalar(blocks_over[:, :], bend[:, NE - 1:NE], -float(MIN_BLOCKS), None, ALU.add))
            nb = BLOCK_COLUMNS
            link(dve.tensor_scalar(bcmp[:, 0:NE], bend[:, :], row_id[:, 0:1], None, ALU.is_le))
            link(dve.tensor_reduce(bsum[:, 0:1], bcmp[:, 0:NE], axis=AX.X, op=ALU.add))
            dve.tensor_scalar(bsum[:, 0:1], bsum[:, 0:1], float(NE - 1), None, ALU.min).then_inc(bexp_ready, 1)
            link(dve.tensor_tensor(bend[:, :], bend[:, :], bcount[:, :], ALU.subtract))
            link(dve.tensor_scalar(bend[:, :], bend[:, :], float(P), None, ALU.mult))
            link(dve.tensor_tensor(slots[:, :, :], bank[0][:, 0:NT * NE].rearrange("p (t e) -> p t e", e=NE),
                                   offset[:, 0:NT, :], ALU.add))
            link(dve.tensor_tensor(slots[:, :, :], slots[:, :, :],
                                   bend[:, :].unsqueeze(1).to_broadcast(over_tiles), ALU.add))
            dve.wait_ge(bexp_turned, 1)
            dve.tensor_copy(expert_of[0:1, :], bank[3][0:1, 0:nb]).then_inc(blocks_known, 1)
            for j in range(2):
                link(dve.tensor_tensor(masked[:, :, :], pick[j][:, :, :], slots[:, :, :], ALU.mult))
                link(dve.tensor_reduce(where[:, j, :], masked[:, :, :], axis=AX.X, op=ALU.add))
            flat = where[:, :, :].rearrange("p j t -> p (j t)")
            link(dve.tensor_copy(whole[:, 0, :], flat))
            link(dve.tensor_single_scalar(whole[:, 1, :], whole[:, 0, :], 7, ALU.logical_shift_right))
            link(dve.tensor_single_scalar(whole[:, 2, :], whole[:, 0, :], P - 1, ALU.bitwise_and))
            dve.tensor_copy(parts[:, :, :], whole[:, 1:3, :]).then_inc(parts_ready, 1)
            dve.wait_ge(parts_ready, 1)
            for c in range(2 * NT):
                t = c % NT
                if c % 2:
                    dve.tensor_scalar(hot[:, c, :], lane[:, :], parts[:, 1, c:c + 1], None, ALU.is_equal)
                dve.tensor_scalar(hotb[:, c, :], lane[:, 0:nb], parts[:, 0, c:c + 1],
                                  token_id[:, t:t + 1], ALU.is_equal, ALU.mult).then_inc(hot_ready, 1)
            dve.wait_ge(tokens_summed, 1)
            link(dve.tensor_scalar(slot_free[:, :], bank[2][:, 0:nb], 0.0, row_id[:, 0:1], ALU.is_equal, ALU.mult))
            link(dve.scalar_tensor_tensor(out=slot_free[:, :], in0=bank[2][:, 0:nb], scalar=float(T),
                                          in1=slot_free[:, :], op0=ALU.add, op1=ALU.add))
            dve.tensor_copy(token_of[:, :], slot_free[:, :]).then_inc(routed, 1)
            dve.wait_ge(routed, 1)

            used = dve.value_load(blocks_over[0:1, 0:1], min_val=0, max_val=MAX_BLOCKS - MIN_BLOCKS) + MIN_BLOCKS

            def next_rows(b, s):
                if not (isinstance(b, int) and b < 2):
                    dve.wait_ge(xg_loaded[s], b * 8 - 8 * s)
                    dve.wait_ge(xgT_ready, 2 * b - 2)
                dve.tensor_copy(gidx[:, s:s + 1], token_of[:, ds(b, 1)]).then_inc(gidx_ready, 1)

            def hidden(b):
                dve.wait_ge(sil_ready, b + 1)
                dve.wait_ge(h3_ready, b + 1)
                ge(dve, hidT_ready, b)
                dve.tensor_tensor(hid[:, :], sil[:, :], bank[3][:, :], ALU.mult).then_inc(hid_ready, 1)

            def copy_hidT(b):
                dve.wait_ge(hidT_ready, b + 1)
                dve.tensor_copy(hidT[:, :, :], bank[4][:, :].rearrange("p (k c) -> p k c", c=P)
                                ).then_inc(hidT_copied, 1)

            def copy_y(b, s):
                if not (isinstance(b, int) and b < 2):
                    dve.wait_ge(y_added[s], b * 8 - 8 * s)
                dve.tensor_copy(sidx[:, s:s + 1], token_of[:, ds(b, 1)])
                for half in range(2):
                    dve.wait_ge(y_ready, 2 * b + (half + 1))
                    dve.tensor_scalar(yst[:, s, half * 512:(half + 1) * 512], bank[5 + half][:, :],
                                      gate_of[:, ds(b, 1)], None, ALU.mult).then_inc(y_copied, 1)

            next_rows(0, 0)
            next_rows(1, 1)
            for c in range(2 * NT):
                j, t = divmod(c, NT)
                dve.tensor_scalar(hotg[:, c, :], lane[:, 0:nb], parts[:, 0, c:c + 1],
                                  gate[:, t, j:j + 1], ALU.is_equal, ALU.mult).then_inc(hotg_ready, 1)
            next_rows(2, 0)
            dve.wait_ge(gates_summed, 1)
            dve.tensor_copy(gate_of[:, :], bank[7][:, 0:nb]).then_inc(gates_known, 1)
            dve.wait_ge(gates_known, 1)
            hidden(0)

            def expert_step(b, s):
                next_rows(b + 2, s)
                copy_hidT(b - 1)
                hidden(b)
                copy_y(b - 1, 1 - s)

            expert_step(1, 1)
            expert_step(2, 0)
            blocks_loop(dve, 3, used, expert_step)
            dve.wait_ge(hidT_ready, used)
            dve.tensor_copy(hidT[:, :, :], bank[4][:, :].rearrange("p (k c) -> p k c", c=P)).then_inc(hidT_copied, 1)
            for s in range(2):
                with dve.If(((used + (1 - s)) & 1) < 1):
                    copy_y(used - 1, s)

            dve.wait_ge(xgT_copied, 2 * used + 2)
            for half in range(2):
                dve.tensor_copy(bank[half][:, :], rowc[:, R_FINAL + half * 512:R_FINAL + (half + 1) * 512]
                                ).then_inc(gain_ready, 1)
            dve.wait_ge(gain_ready, 2)
            chain.start()
            with dve.Fori(0, NT) as t:
                chain.enter(t, 1)
                dve.wait_ge(rms3_ready, t + 1)
                link(dve.reciprocal(fss[:, 2, ds(t, 1)], fss[:, 1, ds(t, 1)]))
                for half in range(2):
                    x = final[:, ds(t, 1), half * 512:(half + 1) * 512].rearrange("p o d -> p (o d)")
                    dve.scalar_tensor_tensor(out=x, in0=x, scalar=fss[:, 2, ds(t, 1)], in1=bank[half][:, :],
                                             op0=ALU.mult, op1=ALU.mult).then_inc(out_ready, 1)
            chain.leave(NT)

        @block.tensor
        def _(pe):
            pe.wait_ge(consts_ready, FIRST_CONSTS)

            def transpose_x(t, s):
                for half in range(2):
                    pe.wait_ge(xs2_ready if half else xs_ready, t + 1)
                    ge(pe, nT_ready, 2 * t + (half - 1))
                    for k in range(KT // 2):
                        c0 = (half * KT // 2 + k) * P
                        last = pe.transpose(XT[half][:, k * P:(k + 1) * P], xs[:, s, c0:c0 + P], ident[:, :])
                    last.then_inc(xT_ready, 1)

            def product(u, slot, g):
                for k in range(KT):
                    last = pe.matmul(PROJ[u % 3][:, :], wsec[:, slot, k, :], nT[:, k, g * GT:(g + 1) * GT],
                                     start=(k == 0), stop=(k == KT - 1))
                last.then_inc(gemm_done, 1)

            def pool_unit(j):
                c, g = divmod(j, NG)
                if g == 0:
                    pe.wait_ge(w_loaded[c], 16)
                ge(pe, dve_units, j - 2)
                product(j, c, g)

            def unit(h, u):
                sec, g = divmod(u, NG)
                if g == 0:
                    pe.wait_ge(w_loaded[sec], h * 16 + (32 if sec < POOLS else 16))
                if u >= 3:
                    wait_left_bank(pe, h, u - 3)
                elif static(h, 0):
                    pe.wait_ge(dve_units, POOL_UNITS - 2 + u)
                else:
                    wait_left_bank(pe, h - 1, UNITS - 3 + u)
                product(u, sec, g)

            def pool_map(c):
                pe.wait_ge(pooled_ready, c + 1)
                if c == 0:
                    pe.wait_ge(wpool_loaded, 16)
                for g in range(NG):
                    ge(pe, pmix_ready, (c - 1) * NG + g + 1)
                    c0 = pool_column(g * GT)
                    pe.matmul(bank[3 + g][:, :], wpool[:, c, :], pooled[:, c0:c0 + GT],
                              start=True, stop=True).then_inc(py_ready, 1)

            transpose_x(0, 0)
            transpose_x(1, 1)
            for g in range(NG):
                i0, i1 = (g * BG + 2) // 2, min(((g + 1) * BG + 2) // 2, NT // 2)
                with pe.Fori(i0, i1) as i:
                    for s in range(2):
                        transpose_x(2 * i + s, s)
                pe.wait_ge(nT_ready, 2 * BG * (g + 1))
                pool_unit(g)
            for c in range(1, POOLS):
                for g in range(NG):
                    pool_unit(c * NG + g)
                pool_map(c - 1)
            for u in range(UNITS):
                unit(0, u)
                if u == NG - 1:
                    pool_map(POOLS - 1)

            def to_tokens(h, n):
                d, g = STEPS[n]
                r = h * NS + n
                pe.wait_ge(keys_ready, r + 1)
                ge(pe, ktok_ready, r)
                if d == BWD:
                    ge(pe, rr_ready, h * NG)
                    pe.wait_ge(rin_loaded[n % 2], in_slot(h, n))
                    for b in range(BG):
                        pe.transpose(TV[:, b * P:(b + 1) * P], rin[:, n % 2, 2, b * P:(b + 1) * P], ident[:, :])
                for b in range(BG):
                    last = pe.transpose(TK[:, b * P:(b + 1) * P], kst[:, b * P:(b + 1) * P], ident[:, :])
                last.then_inc(kT_ready, 1)

            def scores_and_updates(h, n):
                d, g = STEPS[n]
                r = h * NS + n
                ge(pe, st_ready, r)
                for b in range(BG):
                    for j in range(NSUB):
                        c0 = b * P + j * SUB
                        last = pe.matmul(SC[:, c0:c0 + SUB], lev[d][:, b, j * P:(j + 1) * P], qs[:, c0:c0 + SUB],
                                         start=True, stop=True)
                last.then_inc(sc_ready, 1)
                pe.wait_ge(ktok_ready, r + 1)
                for b in range(BG):
                    last = pe.matmul(KV[:, b * P:(b + 1) * P], ktok[:, b, :], vtok[:, g * BG + b, :],
                                     start=True, stop=True)
                last.then_inc(kv_ready, 1)

            def block_outputs(h, n):
                d, g = STEPS[n]
                r = h * NS + n
                pe.wait_ge(st_ready, r + 1)
                pe.wait_ge(qint_ready, r + 1)
                if 1 <= n <= NG:
                    pe.wait_ge(ob_ready, h * NG + n)
                else:
                    ge(pe, osum_ready, h * NG + (n - NG if n else 0))
                for b in range(BG):
                    cs = slice(b * P, (b + 1) * P)
                    pe.matmul(OUT[:, cs], vtok[:, g * BG + b, :], scT[d][:, b, :], start=True, stop=False)
                    last = pe.matmul(OUT[:, cs], state[:, b if d == FWD else b + 1, :], qint[:, cs],
                                     start=False, stop=True)
                last.then_inc(o_ready, 1)

            def mean_square(h, g):
                pe.wait_ge(osq_ready, h * NG + (g + 1))
                if g == 0:
                    pe.wait_ge(ktok_ready, h * NS + NG)
                ge(pe, rr_ready, h * NG + g)
                pe.matmul(MS[:, :], ones[:, :], osq[:, :], start=True, stop=True).then_inc(ms_ready, 1)

            def first_part(t):
                if t == 0:
                    pe.wait_ge(wout_loaded, 16)
                pe.wait_ge(mixp_loaded[t % 2], 16 * (t // 2) + 16)
                for half in range(2):
                    v = 2 * t + half
                    if v < 3:
                        wait_left_bank(pe, HEADS - 1, UNITS - 3 + v)
                    else:
                        pe.wait_ge(part_ready, v - 2)
                    for k in range(PK):
                        last = pe.matmul(PROJ[v % 3][:, :], mixp[:, t % 2, k, :],
                                         wfirst[:, k, half * HALF:(half + 1) * HALF],
                                         start=(k == 0), stop=(k == PK - 1))
                    last.then_inc(part_done, 1)

            def recurrence(h):
                more = not static(h, HEADS - 1)
                for u in range(BEFORE if more else 0):
                    unit(h + 1, u)
                if not more:
                    first_part(0)
                for n, (d, g) in enumerate(STEPS):
                    u = BEFORE + PER_STEP * n
                    to_tokens(h, n)
                    scores_and_updates(h, n)
                    if d == FWD and g > 0:
                        mean_square(h, g - 1)
                    if more:
                        unit(h + 1, u)
                        unit(h + 1, u + 1)
                    else:
                        first_part(2 * n + 1)
                        if n + 1 < NS:
                            first_part(2 * n + 2)
                    block_outputs(h, n)
                mean_square(h, NG - 1)

            recurrence(0)
            with pe.Fori(1, HEADS - 1) as h:
                recurrence(h)
            recurrence(HEADS - 1)

            pe.wait_ge(wrest_loaded, 48)
            pe.wait_ge(part_ready, PARTS)

            def project_half(t, s, half):
                if half == 0:
                    pe.wait_ge(mixt_loaded[s], t * 8 + (16 - 8 * s))
                if not (isinstance(t, int) and t < 2):
                    pe.wait_ge(x1_ready, 2 * t - 3 + half)
                for k in range(PK, KT):
                    last = pe.matmul(bank[2 * s + half][:, :], mixt[:, s, k - PK, :],
                                     wrest[:, k - PK, half * HALF:(half + 1) * HALF], start=(k == PK), stop=(k == KT - 1))
                last.then_inc(wo_ready, 1)

            def transpose_tile(t, s):
                if static(t, 0):
                    pe.wait_ge(rr_ready, HEADS * NG)
                pe.wait_ge(xn_ready, t + 1)
                for half in range(2):
                    ge(pe, xnT_copied, 2 * t + (half - 1))
                    for k in range(KT // 2):
                        c0 = (half * KT // 2 + k) * P
                        last = pe.transpose(bank[4 + half][:, k * P:(k + 1) * P], xnt[:, s, c0:c0 + P], ident[:, :])
                    last.then_inc(xnT_ready, 1)

            def route_tile(t):
                pe.wait_ge(xnT_copied, 2 * t + 2)
                ge(pe, logits_ready, t)
                for k in range(KT):
                    last = pe.matmul(bank[6][:, 0:NLOG], xnT[:, k, :], rw[:, k, :],
                                     start=(k == 0), stop=(k == KT - 1))
                last.then_inc(router_ready, 1)

            for t in range(2):
                project_half(t, t, 0)
                project_half(t, t, 1)
            for t in range(2, 4):
                project_half(t, t % 2, 0)
                transpose_tile(t - 2, t % 2)
                project_half(t, t % 2, 1)
                route_tile(t - 2)
            with pe.Fori(2, NT // 2) as i:
                for s in range(2):
                    project_half(2 * i + s, s, 0)
                    transpose_tile(2 * i + (s - 2), s)
                    project_half(2 * i + s, s, 1)
                    route_tile(2 * i + (s - 2))
            for s in range(2):
                transpose_tile(NT - 2 + s, s)
                route_tile(NT - 2 + s)

            pe.wait_ge(picks_ready, 1)
            chosen = work[:, :, :].rearrange("p t e -> p (t e)")
            pe.matmul(bank[0][:, 0:NT * NE], before[:, :], chosen, start=True, stop=True)
            pe.matmul(bank[1][:, 0:NT * NE], ones[:, :], chosen, start=True, stop=True).then_inc(count_ready, 1)
            nb = BLOCK_COLUMNS
            pe.wait_ge(bexp_ready, 1)
            pe.matmul(bank[3][0:1, 0:nb], bsum[:, 0:1], ident[:, 0:nb], start=True, stop=True).then_inc(bexp_turned, 1)
            for c in range(2 * NT):
                pe.wait_ge(hot_ready, c + 1)
                if c % 2 == 0:
                    pe.wait_ge(hotrow_ready, c // 2 + 1)
                last = pe.matmul(bank[2][:, 0:nb], hot[:, c, :], hotb[:, c, :],
                                 start=(c == 0), stop=(c == 2 * NT - 1))
            last.then_inc(tokens_summed, 1)

            def sum_gates(c0, c1):
                for c in range(c0, c1):
                    pe.wait_ge(hotg_ready, c + 1)
                    last = pe.matmul(bank[7][:, 0:nb], hot[:, c, :], hotg[:, c, :],
                                     start=(c == 0), stop=(c == 2 * NT - 1))
                if c1 == 2 * NT:
                    last.then_inc(gates_summed, 1)

            sum_gates(0, NT)

            pe.wait_ge(routed, 1)
            used = pe.value_load(blocks_over[0:1, 0:1], min_val=0, max_val=MAX_BLOCKS - MIN_BLOCKS) + MIN_BLOCKS

            def transpose_rows(b, s):
                pe.wait_ge(xg_loaded[s], b * 8 + (16 - 8 * s))
                for half in range(2):
                    ge(pe, xgT_copied, 2 * b + (half - 1))
                    for k in range(KT // 2):
                        c0 = (half * KT // 2 + k) * P
                        last = pe.transpose(bank[half][:, k * P:(k + 1) * P], xg[:, s, c0:c0 + P], ident[:, :])
                    last.then_inc(xgT_ready, 1)

            def up(b, s, weights, loaded, out_bank, free, done):
                pe.wait_ge(loaded[s], b * 8 + (16 - 8 * s))
                ge(pe, free, b)
                for k in range(KT):
                    last = pe.matmul(bank[out_bank][:, :], xgT[:, k, :], weights[:, s, k, :],
                                     start=(k == 0), stop=(k == KT - 1))
                last.then_inc(done, 1)

            def first_up(b, s):
                pe.wait_ge(xgT_copied, 2 * b + 2)
                up(b, s, w1t, w1_loaded, 2, sil_ready, h1_ready)

            def second_up(b, s):
                up(b, s, w3t, w3_loaded, 3, hid_ready, h3_ready)

            def transpose_hidden(b):
                pe.wait_ge(hid_ready, b + 1)
                ge(pe, hidT_copied, b)
                for k in range(FT):
                    last = pe.transpose(bank[4][:, k * P:(k + 1) * P], hid[:, k * P:(k + 1) * P], ident[:, :])
                last.then_inc(hidT_ready, 1)

            def down(b, s):
                pe.wait_ge(w2_loaded[s], b * 8 + (16 - 8 * s))
                pe.wait_ge(hidT_copied, b + 1)
                for half in range(2):
                    ge(pe, y_copied, 2 * b + (half - 1))
                    for k in range(FT):
                        last = pe.matmul(bank[5 + half][:, :], hidT[:, k, :], w2t[:, s, k, half * 512:(half + 1) * 512],
                                         start=(k == 0), stop=(k == FT - 1))
                    last.then_inc(y_ready, 1)

            transpose_rows(0, 0)
            first_up(0, 0)
            sum_gates(NT, 2 * NT)
            second_up(0, 0)
            transpose_rows(1, 1)

            def expert_step(b, s):
                first_up(b, s)
                transpose_hidden(b - 1)
                second_up(b, s)
                transpose_rows(b + 1, 1 - s)
                down(b - 1, 1 - s)

            expert_step(1, 1)
            expert_step(2, 0)
            blocks_loop(pe, 3, used, expert_step)
            transpose_hidden(used - 1)
            for s in range(2):
                with pe.If(((used + (1 - s)) & 1) < 1):
                    down(used - 1, s)


def kernel(**inputs):
    import numpy as np
    import concourse.bacc as bacc
    from concourse.bass_utils import run_bass_kernel_spmd as run

    nc = bacc.Bacc("TRN2", target_bir_lowering=False, num_devices=1)
    f32 = mybir.dt.float32
    a = {k: np.ascontiguousarray(v) for k, v in inputs.items()}
    cols = np.concatenate([a["norm_mix"].reshape(KT, P).T, a["pool_scale"].reshape(POOLS, P).T,
                           a["hg_norm_gain"].reshape(1, P).T,
                           a["hg_lb_fwd"].reshape(2 * HEADS, P).T, a["hg_lb_bwd"].reshape(2 * HEADS, P).T], axis=1)
    rows = np.concatenate([a["norm_ffn"].reshape(-1), a["norm_final"].reshape(-1),
                           a["router_group_b"].reshape(-1), a["router_expert_b"].reshape(-1)])
    inv = np.ones((POOLS, POOL_W), np.float32)
    for c, w in enumerate(WINDOWS):
        for start, length in ((0, T_PROMPT), (T_PROMPT, T_SAMPLE)):
            t = np.arange(length)
            count = np.clip(t + w // 2, 0, length) - np.clip(t - w // 2, 0, length)
            inv[c, pool_column(start):pool_column(start) + length] = 1.0 / count
    arrays = {
        "x_all": np.concatenate([a["x_prompt"].reshape(-1, D), a["x_sample"].reshape(-1, D)]),
        "w_in": a["w_in"][0], "w_out": a["w_out"][0], "pool_w": a["pool_w"][0],
        "cols": np.ascontiguousarray(cols), "rows": np.broadcast_to(rows, (P, R_N)).copy(), "inv_count": inv,
        "router_w": np.concatenate([a["router_group_w"][0], a["router_expert_w"][0]], axis=1),
        "w1": a["expert_w1"].reshape(NE * D, FE), "w3": a["expert_w3"].reshape(NE * D, FE),
        "w2": a["expert_w2"].reshape(NE * FE, D),
    }
    args = [nc.dram_tensor(k, v.shape, f32, kind="ExternalInput").ap() for k, v in arrays.items()]
    out = nc.dram_tensor("y", (T, D), f32, kind="ExternalOutput").ap()
    trunk_program(nc, *args, out)
    y = run(nc, [arrays], core_ids=[0]).results[0]["y"]
    return y[:T_PROMPT].reshape(1, T_PROMPT, D), y[T_PROMPT:].reshape(1, T_SAMPLE, D)
```
